# Optimizing a Trainium2 kernel written in Bass

```python
import jax, jax.numpy as jnp
from jax import lax
import numpy as np
import math

D_MODEL = 2048
BATCH = 1
SEQ = 256
DEPTH = 1

MIX_W = D_MODEL
ATT_W = MIX_W // 2
HEAD_DIM = 128
N_ATT_HEADS = ATT_W // HEAD_DIM
CONV_W = MIX_W // 4
CONV_TAPS = 3
POOL_W = MIX_W - ATT_W - CONV_W
POOL_WINDOWS = (2, 4, 8, 16)
POOL_GROUP = POOL_W // len(POOL_WINDOWS)
Q_BLOCK = 128
LN_EPS = 1e-5
DEEPNORM_ALPHA = (2 * DEPTH) ** 0.25
DEEPNORM_BETA = (8 * DEPTH) ** -0.25

IN_WIDTHS = (ATT_W, ATT_W, ATT_W, ATT_W, N_ATT_HEADS,
             CONV_W, CONV_W, CONV_W, CONV_W, POOL_W, POOL_W)
IN_W = sum(IN_WIDTHS)
IN_SPLITS = tuple(sum(IN_WIDTHS[:i + 1]) for i in range(len(IN_WIDTHS) - 1))


def layer_norm(x, g, b):
    x32 = x.astype(jnp.float32)
    mu = jnp.mean(x32, axis=-1, keepdims=True)
    var = jnp.mean(jnp.square(x32 - mu), axis=-1, keepdims=True)
    return ((x32 - mu) * lax.rsqrt(var + LN_EPS) * g + b).astype(x.dtype)

def forgetting_attention(q, k, v, fg_logit, b_f):
    b, s, h, dh = q.shape
    nb = s // Q_BLOCK
    log_f = jax.nn.log_sigmoid(fg_logit.astype(jnp.float32) + b_f.astype(jnp.float32))
    cum = jnp.cumsum(log_f, axis=1)
    cum_k = jnp.transpose(cum, (0, 2, 1))
    q_blocks = q.reshape(b, nb, Q_BLOCK, h, dh).transpose(1, 0, 2, 3, 4)
    c_blocks = cum.reshape(b, nb, Q_BLOCK, h).transpose(1, 0, 3, 2)
    k_pos = jnp.arange(s)
    scale = HEAD_DIM ** -0.5

    def block(args):
        qb, cb, i = args
        logits = jnp.einsum('bqhd,bkhd->bhqk', qb, k).astype(jnp.float32) * scale
        logits = logits + cb[..., None] - cum_k[:, :, None, :]
        q_pos = i * Q_BLOCK + jnp.arange(Q_BLOCK)
        causal = k_pos[None, :] <= q_pos[:, None]
        logits = jnp.where(causal, logits, -jnp.inf)
        p = jax.nn.softmax(logits, axis=-1).astype(v.dtype)
        return jnp.einsum('bhqk,bkhd->bqhd', p, v)

    out = lax.map(block, (q_blocks, c_blocks, jnp.arange(nb)))
    return out.transpose(1, 0, 2, 3, 4).reshape(b, s, h * dh)

def short_conv_mixer(gate_b, gate_c, h, conv_w):
    s = h.shape[1]
    u = gate_c * h
    up = jnp.pad(u, ((0, 0), (CONV_TAPS - 1, 0), (0, 0)))
    y = conv_w[0] * up[:, 0:s]
    for j in range(1, CONV_TAPS):
        y = y + conv_w[j] * up[:, j:j + s]
    return gate_b * y

def multiscale_pool_mixer(u, pool_w, pool_scale):
    s = u.shape[1]
    u32 = u.astype(jnp.float32)
    cs = jnp.pad(jnp.cumsum(u32, axis=1), ((0, 0), (1, 0), (0, 0)))
    t1 = jnp.arange(1, s + 1, dtype=jnp.float32)
    outs = []
    for g, w in enumerate(POOL_WINDOWS):
        sl = slice(g * POOL_GROUP, (g + 1) * POOL_GROUP)
        csg = cs[:, :, sl]
        lagged = jnp.pad(csg[:, :s - w + 1], ((0, 0), (w - 1, 0), (0, 0)))
        count = jnp.minimum(t1, float(w))
        mean = (csg[:, 1:] - lagged) / count[None, :, None]
        z = (mean - u32[:, :, sl]).astype(u.dtype)
        outs.append(jnp.einsum('bsc,cd->bsd', z, pool_w[g]))
    return jnp.concatenate(outs, axis=-1) * pool_scale

def first_inputs(seed: int = 0) -> dict:
    key = jax.random.key(seed)
    ks = jax.random.split(key, 10)
    x = jax.random.normal(ks[0], (BATCH, SEQ, D_MODEL), jnp.float32)
    w_in = jax.random.normal(ks[1], (DEPTH, D_MODEL, IN_W), jnp.float32) * D_MODEL ** -0.5
    b_f = jax.random.uniform(ks[2], (DEPTH, N_ATT_HEADS), jnp.float32, 1.0, 4.0)
    conv_w = jax.random.normal(ks[3], (DEPTH, CONV_TAPS, CONV_W), jnp.float32) * CONV_TAPS ** -0.5
    pool_w = jax.random.normal(ks[4], (DEPTH, len(POOL_WINDOWS), POOL_GROUP, POOL_GROUP),
                               jnp.float32) * POOL_GROUP ** -0.5
    pool_scale = 1.0 + 0.1 * jax.random.normal(ks[5], (DEPTH, POOL_W), jnp.float32)
    w_out = jax.random.normal(ks[6], (DEPTH, MIX_W, D_MODEL), jnp.float32) * (
        MIX_W ** -0.5 * DEEPNORM_BETA)
    ln_g = 1.0 + 0.1 * jax.random.normal(ks[7], (DEPTH, D_MODEL), jnp.float32)
    ln_b = 0.02 * jax.random.normal(ks[8], (DEPTH, D_MODEL), jnp.float32)
    return {"x": x, "w_in": w_in, "b_f": b_f, "conv_w": conv_w, "pool_w": pool_w,
            "pool_scale": pool_scale, "w_out": w_out, "ln_g": ln_g, "ln_b": ln_b}

def first_block(x, w_in, b_f, conv_w, pool_w, pool_scale, w_out, ln_g, ln_b):
    b, s, _ = x.shape
    for l in range(DEPTH):
        proj = jnp.einsum('bsd,de->bse', x, w_in[l])
        (q, k, v, g_att, fg, c_b, c_c, c_h, g_conv, p_u, g_pool) = jnp.split(
            proj, IN_SPLITS, axis=-1)
        heads = (b, s, N_ATT_HEADS, HEAD_DIM)
        y_att = forgetting_attention(q.reshape(heads), k.reshape(heads), v.reshape(heads),
                                     fg, b_f[l]) * jax.nn.silu(g_att)
        y_conv = short_conv_mixer(c_b, c_c, c_h, conv_w[l]) * jax.nn.silu(g_conv)
        y_pool = multiscale_pool_mixer(p_u, pool_w[l], pool_scale[l]) * jax.nn.silu(g_pool)
        y = jnp.concatenate([y_att, y_conv, y_pool], axis=-1)
        y = jnp.einsum('bse,ed->bsd', y, w_out[l])
        x = layer_norm(DEEPNORM_ALPHA * x + y, ln_g[l], ln_b[l])
    return x


NUM_MIXERS = 2
N_GLA_LAYERS = (DEPTH + NUM_MIXERS - 1) // NUM_MIXERS
N_GDN_LAYERS = DEPTH // NUM_MIXERS

EPS = 1e-6
CHUNK = 64
PLE_DIM = 256
D_FF = ((8 * D_MODEL + 3 * 256 - 1) // (3 * 256)) * 256

GLA_HEADS = 4
GLA_DK = D_MODEL // (2 * GLA_HEADS)
GLA_DV = D_MODEL // GLA_HEADS
GLA_KEY_DIM = GLA_HEADS * GLA_DK
GLA_VAL_DIM = GLA_HEADS * GLA_DV
GLA_GATE_RANK = 16
GLA_GATE_NORM = 16.0
GLA_PROJ = 2 * GLA_KEY_DIM + 2 * GLA_VAL_DIM + 2 * GLA_GATE_RANK

GDN_QK_HEADS = D_MODEL // 128
GDN_V_HEADS = 2 * GDN_QK_HEADS
GDN_DK = 128
GDN_DV = 128
GDN_KEY_DIM = GDN_QK_HEADS * GDN_DK
GDN_VAL_DIM = GDN_V_HEADS * GDN_DV
GDN_CONV_DIM = 2 * GDN_KEY_DIM + GDN_VAL_DIM
CONV_W_2 = 5
GDN_PROJ = GDN_CONV_DIM + GDN_VAL_DIM + 4 * GDN_V_HEADS


def rmsnorm(x, w):
    xf = x.astype(jnp.float32)
    y = xf * lax.rsqrt(jnp.mean(xf * xf, axis=-1, keepdims=True) + EPS)
    return (y * w.astype(jnp.float32)).astype(x.dtype)

def l2norm(x):
    xf = x.astype(jnp.float32)
    return xf * lax.rsqrt(jnp.sum(xf * xf, axis=-1, keepdims=True) + EPS)

def to_heads(x, n):
    b, t, _ = x.shape
    return x.reshape(b, t, n, -1).transpose(0, 2, 1, 3)

def from_heads(x):
    b, n, t, d = x.shape
    return x.transpose(0, 2, 1, 3).reshape(b, t, n * d)

def flip_t(x):
    return jnp.flip(x, axis=2)

def gla_chunked(q, k, v, g):
    b, h, t, dk = q.shape
    dv = v.shape[-1]
    nc = t // CHUNK
    q, k, g = (a.reshape(b, h, nc, CHUNK, dk) for a in (q, k, g))
    v = v.reshape(b, h, nc, CHUNK, dv)
    cum = jnp.cumsum(g, axis=-2)
    last = cum[..., -1:, :]
    q_dec = q * jnp.exp(cum)
    k_dec = k * jnp.exp(last - cum)
    chunk_decay = jnp.exp(last[..., 0, :])
    lower = jnp.tril(jnp.ones((CHUNK, CHUNK), dtype=bool))
    xs = tuple(jnp.moveaxis(a, 2, 0) for a in (q, k, v, cum, q_dec, k_dec, chunk_decay))

    def step(S, inp):
        q_i, k_i, v_i, c_i, qd_i, kd_i, cd_i = inp
        pair = jnp.where(lower[..., None],
                         jnp.exp(jnp.minimum(c_i[..., :, None, :] - c_i[..., None, :, :], 0.0)), 0.0)
        a_i = jnp.einsum('bhid,bhjd,bhijd->bhij', q_i, k_i, pair)
        o_i = jnp.einsum('bhij,bhjv->bhiv', a_i, v_i) + jnp.einsum('bhid,bhdv->bhiv', qd_i, S)
        S = S * cd_i[..., None] + jnp.einsum('bhcd,bhcv->bhdv', kd_i, v_i)
        return S, o_i

    S0 = jnp.zeros((b, h, dk, dv), jnp.float32)
    _, o = lax.scan(step, S0, xs)
    return jnp.moveaxis(o, 0, 2).reshape(b, h, t, dv)

def gated_delta_chunked(q, k, v, g, beta):
    b, h, t, dk = q.shape
    dv = v.shape[-1]
    nc = t // CHUNK
    q = q.reshape(b, h, nc, CHUNK, dk)
    k = k.reshape(b, h, nc, CHUNK, dk)
    v = v.reshape(b, h, nc, CHUNK, dv)
    cum = jnp.cumsum(g.reshape(b, h, nc, CHUNK), axis=-1)
    beta = beta.reshape(b, h, nc, CHUNK, 1)
    idx = jnp.arange(CHUNK)
    lower = idx[:, None] >= idx[None, :]
    strict = idx[:, None] > idx[None, :]
    decay = jnp.where(lower, jnp.exp(jnp.minimum(cum[..., :, None] - cum[..., None, :], 0.0)), 0.0)
    k_beta = k * beta
    tri = jnp.where(strict, jnp.einsum('bhnid,bhnjd->bhnij', k_beta, k) * decay, 0.0) \
        + jnp.eye(CHUNK, dtype=jnp.float32)
    rhs = jnp.concatenate([v * beta, k_beta * jnp.exp(cum)[..., None]], axis=-1)
    sol = lax.linalg.triangular_solve(tri, rhs, left_side=True, lower=True, unit_diagonal=True)
    u, w = sol[..., :dv], sol[..., dv:]
    attn = jnp.einsum('bhnid,bhnjd->bhnij', q, k) * decay
    last = cum[..., -1:]
    q_dec = q * jnp.exp(cum)[..., None]
    k_dec = k * jnp.exp(last - cum)[..., None]
    chunk_decay = jnp.exp(last)
    xs = tuple(jnp.moveaxis(a, 2, 0) for a in (u, w, attn, q_dec, k_dec, chunk_decay))

    def step(S, inp):
        u_i, w_i, a_i, qd_i, kd_i, cd_i = inp
        v_new = u_i - jnp.einsum('bhcd,bhdv->bhcv', w_i, S)
        o_i = jnp.einsum('bhcd,bhdv->bhcv', qd_i, S) + jnp.einsum('bhij,bhjv->bhiv', a_i, v_new)
        S = S * cd_i[..., None] + jnp.einsum('bhcd,bhcv->bhdv', kd_i, v_new)
        return S, o_i

    S0 = jnp.zeros((b, h, dk, dv), jnp.float32)
    _, o = lax.scan(step, S0, xs)
    return jnp.moveaxis(o, 0, 2).reshape(b, h, t, dv)

def centred_short_conv(x, w):
    c = x.shape[-1]
    return lax.conv_general_dilated(
        x, w[:, None, :].astype(x.dtype), window_strides=(1,),
        padding=[(CONV_W_2 // 2, CONV_W_2 // 2)],
        dimension_numbers=('NWC', 'WIO', 'NWC'), feature_group_count=c)

def gla_mixer(hn, w_in, w_gate_up, b_gate, out_norm, w_out):
    b, t, _ = hn.shape
    proj = jnp.einsum('btd,de->bte', hn, w_in)
    q, k, v, og, lr = jnp.split(
        proj, [GLA_KEY_DIM, 2 * GLA_KEY_DIM, 2 * GLA_KEY_DIM + GLA_VAL_DIM,
               2 * GLA_KEY_DIM + 2 * GLA_VAL_DIM], axis=-1)
    lr = lr.reshape(b, t, 2, GLA_GATE_RANK)
    gk = jnp.einsum('btzr,zrd->zbtd', lr, w_gate_up) + b_gate[:, None, None, :]
    logdec = jax.nn.log_sigmoid(gk.astype(jnp.float32)) / GLA_GATE_NORM
    qh = to_heads(q, GLA_HEADS).astype(jnp.float32) * (GLA_DK ** -0.5)
    kh = to_heads(k, GLA_HEADS).astype(jnp.float32)
    vh = to_heads(v, GLA_HEADS).astype(jnp.float32)
    g_fwd = to_heads(logdec[0], GLA_HEADS)
    g_bwd = to_heads(logdec[1], GLA_HEADS)
    o = gla_chunked(qh, kh, vh, g_fwd) \
        + flip_t(gla_chunked(flip_t(qh), flip_t(kh), flip_t(vh), flip_t(g_bwd)))
    o = rmsnorm(o, out_norm)
    o = from_heads(o).astype(hn.dtype) * jax.nn.silu(og)
    return jnp.einsum('bte,ed->btd', o, w_out)

def gdn_mixer(hn, w_in, conv_w, a_log, dt_bias, out_norm, w_out):
    b, t, _ = hn.shape
    proj = jnp.einsum('btd,de->bte', hn, w_in)
    qkv, z, ba = jnp.split(proj, [GDN_CONV_DIM, GDN_CONV_DIM + GDN_VAL_DIM], axis=-1)
    qkv = jax.nn.silu(centred_short_conv(qkv, conv_w))
    q, k, v = jnp.split(qkv, [GDN_KEY_DIM, 2 * GDN_KEY_DIM], axis=-1)
    rep = GDN_V_HEADS // GDN_QK_HEADS
    qh = jnp.repeat(l2norm(to_heads(q, GDN_QK_HEADS)), rep, axis=1) * (GDN_DK ** -0.5)
    kh = jnp.repeat(l2norm(to_heads(k, GDN_QK_HEADS)), rep, axis=1)
    vh = to_heads(v, GDN_V_HEADS).astype(jnp.float32)
    ba = ba.reshape(b, t, 2, 2, GDN_V_HEADS).astype(jnp.float32)
    beta = jax.nn.sigmoid(ba[:, :, 0]).transpose(2, 0, 3, 1)
    a_in = ba[:, :, 1].transpose(2, 0, 3, 1)
    g = -jnp.exp(a_log.astype(jnp.float32))[:, None, :, None] \
        * jax.nn.softplus(a_in + dt_bias.astype(jnp.float32)[:, None, :, None])
    o = gated_delta_chunked(qh, kh, vh, g[0], beta[0]) \
        + flip_t(gated_delta_chunked(flip_t(qh), flip_t(kh), flip_t(vh), flip_t(g[1]), flip_t(beta[1])))
    o = rmsnorm(o, out_norm)
    o = from_heads(o).astype(hn.dtype) * jax.nn.silu(z)
    return jnp.einsum('bte,ed->btd', o, w_out)

def swiglu(hn, w_in, w_out):
    gate, up = jnp.split(jnp.einsum('btd,de->bte', hn, w_in), 2, axis=-1)
    return jnp.einsum('btf,fd->btd', jax.nn.silu(gate) * up, w_out)

def second_inputs(seed: int = 0) -> dict:
    key = jax.random.key(seed)
    ks = jax.random.split(key, 21)
    f32 = jnp.float32

    def nrm(k, shape, scale):
        return jax.random.normal(k, shape, f32) * scale

    def gain(k, shape):
        return 1.0 + 0.05 * jax.random.normal(k, shape, f32)

    x = nrm(ks[0], (BATCH, SEQ, D_MODEL), 1.0)
    p = nrm(ks[1], (DEPTH, BATCH, SEQ, PLE_DIM), 1.0)
    mixer_norm = gain(ks[2], (DEPTH, D_MODEL))
    gla_w_in = nrm(ks[3], (N_GLA_LAYERS, D_MODEL, GLA_PROJ), D_MODEL ** -0.5)
    gla_w_gate_up = nrm(ks[4], (N_GLA_LAYERS, 2, GLA_GATE_RANK, GLA_KEY_DIM), GLA_GATE_RANK ** -0.5)
    gla_b_gate = nrm(ks[5], (N_GLA_LAYERS, 2, GLA_KEY_DIM), 0.5)
    gla_out_norm = gain(ks[6], (N_GLA_LAYERS, GLA_DV))
    gla_w_out = nrm(ks[7], (N_GLA_LAYERS, GLA_VAL_DIM, D_MODEL), GLA_VAL_DIM ** -0.5)
    gdn_w_in = nrm(ks[8], (N_GDN_LAYERS, D_MODEL, GDN_PROJ), D_MODEL ** -0.5)
    gdn_conv = nrm(ks[9], (N_GDN_LAYERS, CONV_W_2, GDN_CONV_DIM), CONV_W_2 ** -0.5)
    gdn_a_log = jnp.log(jax.random.uniform(ks[10], (N_GDN_LAYERS, 2, GDN_V_HEADS), f32, 1.0, 16.0))
    dt = jnp.exp(jax.random.uniform(ks[11], (N_GDN_LAYERS, 2, GDN_V_HEADS), f32,
                                    math.log(1e-3), math.log(1e-1)))
    gdn_dt_bias = dt + jnp.log(-jnp.expm1(-dt))
    gdn_out_norm = gain(ks[12], (N_GDN_LAYERS, GDN_DV))
    gdn_w_out = nrm(ks[13], (N_GDN_LAYERS, GDN_VAL_DIM, D_MODEL), GDN_VAL_DIM ** -0.5)
    ffn_norm = gain(ks[14], (DEPTH, D_MODEL))
    ffn_w_in = nrm(ks[15], (DEPTH, D_MODEL, 2 * D_FF), D_MODEL ** -0.5)
    ffn_w_out = nrm(ks[16], (DEPTH, D_FF, D_MODEL), D_FF ** -0.5)
    ple_norm = gain(ks[17], (DEPTH, D_MODEL))
    ple_w_gate = nrm(ks[18], (DEPTH, D_MODEL, D_MODEL), D_MODEL ** -0.5)
    ple_w_proj = nrm(ks[19], (DEPTH, PLE_DIM, D_MODEL), PLE_DIM ** -0.5)
    final_norm = gain(ks[20], (D_MODEL,))
    return {"x": x, "p": p, "mixer_norm": mixer_norm,
            "gla_w_in": gla_w_in, "gla_w_gate_up": gla_w_gate_up, "gla_b_gate": gla_b_gate,
            "gla_out_norm": gla_out_norm, "gla_w_out": gla_w_out,
            "gdn_w_in": gdn_w_in, "gdn_conv": gdn_conv, "gdn_a_log": gdn_a_log,
            "gdn_dt_bias": gdn_dt_bias, "gdn_out_norm": gdn_out_norm, "gdn_w_out": gdn_w_out,
            "ffn_norm": ffn_norm, "ffn_w_in": ffn_w_in, "ffn_w_out": ffn_w_out,
            "ple_norm": ple_norm, "ple_w_gate": ple_w_gate, "ple_w_proj": ple_w_proj,
            "final_norm": final_norm}

def second_block(x, p, mixer_norm, gla_w_in, gla_w_gate_up, gla_b_gate, gla_out_norm, gla_w_out,
              gdn_w_in, gdn_conv, gdn_a_log, gdn_dt_bias, gdn_out_norm, gdn_w_out,
              ffn_norm, ffn_w_in, ffn_w_out, ple_norm, ple_w_gate, ple_w_proj, final_norm):
    h = x
    for i in range(DEPTH):
        j = i // NUM_MIXERS
        hn = rmsnorm(h, mixer_norm[i])
        if i % NUM_MIXERS == 0:
            mix = gla_mixer(hn, gla_w_in[j], gla_w_gate_up[j], gla_b_gate[j],
                            gla_out_norm[j], gla_w_out[j])
        else:
            mix = gdn_mixer(hn, gdn_w_in[j], gdn_conv[j], gdn_a_log[j], gdn_dt_bias[j],
                            gdn_out_norm[j], gdn_w_out[j])
        h = h + mix
        h = h + swiglu(rmsnorm(h, ffn_norm[i]), ffn_w_in[i], ffn_w_out[i])
        gate = jax.nn.sigmoid(jnp.einsum('btd,de->bte', rmsnorm(h, ple_norm[i]), ple_w_gate[i]))
        h = h + gate * jnp.einsum('btk,kd->btd', p[i], ple_w_proj[i])
    return rmsnorm(h, final_norm)


def setup_inputs(seed=0):
    out = dict(first_inputs(seed))
    for name, value in second_inputs(seed + 1).items():
        if name != "x":
            out[name + "_2"] = value
    return out


def reference(
    x, w_in, b_f, conv_w, pool_w, pool_scale, w_out, ln_g, ln_b, p_2, mixer_norm_2, gla_w_in_2,
    gla_w_gate_up_2, gla_b_gate_2, gla_out_norm_2, gla_w_out_2, gdn_w_in_2, gdn_conv_2,
    gdn_a_log_2, gdn_dt_bias_2, gdn_out_norm_2, gdn_w_out_2, ffn_norm_2, ffn_w_in_2,
    ffn_w_out_2, ple_norm_2, ple_w_gate_2, ple_w_proj_2, final_norm_2,
):
    x = first_block(
        x, w_in, b_f, conv_w, pool_w, pool_scale, w_out, ln_g, ln_b,
    )
    return second_block(
        x, p_2, mixer_norm_2, gla_w_in_2, gla_w_gate_up_2, gla_b_gate_2, gla_out_norm_2,
        gla_w_out_2, gdn_w_in_2, gdn_conv_2, gdn_a_log_2, gdn_dt_bias_2, gdn_out_norm_2,
        gdn_w_out_2, ffn_norm_2, ffn_w_in_2, ffn_w_out_2, ple_norm_2, ple_w_gate_2,
        ple_w_proj_2, final_norm_2,
    )


_drawn_inputs = setup_inputs


def setup_inputs(seed=0):
    import zlib

    import numpy as np

    out = dict(_drawn_inputs(seed))
    spreads = {}
    factors = {'pool_scale': 3.128, 'ple_norm_2': 7.545}
    for name, (base, spread) in spreads.items():
        noise = np.random.default_rng([zlib.crc32(name.encode()), seed]).standard_normal(out[name].shape)
        drawn = base * np.exp(spread * noise) if base else spread * noise
        out[name] = __import__('jax').numpy.asarray(drawn.astype(out[name].dtype))
    for name, factor in factors.items():
        out[name] = (out[name] * factor).astype(out[name].dtype)
    return out
```

```python
from contextlib import ExitStack

import concourse.bass as bass
from concourse import mybir

F32 = mybir.dt.float32
F32R = mybir.dt.float32r
I32 = mybir.dt.int32
ALU = mybir.AluOpType
ACT = mybir.ActivationFunctionType
AX_X = mybir.AxisListType.X

P = 128
N = 512
TOK = 256
TT = TOK // P
D = 2048
KD = D // P
UNIT = 2
UPP = KD // UNIT
RING = 4
ATT = 1024
NH = ATT // P
D_FF = 5632
NF = D_FF // N
ROWS_F = N // P // UNIT
PO = D // N
LN_EPS, RMS_EPS = 1e-5, 1e-6
ALPHA = 2.0 ** 0.25
GH, GDK, GDV = 4, 256, 512
RANK = 16
DB = GH * GDK // P

Q0, K0, V0, GA0, FG0 = 0, ATT, 2 * ATT, 3 * ATT, 4 * ATT
CB0 = FG0 + NH
CC0, CH0, CG0, PU0, PG0 = (CB0 + i * N for i in range(1, 6))
COLS1 = [Q0, Q0 + N, K0, K0 + N, GA0, GA0 + N, V0, V0 + N, PU0, CC0, CH0, CG0, CB0, PG0]
NP1 = len(COLS1)
(PQ, PK, PGA, PV, PPU, PCC, PCH, PCG, PCB, PPG) = (0, 2, 4, 6, 8, 9, 10, 11, 12, 13)
NPG = 12
LR0 = NPG * N

U_IN, P_IN = 0, 0
U_OUT, P_OUT = U_IN + NP1 * UPP, P_IN + NP1
U_G, P_G = U_OUT + PO * UPP, P_OUT + PO
U_GO, P_GO = U_G + NPG * UPP, P_G + NPG
U_F, P_F = U_GO + PO * UPP, P_GO + PO
U_FL, P_FL = U_F + 2 * UPP, P_F + 2
FU, FP = 2 * UPP + PO * ROWS_F, 2 + PO
U_FE, P_FE = U_FL + (NF - 1) * FU, P_FL + (NF - 1) * FP
U_PP, P_PP = U_FE + PO * ROWS_F, P_FE + PO
U_PG, P_PG = U_PP + PO, P_PP + PO
U_END = U_PG + PO * UPP

HEAD0, HEAD_STEP = U_IN + PV * UPP + 2 * UPP + 2, 4
LEVELS = [1, 2, 4, 8, 16, 32, 64, 128]
NL = len(LEVELS)
STEPS = 2 * NL
STEP0, STEP_GAP = 37, 3
AV0 = 84

V_CONV, V_PS, V_MIX, V_ON, V_FFN, V_PLE, NVEC = 0, 12, 16, 32, 36, 52, 68


def small_products():
    order = [("vec", 0)] + [("x", i) for i in range(UPP)]
    for p in range(NP1):
        for j in range(UPP):
            u = p * UPP + j
            if (p, j) == (1, 0):
                order.append(("fg", 0))
            if j == 1 and p >= 1 and p - 1 not in (PV, PV + 1):
                order += [("t", 2 * (p - 1)), ("t", 2 * (p - 1) + 1)]
            if (p, j) == (1, 2):
                order.append(("fgt", 0))
            if (p, j) == (1, 6):
                order.append(("ci", 0))
            if (p, j) == (13, 3):
                order += [("pool", 0), ("pool", 1)]
            order += head_jobs(u)
    order += [("t", 2 * PPG), ("t", 2 * PPG + 1)]
    order += [("hn", i) for i in range(UPP)]
    for g in range(NPG * UPP):
        order += [(name, i) for name, i in gla_jobs(g)]
    order += [("o", 6), ("o", 7), ("pt", 0)]
    order += [("h1", i) for i in range(2 * PO)]
    named = {}
    turns = [0, 0, 0, 0]
    for n, key in enumerate(order):
        named[key] = (n, n % 4, turns[n % 4])
        turns[n % 4] += 1
    n = len(order)
    for f in range(NF):
        for b in range(2):
            named[("a", 2 * f + b)] = (n, b, turns[b])
            turns[b] += 1
            n += 1
    for i in range(2 * PO):
        b = (2 + i) % 4
        named[("h2", i)] = (n, b, turns[b])
        turns[b] += 1
        n += 1
    return named


def panel_end(p):
    for u0, p0, units in ((U_PG, P_PG, UPP), (U_PP, P_PP, 1), (U_FE, P_FE, ROWS_F)):
        if p >= p0:
            return u0 + (p - p0 + 1) * units
    if p >= P_FL + 2:
        return U_FL + 2 * UPP + (p - P_FL - 1) * ROWS_F
    return (p + 1) * UPP


def head_jobs(u):
    found = []
    for h in range(NH):
        for name, lag in (("s", 0), ("pt_", 2), ("ot", 3)):
            if u == HEAD0 + HEAD_STEP * h + lag:
                found.append((name, h))
    return found


def gla_jobs(g):
    found = []
    if g == 8:
        found.append(("lr", 0))
    if g in (9, 17, 25, 33):
        p = (g - 9) // 8
        found += [("gt", 2 * p), ("gt", 2 * p + 1)]
    if g == 10:
        found.append(("lrt", 0))
    if 16 <= g < 20:
        found.append(("gk", g - 16))
    if g == 34:
        found += [("dg", 0), ("dg", 1)]
    if g >= STEP0 and (g - STEP0) % STEP_GAP == 0 and (g - STEP0) // STEP_GAP < STEPS:
        found.append(("step", (g - STEP0) // STEP_GAP))
    if g in (41, 42, 44, 45):
        found.append(("gk", 4 + (41, 42, 44, 45).index(g)))
    if g >= AV0 and (g - AV0) % 3 == 0 and (g - AV0) // 3 < GH:
        h = (g - AV0) // 3
        found += [("av", 2 * h), ("av", 2 * h + 1)]
    if g in (AV0 + 2, AV0 + 5, AV0 + 8):
        h = (g - AV0 - 2) // 3
        found += [("o", 2 * h), ("o", 2 * h + 1)]
    return found


def halves(ap, h):
    return ap.rearrange("p (q s r) -> p q s r", s=2, r=h)


def block_kernel(nc, x, w_in, b_f, conv_w, pool_w, pool_scale, w_out, ln_g, ln_b, p_2,
                 mixer_norm, gla_w_in, gla_w_gate_up, gla_b_gate, gla_out_norm, gla_w_out,
                 ffn_norm, ffn_w_in, ffn_w_out, ple_norm, ple_w_gate, ple_w_proj, final_norm, out):
    JOB = small_products()
    KB = 1024
    base = 16512

    def at(name, shape, dt, offset):
        return nc.alloc_sbuf_tensor_at(name, shape, dt, offset=base + offset)

    w_raw = [at(f"w_raw{s}", [P, UNIT, N], F32, s * 4 * KB) for s in range(RING)]
    w_hi = [at(f"w_hi{s}", [P, UNIT, N], F32R, (16 + s * 4) * KB) for s in range(RING)]
    w_lo = [at(f"w_lo{s}", [P, UNIT, N], F32R, (32 + s * 4) * KB) for s in range(RING)]
    a_hi = at("a_hi", [P, KD, TOK], F32R, 48 * KB)
    a_lo = at("a_lo", [P, KD, TOK], F32R, 64 * KB)
    y_hi = at("y_hi", [P, KD, TOK], F32R, 80 * KB)
    y_lo = at("y_lo", [P, KD, TOK], F32R, 96 * KB)
    x_tok = at("x_tok", [P, TT, D], F32, 80 * KB)
    decayed = [at(f"decayed{s}", [P, DB, TOK], F32, (80 + 8 * s) * KB) for s in range(3)]
    gate_up = at("gate_up", [2 * RANK + 1, 2, GH * GDK], F32, 104 * KB)
    h_tok = at("h_tok", [P, TT, D], F32, 112 * KB)
    qT = at("qT", [P, NH, TOK], F32, 112 * KB)
    kT = at("kT", [P, NH, TOK], F32, 120 * KB)
    W = 128 * KB
    stage = [at(f"stage{s}", [P, TT, N], F32, W + s * 4 * KB) for s in range(2)]
    v_tok = at("v_tok", [P, TT, ATT], F32, W + 8 * KB)
    gaT = at("gaT", [P, NH, TOK], F32, W + 16 * KB)
    PAD = 16
    poolu = at("poolu", [P, 4, PAD + TOK], F32, W + 24 * KB)
    convu = at("convu", [P, 4, 2 + TOK], F32, W + 24 * KB)
    sum_a = at("sum_a", [P, 4, PAD + TOK], F32, W + 28 * KB + 512)
    convg = at("convg", [P, 4, TOK], F32, W + 28 * KB + 512)
    sum_b = at("sum_b", [P, 4, PAD + TOK], F32, W + 33 * KB)
    convy = at("convy", [P, 4, TOK], F32, W + 33 * KB)
    poolz = at("poolz", [P, 4, TOK], F32, W + 37 * KB + 512)
    poolg = at("poolg", [P, 4, TOK], F32, W + 41 * KB + 512)
    tanh = [at(f"tanh{s}", [P, 2, TOK], F32, W + (45 + 2 * s) * KB + 512) for s in range(2)]
    logits = at("logits", [P, 3 * P], F32, W + 49 * KB + 512)
    probs = at("probs", [P, 3 * P], F32, W + 51 * KB)
    probsT = at("probsT", [P, 3 * P], F32, W + 52 * KB + 512)
    y_head = at("y_head", [P, TOK], F32, W + 54 * KB)
    sel = at("sel", [NH, NH, P], F32, W + 55 * KB)
    inv_count = at("inv_count", [P, 4, TOK], F32, W + 59 * KB)
    causal = at("causal", [P, 3 * P], F32, W + 63 * KB)
    pool_sb = at("pool_sb", [P, 4, P], F32, W + 64 * KB + 512)
    ln_gb = at("ln_gb", [P, 2, D], F32, W)
    og = [at(f"og{s}", [P, TT, N], F32, W + 4 * s * KB) for s in range(4)]
    gate_tmp = [decayed[0], at("gate_tmp", [P, DB, TOK], F32, W)]
    gv = at("gv", [P, TT, GH * GDV], F32, W + 16 * KB)
    gqT = at("gqT", [P, DB, TOK], F32, W + 32 * KB)
    gkT = at("gkT", [P, DB, TOK], F32, W + 40 * KB)
    cum = [at("cum_fwd", [P, DB, TOK], F32, W + 48 * KB), at("cum_bwd", [P, DB, TOK], F32, W + 8 * KB)]
    at_diag = at("at_diag", [P, GH, TT, P], F32, W + 56 * KB)
    at_off = at("at_off", [P, GH, 2, P], F32, W + 60 * KB)
    lr_raw = at("lr_raw", [P, KD, 2 * RANK], F32, W + 56 * KB)
    lr_hi = at("lr_hi", [P, KD, 2 * RANK], F32R, W + 58 * KB)
    lr_lo = at("lr_lo", [P, KD, 2 * RANK], F32R, W + 60 * KB)
    lrt = at("lrt", [P, TT, 2 * RANK + 1], F32, W + 64 * KB)
    lrT = at("lrT", [2 * RANK + 1, TOK], F32, W + 64 * KB + 288)
    restart = at("restart", [P, TOK + 1], F32, W + 65 * KB + 288)
    act_tok = at("act_tok", [P, TT, N], F32, W)
    act_hi = at("act_hi", [P, N // P, TOK], F32R, W + 4 * KB)
    act_lo = at("act_lo", [P, N // P, TOK], F32R, W + 8 * KB)
    emb = at("emb", [P, TT, D], F32, W + 16 * KB)
    fin_w = at("fin_w", [P, D], F32, W + 32 * KB)
    gate_tok = at("gate_tok", [P, TT, N], F32, W + 40 * KB)
    p_hi = at("p_hi", [P, UNIT, TOK], F32R, W + 44 * KB)
    p_lo = at("p_lo", [P, UNIT, TOK], F32R, W + 46 * KB)
    p_tok = at("p_tok", [P, TT, 2 * P], F32, W + 48 * KB)
    C = W + 66 * KB + 512
    off = [C]

    def small(name, shape, dt=F32):
        size = 4
        for s in shape[1:]:
            size *= s
        t = at(name, shape, dt, off[0])
        off[0] += (size + 31) // 32 * 32
        return t

    ident = small("ident", [P, P])
    masks = small("masks", [P, NL - 1, 2, 64])
    vec_raw = small("vec_raw", [NVEC, P])
    vec = small("vec", [P, NVEC])
    square = small("square", [P, N])
    fg_raw = small("fg_raw", [P, KD, NH])
    fg_hi = small("fg_hi", [P, KD, NH], F32R)
    fg_lo = small("fg_lo", [P, KD, NH], F32R)
    fg_tok = small("fg_tok", [P, TT, NH])
    ncum = small("ncum", [NH, TOK])
    fgz = at("fgz", [NH, TOK], F32, W + 49 * KB + 512)
    fge = at("fge", [NH, TOK], F32, W + 51 * KB)
    cum_i = small("cum_i", [P, TT, NH])
    bf_col = small("bf_col", [NH, 1])
    neg_max = small("neg_max", [P, 2])
    row_sum = small("row_sum", [P, 2])
    inv_sum = small("inv_sum", [P, 2])
    bn = small("bn", [P, TT, PO, 6])
    mv = small("mv", [P, TT, 2])
    ms = small("ms", [P, TT])
    minus_half = small("minus_half", [P, TT])
    rstd = [small(f"rstd{i}", [P, TT]) for i in range(4)]
    ssq = [small(f"ssq{i}", [P, TT, PO]) for i in range(3)]
    o_ssq = small("o_ssq", [P, GH, TT])
    o_ms = small("o_ms", [P, GH, TT])
    o_rstd = small("o_rstd", [P, GH, TT])
    iota_i = at("iota_i", [P, TOK], I32, W + 45 * KB + 512)
    iota_f = at("iota_f", [P, TOK], F32, W + 46 * KB + 512)
    assert base + off[0] <= 229344, off[0]

    with ExitStack() as ctx:
        def sem(name):
            return ctx.enter_context(nc.semaphore(name))

        acc = [ctx.enter_context(nc.psum_tensor(f"acc{i}", [P, N], F32)) for i in range(4)]
        aux = [ctx.enter_context(nc.psum_tensor(f"aux{i}", [P, N], F32)) for i in range(4)]

        landed = [sem(f"landed{s}") for s in range(RING)]
        hi_done, lo_done = sem("hi_done"), sem("lo_done")
        unit_used = sem("unit_used")
        acc_read = [sem(f"acc_read{b}") for b in range(2)]
        aux_done = sem("aux_done")
        aux_read = [sem(f"aux_read{b}") for b in range(4)]
        x_in, x_back = sem("x_in"), sem("x_back")
        vec_in, fg_in, pool_in = sem("vec_in"), sem("fg_in"), sem("pool_in")
        gb_in, lr_in, up_in, p_in, fin_in = (sem(n) for n in ("gb_in", "lr_in", "up_in", "p_in", "fin_in"))
        up_clear = sem("up_clear")
        consts = sem("consts")
        zeros = sem("zeros")
        x_hi_done, hn_hi_done, o_hi_done, h1_hi_done = (sem(n) for n in ("x_hi_done", "hn_hi_done", "o_hi_done", "h1_hi_done"))
        act_hi_done, h2_hi_done, p_hi_done, fg_hi_done, lr_hi_done = (
            sem(n) for n in ("act_hi_done", "h2_hi_done", "p_hi_done", "fg_hi_done", "lr_hi_done"))
        fg_split, lr_split = sem("fg_split"), sem("lr_split")
        tanh_done = sem("tanh_done")
        fg_abs, fg_exp, fg_ln, fg_cum, fg_neg = (
            sem(n) for n in ("fg_abs", "fg_exp", "fg_ln", "fg_cum", "fg_neg"))
        max_done, exp_done, inv_done, probs_done, y_hi_done, y_done = (
            sem(n) for n in ("max_done", "exp_done", "inv_done", "probs_done", "y_hi_done", "y_done"))
        mixed = sem("mixed")
        z_done = sem("z_done")
        bn_done, var_done, ms_done, rstd_done = (sem(n) for n in ("bn_done", "var_done", "ms_done", "rstd_done"))
        centred, ln_dve, ln_pool = sem("centred"), sem("ln_dve"), sem("ln_pool")
        ssq_done = sem("ssq_done")
        gk_min, gk_exp, gk_abs, gk_ln, cum_done = (sem(n) for n in ("gk_min", "gk_exp", "gk_abs", "gk_ln", "cum_done"))
        diff_done, decay_done, mul_dve, mul_pool = (sem(n) for n in ("diff_done", "decay_done", "mul_dve", "mul_pool"))
        o_sq, o_ms_done, o_rstd_done = (sem(n) for n in ("o_sq", "o_ms_done", "o_rstd_done"))
        gated, h_added, scaled = sem("gated"), sem("h_added"), sem("scaled")
        stored = sem("stored")
        dve_step = sem("dve_step")
        act_step = sem("act_step")

        block = ctx.enter_context(nc.Block())

        def job(name, i=0):
            return JOB[(name, i)]

        def job_done(eng, name, i=0):
            eng.wait_ge(aux_done, job(name, i)[0] + 1)

        def job_read(eng, name, i=0):
            _, bank, turn = job(name, i)
            eng.wait_ge(aux_read[bank], turn + 1)

        def bank_of(name, i=0):
            return aux[job(name, i)[1]]

        def read_of(name, i=0):
            return aux_read[job(name, i)[1]]

        def panel_banks(p):
            return acc[2 * (p % 2)], acc[2 * (p % 2) + 1]

        def panel_done(eng, p, i=0, uper=0):
            eng.wait_ge(unit_used, i * uper + panel_end(p))

        def panel_read(eng, p, tiles=2, i=0, per=0):
            eng.wait_ge(acc_read[p % 2], i * per + (2 * (p // 2) + tiles))

        @block.sync
        def _(sp):
            def load(u, src, i=0, per=0):
                if u >= RING:
                    sp.wait_ge(lo_done, i * per + (u - RING + 1))
                    if per:
                        sp.nop(nofuse=True)
                sp.dma_start(w_raw[u % RING][:], src).then_inc(landed[u % RING], 16)

            def rows(w, r, col):
                return w[r:r + UNIT * P, col].rearrange("(c p) n -> p c n", p=P)

            def panel(w, u, col, i=0, per=0):
                for j in range(UPP):
                    load(u + j, rows(w, j * UNIT * P, col), i, per)

            xs = x[0].rearrange("(t p) d -> p t d", p=P)
            for c in range(4):
                sp.dma_start(x_tok[:, :, c * N:(c + 1) * N], xs[:, :, c * N:(c + 1) * N]).then_inc(x_in, 16)
            for p, c in enumerate(COLS1):
                panel(w_in[0], U_IN + p * UPP, slice(c, c + N))
            with sp.Fori(0, PO) as n:
                panel(w_out[0], U_OUT, bass.ds(n * N, N), n, UPP)
            with sp.Fori(0, NPG) as n:
                panel(gla_w_in[0], U_G, bass.ds(n * N, N), n, UPP)
            with sp.Fori(0, PO) as n:
                panel(gla_w_out[0], U_GO, bass.ds(n * N, N), n, UPP)
            panel(ffn_w_in[0], U_F, slice(0, N))
            panel(ffn_w_in[0], U_F + UPP, slice(D_FF, D_FF + N))

            def out_rows(f, n, k):
                r = f * N + k * UNIT * P
                return ffn_w_out[0][bass.ds(r, UNIT * P), n * N:(n + 1) * N].rearrange("(c p) n -> p c n", p=P)

            with sp.Fori(0, NF - 1) as f:
                panel(ffn_w_in[0], U_FL, bass.ds(f * N + N, N), f, FU)
                panel(ffn_w_in[0], U_FL + UPP, bass.ds(f * N + (D_FF + N), N), f, FU)
                for n in range(PO):
                    for k in range(ROWS_F):
                        load(U_FL + 2 * UPP + n * ROWS_F + k, out_rows(f, n, k), f, FU)
            for n in range(PO):
                for k in range(ROWS_F):
                    load(U_FE + n * ROWS_F + k, out_rows(NF - 1, n, k))
            for n in range(PO):
                load(U_PP + n, rows(ple_w_proj[0], 0, slice(n * N, (n + 1) * N)))
            with sp.Fori(0, PO) as n:
                panel(ple_w_gate[0], U_PG, bass.ds(n * N, N), n, UPP)
            outs = out[0].rearrange("(t p) d -> p t d", p=P)
            for t in range(TT):
                for c in range(2):
                    sp.wait_ge(scaled, 2 * t + c + 1)
                    sp.dma_start(outs[:, t, c * 1024:(c + 1) * 1024],
                                 h_tok[:, t, c * 1024:(c + 1) * 1024]).then_inc(stored, 16)
            sp.wait_ge(stored, 16 * 2 * TT)

        @block.gpsimd
        def _(pool):
            with nc.allow_non_contiguous_dma(reason="columns of eight"):
                pool.dma_start(fg_raw[:], w_in[0][:, FG0:FG0 + NH].rearrange("(c p) n -> p c n", p=P)).then_inc(fg_in, 16)
            for r, n, src in ((V_CONV, 12, conv_w[0].rearrange("k (b p) -> (k b) p", p=P)),
                              (V_PS, 4, pool_scale[0].rearrange("(b p) -> b p", p=P)),
                              (V_MIX, 16, mixer_norm[0].rearrange("(b p) -> b p", p=P)),
                              (V_ON, 4, gla_out_norm[0].rearrange("(b p) -> b p", p=P)),
                              (V_FFN, 16, ffn_norm[0].rearrange("(b p) -> b p", p=P)),
                              (V_PLE, 16, ple_norm[0].rearrange("(b p) -> b p", p=P))):
                pool.dma_start(vec_raw[r:r + n, :], src).then_inc(vec_in, 16)
            pool.dma_start(bf_col[:], b_f[0].rearrange("(h a) -> h a", a=1)).then_inc(vec_in, 16)
            pool.dma_start(pool_sb[:], pool_w[0].rearrange("g c d -> c g d")).then_inc(pool_in, 16)
            nc.gpsimd.memset(ident[:], 0.0).then_inc(consts, 1)
            pool.wait_ge(consts, 1)
            nc.gpsimd.affine_select(ident[:], ident[:], [[-1, P]], ALU.not_equal, 1.0, base=0,
                                    channel_multiplier=1).then_inc(consts, 1)
            nc.gpsimd.memset(sel[:], 0.0).then_inc(consts, 1)
            pool.wait_ge(consts, 3)
            nc.gpsimd.affine_select(sel[:], sel[:], [[-1, NH], [0, P]], ALU.not_equal, 1.0, base=0,
                                    channel_multiplier=1).then_inc(consts, 1)
            nc.gpsimd.memset(causal[:], 0.0).then_inc(consts, 1)
            pool.wait_ge(consts, 5)
            for c in (0, 2 * P):
                nc.gpsimd.affine_select(causal[:, c:c + P], causal[:, c:c + P], [[-1, P]], ALU.is_ge, -3.0e38,
                                        base=0, channel_multiplier=1).then_inc(consts, 1)
            nc.gpsimd.iota(iota_i[:], [[1, TOK]], base=1, channel_multiplier=0).then_inc(consts, 1)
            pool.wait_ge(consts, 8)
            nc.gpsimd.tensor_copy(iota_f[:], iota_i[:]).then_inc(consts, 1)
            nc.gpsimd.memset(minus_half[:], -0.5).then_inc(consts, 1)
            nc.gpsimd.memset(masks[:], 1.0).then_inc(consts, 1)
            pool.wait_ge(consts, 11)
            k = 11
            for li, h in enumerate(LEVELS[:-1]):
                nb = P // (2 * h)
                for way in range(2):
                    m = masks[:, li, way, :].rearrange("p (b r) -> p b r", r=h)
                    lo = h * way
                    nc.gpsimd.affine_select(m, m, [[-2 * h, nb], [0, h]], ALU.is_ge, 0.0, base=-lo,
                                            channel_multiplier=1).then_inc(consts, 1)
                    k += 1
                    pool.wait_ge(consts, k)
                    nc.gpsimd.affine_select(m, m, [[2 * h, nb], [0, h]], ALU.is_ge, 0.0, base=lo + h - 1,
                                            channel_multiplier=-1).then_inc(consts, 1)
                    k += 1
                    pool.wait_ge(consts, k)

            job_done(pool, "s", NH - 1)
            pool.dma_start(h_tok[:], x[0].rearrange("(t p) d -> p t d", p=P)).then_inc(x_back, 16)
            pool.wait_ge(y_done, NH + 2)
            pool.dma_start(ln_gb[:, 0, :], ln_g[0].partition_broadcast(P)).then_inc(gb_in, 16)
            pool.dma_start(ln_gb[:, 1, :], ln_b[0].partition_broadcast(P)).then_inc(gb_in, 16)
            pool.dma_start(lr_raw[:], gla_w_in[0][:, LR0:LR0 + 2 * RANK].rearrange("(c p) n -> p c n", p=P)).then_inc(lr_in, 16)
            pool.wait_ge(unit_used, U_G)
            nc.gpsimd.memset(gate_up[:], 0.0).then_inc(up_clear, 1)
            pool.wait_ge(up_clear, 1)
            for z in range(2):
                pool.dma_start(gate_up[z * RANK:(z + 1) * RANK, z, :], gla_w_gate_up[0, z]).then_inc(up_in, 16)
                pool.dma_start(gate_up[2 * RANK:2 * RANK + 1, z, :], gla_b_gate[0, z:z + 1, :]).then_inc(up_in, 16)
            pool.wait_ge(ms_done, 1)
            nc.gpsimd.tensor_tensor(rstd[0][:], ms[:], minus_half[:], ALU.pow).then_inc(rstd_done, 1)
            pool.wait_ge(centred, 2)
            pool.wait_ge(gb_in, 32)
            for n in (2, 3):
                s = slice(n * N, (n + 1) * N)
                nc.gpsimd.tensor_tensor(h_tok[:, 1, s], h_tok[:, 1, s], ln_gb[:, 0, s], ALU.mult).then_inc(ln_pool, 1)
                pool.wait_ge(ln_pool, 2 * (n - 2) + 1)
                nc.gpsimd.tensor_tensor(h_tok[:, 1, s], h_tok[:, 1, s], ln_gb[:, 1, s], ALU.add).then_inc(ln_pool, 1)
            pool.wait_ge(ms_done, 2)
            nc.gpsimd.tensor_tensor(rstd[1][:], ms[:], minus_half[:], ALU.pow).then_inc(rstd_done, 1)
            for s in range(STEPS):
                way, h = s // NL, LEVELS[s % NL]
                pool.wait_ge(decay_done, s + 1)
                if s == 0:
                    for i in range(8):
                        job_read(pool, "gt", i)
                if s == NL:
                    pool.dma_start(p_tok[:], p_2[0, 0].rearrange("(t p) d -> p t d", p=P)).then_inc(p_in, 16)
                d = halves(decayed[s % 3][:].rearrange("p d t -> p (d t)"), h)
                src = halves((gkT, gqT)[way][:].rearrange("p d t -> p (d t)"), h)
                nc.gpsimd.tensor_tensor(d[:, :, 0, :], d[:, :, 0, :], src[:, :, 0, :], ALU.mult).then_inc(mul_pool, 1)
            for hd in range(GH):
                pool.wait_ge(o_ms_done, hd + 1)
                nc.gpsimd.tensor_tensor(o_rstd[:, hd, :], o_ms[:, hd, :], minus_half[:], ALU.pow).then_inc(o_rstd_done, 1)
            pool.wait_ge(unit_used, U_GO + UPP)
            pool.dma_start(fin_w[:], final_norm.partition_broadcast(P)).then_inc(fin_in, 16)
            for i in (2, 3):
                pool.wait_ge(ms_done, i + 1)
                nc.gpsimd.tensor_tensor(rstd[i][:], ms[:], minus_half[:], ALU.pow).then_inc(rstd_done, 1)
            pool.wait_ge(ms_done, 5)
            nc.gpsimd.tensor_tensor(rstd[0][:], ms[:], minus_half[:], ALU.pow).then_inc(rstd_done, 1)

        @block.tensor
        def _(pe):
            def unit(u, p, hi, lo, k, first, last, i=0, per=0, pper=0):
                pe.wait_ge(lo_done, i * per + (u + 1))
                if first and p >= 2:
                    panel_read(pe, p - 2, 2, i, pper)
                banks = panel_banks(p)
                for c in range(UNIT):
                    for t in range(TT):
                        tok = slice(t * P, (t + 1) * P)
                        st, en = first and c == 0, last and c == UNIT - 1
                        wh, wl = w_hi[u % RING][:, c, :], w_lo[u % RING][:, c, :]
                        pe.matmul(banks[t][:], hi[:, k + c, tok], wh, start=st, stop=False)
                        pe.matmul(banks[t][:], hi[:, k + c, tok], wl, start=False, stop=False)
                        mm = pe.matmul(banks[t][:], lo[:, k + c, tok], wh, start=False, stop=en)
                mm.then_inc(unit_used, 1)

            def begin(name, i=0):
                _, bank, turn = job(name, i)
                if turn:
                    pe.wait_ge(aux_read[bank], turn)
                return aux[bank]

            def turn_tiles(src, b, cols):
                for k in range(2):
                    for t in range(TT):
                        mm = pe.transpose(b[:, (k * TT + t) * P:(k * TT + t + 1) * P],
                                          src[:, t, cols + k * P:cols + (k + 1) * P], ident[:])
                return mm

            pe.wait_ge(consts, 2)
            pe.wait_ge(vec_in, 7 * 16)
            b = begin("vec")
            pe.transpose(b[:, 0:NVEC], vec_raw[:], ident[0:NVEC, 0:NVEC]).then_inc(aux_done, 1)

            def turn_x(c):
                if c % 2 == 0:
                    pe.wait_ge(x_in, 16 * 4)
                b = begin("x", c)
                turn_tiles(x_tok, b, 2 * c * P).then_inc(aux_done, 1)

            def turn_stage(p):
                panel_read(pe, P_IN + p)
                for i in range(2):
                    b = begin("t", 2 * p + i)
                    turn_tiles(stage[p % 2], b, 2 * i * P).then_inc(aux_done, 1)

            def thin(name, hi, lo, n):
                b = begin(name)
                for t in range(TT):
                    tok = slice(t * P, (t + 1) * P)
                    o = b[:, t * n:(t + 1) * n]
                    for k in range(KD):
                        pe.matmul(o, a_hi[:, k, tok], hi[:, k, :], start=k == 0, stop=False)
                        pe.matmul(o, a_hi[:, k, tok], lo[:, k, :], start=False, stop=False)
                        mm = pe.matmul(o, a_lo[:, k, tok], hi[:, k, :], start=False, stop=k == KD - 1)
                mm.then_inc(aux_done, 1)

            def scores(h):
                if h == 0:
                    job_read(pe, "ci")
                b = begin("s", h)
                for c, n, q in ((0, P, 0), (P, TOK, P)):
                    o = b[:, c:c + n]
                    pe.matmul(o, qT[:, h, q:q + P], kT[:, h, 0:n], start=True, stop=False)
                    mm = pe.matmul(o, sel[:, h, :], ncum[:, 0:n], start=False, stop=True)
                mm.then_inc(aux_done, 1)

            def turn_probs(h):
                b = begin("pt_", h)
                pe.wait_ge(probs_done, 2 * (h + 1))
                for c in range(3):
                    mm = pe.transpose(b[:, c * P:(c + 1) * P], probs[:, c * P:(c + 1) * P], ident[:])
                mm.then_inc(aux_done, 1)

            def weigh_values(h):
                job_read(pe, "pt_", h)
                b = begin("ot", h)
                f = slice(h * P, (h + 1) * P)
                pe.matmul(b[:, 0:TOK], v_tok[:, 0, f], probsT[:, 0:TOK], start=True, stop=False)
                pe.matmul(b[:, P:TOK], v_tok[:, 1, f], probsT[:, TOK:3 * P], start=False,
                          stop=True).then_inc(aux_done, 1)

            for c in range(4):
                turn_x(c)
            for p in range(NP1):
                for j in range(UPP):
                    u = U_IN + p * UPP + j
                    if p == 0:
                        job_read(pe, "x", j)
                    unit(u, P_IN + p, a_hi, a_lo, 2 * j, j == 0, j == UPP - 1)
                    if p == 0 and j < 4:
                        turn_x(4 + j)
                    if (p, j) == (1, 0):
                        pe.wait_ge(fg_split, 1)
                        thin("fg", fg_hi, fg_lo, NH)
                    if j == 1 and p >= 1 and p - 1 not in (PV, PV + 1):
                        turn_stage(p - 1)
                    if (p, j) == (1, 2):
                        job_read(pe, "fg")
                        b = begin("fgt")
                        for t in range(TT):
                            mm = pe.transpose(b[0:NH, t * P:(t + 1) * P], fg_tok[:, t, :], ident[:])
                        mm.then_inc(aux_done, 1)
                    if (p, j) == (1, 6):
                        pe.wait_ge(fg_cum, 1)
                        b = begin("ci")
                        for t in range(TT):
                            mm = pe.transpose(b[:, t * NH:(t + 1) * NH], fgz[:, t * P:(t + 1) * P], ident[0:NH, 0:NH])
                        mm.then_inc(aux_done, 1)
                    if (p, j) == (13, 3):
                        pe.wait_ge(z_done, 1)
                        pe.wait_ge(pool_in, 16)
                        for i in range(2):
                            b = begin("pool", i)
                            for k in range(2):
                                mm = pe.matmul(b[:, k * TOK:(k + 1) * TOK], pool_sb[:, 2 * i + k, :],
                                               poolz[:, 2 * i + k, :], start=True, stop=True)
                            mm.then_inc(aux_done, 1)
                    for name, h in head_jobs(u):
                        {"s": scores, "pt_": turn_probs, "ot": weigh_values}[name](h)

            def out_panel(n, j, i=0, per=0, pper=0):
                unit(U_OUT + n * UPP + j, P_OUT + n, y_hi, y_lo, 2 * j, j == 0, j == UPP - 1, i, per, pper)

            for j in range(UPP):
                pe.wait_ge(y_done, NH if j < 4 else NH + 1 if j < 6 else NH + 2)
                out_panel(0, j)
                if j == 1:
                    turn_stage(PPG)
            for n in range(1, PO):
                for j in range(UPP):
                    out_panel(n, j)

            def turn_hn(c):
                n = c // 2
                pe.wait_ge(ln_dve, 2 * (2 * (n + 1)) if n < 2 else 8 + 2 * (n - 1))
                if n >= 2:
                    pe.wait_ge(ln_pool, 2 * (n - 1))
                b = begin("hn", c)
                turn_tiles(h_tok, b, 2 * c * P).then_inc(aux_done, 1)

            def diagonal(i):
                b = begin("dg", i)
                for c in range(4):
                    hd, t = 2 * i + c // 2, c % 2
                    tok = slice(t * P, (t + 1) * P)
                    for kb in range(2):
                        mm = pe.matmul(b[:, c * P:(c + 1) * P], gkT[:, 2 * hd + kb, tok], gqT[:, 2 * hd + kb, tok],
                                       start=kb == 0, stop=kb == 1)
                mm.then_inc(aux_done, 1)

            def step(s):
                way, h = s // NL, LEVELS[s % NL]
                pe.wait_ge(mul_dve, s + 1)
                pe.wait_ge(mul_pool, s + 1)
                b = begin("step", s)
                d = decayed[s % 3]
                if h == P:
                    for hd in range(GH):
                        for kb in range(2):
                            tiles = [d[:, 2 * hd + kb, t * P:(t + 1) * P] for t in range(TT)]
                            mm = pe.matmul(b[:, hd * P:(hd + 1) * P], tiles[way], tiles[1 - way],
                                           start=kb == 0, stop=kb == 1)
                else:
                    for c in range(GH * TT):
                        hd, t = c // 2, c % 2
                        for kb in range(2):
                            tile = d[:, 2 * hd + kb, t * P:(t + 1) * P]
                            mm = pe.matmul(b[:, c * 64:(c + 1) * 64], tile, halves(tile, h)[:, :, 1 - way, :],
                                           start=kb == 0, stop=kb == 1)
                mm.then_inc(aux_done, 1)

            def apply_values(hd):
                f = slice(hd * GDV, (hd + 1) * GDV)
                if hd == 0:
                    job_read(pe, "step", STEPS - 1)
                    panel_read(pe, P_G + 7)
                for t in range(TT):
                    b = begin("av", 2 * hd + t)
                    pe.matmul(b[:], at_diag[:, hd, t, :], gv[:, t, f], start=True, stop=False)
                    pe.matmul(b[:], at_off[:, hd, 1 - t, :], gv[:, 1 - t, f], start=False,
                              stop=True).then_inc(aux_done, 1)

            def turn_o(hd):
                for t in range(TT):
                    job_read(pe, "av", 2 * hd + t)
                for i in range(2):
                    b = begin("o", 2 * hd + i)
                    turn_tiles(og[hd], b, 2 * i * P).then_inc(aux_done, 1)

            for c in range(4):
                turn_hn(c)
            for g in range(NPG * UPP):
                p, j = g // UPP, g % UPP
                if p == 0:
                    job_read(pe, "hn", j)
                unit(U_G + g, P_G + p, a_hi, a_lo, 2 * j, j == 0, j == UPP - 1)
                if g < 4:
                    turn_hn(4 + g)
                for name, i in gla_jobs(g):
                    if name == "lr":
                        pe.wait_ge(lr_split, 1)
                        thin("lr", lr_hi, lr_lo, 2 * RANK)
                    if name == "gt":
                        if i % 2 == 0:
                            panel_read(pe, P_G + i // 2)
                        b = begin("gt", i)
                        turn_tiles(og[i // 2], b, 2 * (i % 2) * P).then_inc(aux_done, 1)
                    if name == "lrt":
                        job_read(pe, "lr")
                        b = begin("lrt")
                        for t in range(TT):
                            mm = pe.transpose(b[0:2 * RANK + 1, t * P:(t + 1) * P], lrt[:, t, :], ident[:])
                        mm.then_inc(aux_done, 1)
                    if name == "gk":
                        if i == 0:
                            job_read(pe, "lrt")
                            pe.wait_ge(up_in, 64)
                        b = begin("gk", i)
                        for k in range(2):
                            blk = 2 * (i % 4) + k
                            mm = pe.matmul(b[:, k * TOK:(k + 1) * TOK], gate_up[:, i // 4, blk * P:(blk + 1) * P],
                                           lrT[:], start=True, stop=True)
                        mm.then_inc(aux_done, 1)
                    if name == "dg":
                        if i == 0:
                            job_read(pe, "gt", 6)
                            job_read(pe, "gt", 7)
                        diagonal(i)
                    if name == "step":
                        step(i)
                    if name == "av" and i % 2 == 0:
                        apply_values(i // 2)
                    if name == "o" and i % 2 == 0:
                        turn_o(i // 2)

            def turn_h(name, i, panel):
                b = begin(name, i)
                turn_tiles(h_tok, b, i * 2 * P).then_inc(aux_done, 1)

            for n in range(PO):
                for j in range(UPP):
                    if n == 0 and j == 0:
                        for i in range(6):
                            job_read(pe, "o", i)
                    if n == 0 and j == 6:
                        job_read(pe, "o", 6)
                        job_read(pe, "o", 7)
                    unit(U_GO + n * UPP + j, P_GO + n, y_hi, y_lo, 2 * j, j == 0, j == UPP - 1)
                    if n == 0 and j == 1:
                        turn_o(3)
                        pe.wait_ge(p_in, 16)
                        b = begin("pt")
                        turn_tiles(p_tok, b, 0).then_inc(aux_done, 1)
                    if n >= 1 and j == 1:
                        panel_read(pe, P_GO + n - 1)
                        turn_h("h1", 2 * n - 2, n - 1)
                        turn_h("h1", 2 * n - 1, n - 1)

            for j in range(UPP):
                job_read(pe, "h1", j)
                unit(U_F + j, P_F, a_hi, a_lo, 2 * j, j == 0, j == UPP - 1)
                if j == 1:
                    panel_read(pe, P_GO + 3)
                    turn_h("h1", 6, 3)
                    turn_h("h1", 7, 3)
            for j in range(UPP):
                unit(U_F + UPP + j, P_F + 1, a_hi, a_lo, 2 * j, j == 0, j == UPP - 1)

            def turn_act(f, i=0):
                panel_read(pe, P_F + 1 + f * FP, 2, i, FP)
                for k in range(2):
                    n, bank, turn = job("a", 2 * f + k)
                    pe.wait_ge(aux_read[bank], i + turn)
                    turn_tiles(act_tok, aux[bank], 2 * k * P).then_inc(aux_done, 1)

            def hidden_rows(u, p, n, i=0, per=0, pper=0):
                for k in range(ROWS_F):
                    unit(u + n * ROWS_F + k, p + n, act_hi, act_lo, 2 * k, k == 0, k == ROWS_F - 1, i, per, pper)

            turn_act(0)
            with pe.Fori(0, NF - 1) as f:
                for m in range(2):
                    for j in range(UPP):
                        unit(U_FL + m * UPP + j, P_FL + m, a_hi, a_lo, 2 * j, j == 0, j == UPP - 1, f, FU, FP)
                for k in range(2):
                    n, bank, turn = job("a", k)
                    pe.wait_ge(aux_read[bank], f + (turn + 1))
                for n in range(PO):
                    hidden_rows(U_FL + 2 * UPP, P_FL + 2, n, f, FU, FP)
                turn_act(1, f)
            for k in range(2):
                job_read(pe, "a", 2 * (NF - 1) + k)
            for n in range(PO):
                hidden_rows(U_FE, P_FE, n)
                if n >= 1:
                    panel_read(pe, P_FE + n - 1)
                    turn_h("h2", 2 * n - 2, n - 1)
                    turn_h("h2", 2 * n - 1, n - 1)
            job_read(pe, "pt")
            for n in range(PO):
                unit(U_PP + n, P_PP + n, p_hi, p_lo, 0, True, True)
                if n == 1:
                    panel_read(pe, P_FE + 3)
                    turn_h("h2", 6, 3)
                    turn_h("h2", 7, 3)
            for j in range(UPP):
                job_read(pe, "h2", j)
            with pe.Fori(0, PO // 2) as n:
                for m in range(2):
                    for j in range(UPP):
                        unit(U_PG + m * UPP + j, P_PG + m, a_hi, a_lo, 2 * j, j == 0, j == UPP - 1, n, 2 * UPP, 2)

        @block.scalar
        def _(act):
            def high(u, i=0, per=0):
                turns = per // RING
                act.wait_ge(landed[u % RING], (16 * turns) * i + 16 * (u // RING + 1))
                if u >= RING:
                    act.wait_ge(unit_used, i * per + (u - RING + 1))
                nc.scalar.copy(w_hi[u % RING][:], w_raw[u % RING][:]).then_inc(hi_done, 1)

            def stage_panel(p, dst, scale=None, func=ACT.Copy, i=0, uper=0):
                panel_done(act, p, i, uper)
                for t, b in enumerate(panel_banks(p)):
                    s = 1.0 if scale is None else scale[:, t:t + 1]
                    nc.scalar.activation(dst[:, t, :], b[:], func, scale=s).then_inc(acc_read[p % 2], 1)

            def split_high(name, i, dst, c, done, col=None):
                job_done(act, name, i)
                b = bank_of(name, i)
                if col is None:
                    nc.scalar.copy(dst[:, c:c + 2, :], b[:].rearrange("p (k t) -> p k t", t=TOK)).then_inc(done, 1)
                    return
                for k in range(2):
                    nc.scalar.activation(dst[:, c + k, :], b[:, k * TOK:(k + 1) * TOK], ACT.Copy,
                                         scale=vec[:, col + k:col + k + 1]).then_inc(done, 1)

            counts = {id(ssq_done): 0, id(o_sq): 0}
            last_square = []

            def sum_of_squares(src, dst, done):
                if last_square:
                    act.wait_ge(*last_square[-1])
                nc.scalar.activation(square[:], src, ACT.Square, accum_out=dst).then_inc(done, 1)
                counts[id(done)] += 1
                last_square.append((done, counts[id(done)]))

            for c in range(UPP):
                split_high("x", c, a_hi, 2 * c, x_hi_done)
                if c < RING:
                    high(c)
                if c == 4:
                    act.wait_ge(fg_in, 16)
                    nc.scalar.copy(fg_hi[:], fg_raw[:]).then_inc(fg_hi_done, 1)
                if c >= 4:
                    high(c)
            tanhs = [0]

            def gate_tanh(i):
                job_done(act, "t", i)
                if tanhs[0] >= 2:
                    job_read(act, "t", last_gate[tanhs[0] - 2])
                nc.scalar.activation(tanh[i % 2][:].rearrange("p k t -> p (k t)"), bank_of("t", i)[:], ACT.Tanh,
                                     scale=0.5).then_inc(tanh_done, 1)
                tanhs[0] += 1

            last_gate = [2 * p + k for p in (PGA, PGA + 1, PCG, PPG) for k in range(2)]

            for p in range(NP1):
                for j in range(UPP):
                    u = U_IN + p * UPP + j
                    if u >= 4:
                        high(u + RING)
                    if (p, j) == (1, 0):
                        job_done(act, "fg")
                        nc.scalar.copy(fg_tok[:].rearrange("p t n -> p (t n)"), bank_of("fg")[:, 0:TT * NH]).then_inc(read_of("fg"), 1)
                    if j == 1 and p >= 1:
                        q = p - 1
                        for i in (2 * q, 2 * q + 1):
                            src = bank_of("t", i)[:].rearrange("p (k t) -> p k t", t=TOK) if ("t", i) in JOB else None
                            if q in (PQ, PQ + 1):
                                job_done(act, "t", i)
                                nc.scalar.activation(qT[:, 2 * i:2 * i + 2, :], src, ACT.Copy,
                                                     scale=float(P) ** -0.5).then_inc(read_of("t", i), 1)
                            if q == PCC:
                                job_done(act, "t", i)
                                k = 2 * (i % 2)
                                act.wait_ge(zeros, 2)
                                nc.scalar.copy(convu[:, k:k + 2, 2:], src).then_inc(read_of("t", i), 1)
                            if q == PPU:
                                job_done(act, "t", i)
                                k = 2 * (i % 2)
                                act.wait_ge(zeros, 1)
                                nc.scalar.copy(poolu[:, k:k + 2, PAD:], src).then_inc(read_of("t", i), 1)
                            if q in (PGA, PGA + 1, PCG):
                                gate_tanh(i)
                    if (p, j) == (1, 3):
                        job_read(act, "fgt")
                        nc.scalar.activation(fge[:], fgz[:], ACT.Abs).then_inc(fg_abs, 1)
                        act.wait_ge(fg_abs, 1)
                        nc.scalar.activation(fge[:], fge[:], ACT.Exp, scale=-1.0).then_inc(fg_exp, 1)
                        act.wait_ge(fg_exp, 1)
                        nc.scalar.activation(fge[:], fge[:], ACT.Ln, bias=1.0).then_inc(fg_ln, 1)
                    if (p, j) == (1, 6):
                        job_done(act, "ci")
                        nc.scalar.copy(cum_i[:].rearrange("p t n -> p (t n)"), bank_of("ci")[:, 0:TT * NH]).then_inc(read_of("ci"), 1)
                    for h in range(NH):
                        if u == HEAD0 + HEAD_STEP * h:
                            act.wait_ge(max_done, h + 1)
                            if h:
                                job_done(act, "pt_", h - 1)
                            for t, c in ((0, slice(0, P)), (1, slice(P, 3 * P))):
                                nc.scalar.activation(probs[:, c], logits[:, c], ACT.Exp, bias=neg_max[:, t:t + 1],
                                                     accum_out=row_sum[:, t:t + 1]).then_inc(exp_done, 1)
                        if u == HEAD0 + HEAD_STEP * h + 2:
                            job_done(act, "pt_", h)
                            if h:
                                job_done(act, "ot", h - 1)
                            nc.scalar.copy(probsT[:], bank_of("pt_", h)[:, 0:3 * P]).then_inc(read_of("pt_", h), 1)
                        if u == HEAD0 + HEAD_STEP * h + 3:
                            job_read(act, "ot", h)
                            nc.scalar.activation(y_hi[:, h, :], y_head[:], ACT.Copy, scale=0.5).then_inc(y_hi_done, 1)
                    if (p, j) == (13, 4):
                        act.wait_ge(mixed, 1)
                        nc.scalar.activation(y_hi[:, 8:12, :], convy[:], ACT.Copy, scale=0.5).then_inc(y_hi_done, 1)
                    if j == UPP - 1:
                        if p >= 2 and ("t", 2 * (p - 2)) in JOB and p not in (PV, PV + 1):
                            job_done(act, "t", 2 * (p - 2) + 1)
                        dst = v_tok[:, :, (p - PV) * N:(p - PV + 1) * N] if p in (PV, PV + 1) else stage[p % 2]
                        stage_panel(P_IN + p, dst)

            for j in range(UPP):
                high(U_OUT + j + RING)
                if j == 1:
                    gate_tanh(2 * PPG)
                    gate_tanh(2 * PPG + 1)
                    job_read(act, "pool", 1)
                    nc.scalar.activation(y_hi[:, 12:16, :], poolz[:], ACT.Copy, scale=0.5).then_inc(y_hi_done, 1)
                if j == 5:
                    act.wait_ge(lr_in, 16)
                    nc.scalar.copy(lr_hi[:], lr_raw[:]).then_inc(lr_hi_done, 1)
            with act.Fori(0, PO - 1) as n:
                for j in range(UPP):
                    high(U_OUT + UPP + j + RING, n, UPP)
            for c in range(UPP):
                split_high("hn", c, a_hi, 2 * c, hn_hi_done, V_MIX + 2 * c)
                if c >= 4:
                    high(U_G + c)
            for t in range(TT):
                act.wait_ge(ln_dve, 12)
                act.wait_ge(ln_pool, 4)
                for n in range(PO):
                    sum_of_squares(h_tok[:, t, n * N:(n + 1) * N], ssq[0][:, t, n:n + 1], ssq_done)

            def exp_step(s):
                act.wait_ge(diff_done, 2 * (s + 1))
                d = decayed[s % 3][:].rearrange("p d t -> p (d t)")
                nc.scalar.activation(d, d, ACT.Exp, scale=1.0 / 16.0).then_inc(decay_done, 1)

            for g in range(NPG * UPP):
                p, j = g // UPP, g % UPP
                if g >= 4:
                    high(U_G + g + RING)
                if g == 8:
                    job_done(act, "lr")
                    for t in range(TT):
                        mm = nc.scalar.activation(lrt[:, t, 0:2 * RANK], bank_of("lr")[:, t * 2 * RANK:(t + 1) * 2 * RANK],
                                                  ACT.Copy, scale=rstd[1][:, t:t + 1])
                    mm.then_inc(read_of("lr"), 1)
                if g == 10:
                    job_done(act, "lrt")
                    nc.scalar.copy(lrT[:], bank_of("lrt")[0:2 * RANK + 1, 0:TOK]).then_inc(read_of("lrt"), 1)
                if g in (9, 17, 25, 33):
                    q = (g - 9) // 8
                    for i in (2 * q, 2 * q + 1):
                        job_done(act, "gt", i)
                        src = bank_of("gt", i)[:].rearrange("p (k t) -> p k t", t=TOK)
                        dst, k = (gqT, 2 * i) if q < 2 else (gkT, 2 * (i - 4))
                        nc.scalar.activation(dst[:, k:k + 2, :], src, ACT.Copy,
                                             scale=1.0 / 16.0 if q < 2 else 1.0).then_inc(read_of("gt", i), 1)
                for name, i in gla_jobs(g):
                    if name == "gk":
                        act.wait_ge(gk_min, i + 1)
                        e = gate_tmp[i // 4][:, 2 * (i % 4):2 * (i % 4) + 2, :].rearrange("p k t -> p (k t)")
                        nc.scalar.activation(e, bank_of("gk", i)[:], ACT.Abs).then_inc(read_of("gk", i), 1)
                        act.wait_ge(read_of("gk", i), job("gk", i)[2] + 1)
                        nc.scalar.activation(e, e, ACT.Exp, scale=-1.0).then_inc(gk_exp, 1)
                        if i % 4 == 3:
                            act.wait_ge(gk_exp, i + 1)
                            e = gate_tmp[i // 4][:].rearrange("p k t -> p (k t)")
                            nc.scalar.activation(e, e, ACT.Ln, bias=1.0).then_inc(gk_ln, 1)
                for s in range(STEPS):
                    if g == STEP0 + STEP_GAP * s - 4:
                        exp_step(s)
                for hd in range(GH):
                    if g == AV0 + 3 * hd:
                        for t in range(TT):
                            job_done(act, "av", 2 * hd + t)
                            sum_of_squares(bank_of("av", 2 * hd + t)[:], o_ssq[:, hd, t:t + 1], o_sq)
                    if hd < 3 and g == AV0 + 3 * hd + 2:
                        for i in (2 * hd, 2 * hd + 1):
                            split_high("o", i, y_hi, 2 * i, o_hi_done, V_ON + 2 * (i % 2))
                if j == UPP - 1:
                    if p < 4:
                        act.wait_ge(rstd_done, 2)
                        stage_panel(P_G + p, og[p], rstd[1])
                    elif p < 8:
                        stage_panel(P_G + p, gv[:, :, (p - 4) * N:(p - 3) * N], rstd[1])
                    else:
                        act.wait_ge(cum_done, 2 * DB)
                        if p >= 10:
                            act.wait_ge(diff_done, 2 * STEPS)
                        stage_panel(P_G + p, og[p - 8], rstd[1], ACT.Silu)

            def squares(i, n):
                for t in range(TT):
                    sum_of_squares(h_tok[:, t, n * N:(n + 1) * N], ssq[i % 3][:, t, n:n + 1], ssq_done)

            def split_h(name, n, col):
                for i in (2 * n, 2 * n + 1):
                    split_high(name, i, a_hi, 2 * i, h1_hi_done if name == "h1" else h2_hi_done, col + 2 * i)

            for n in range(PO):
                for j in range(UPP):
                    high(U_GO + n * UPP + j + RING)
                    if n == 0 and j == 1:
                        for i in (6, 7):
                            split_high("o", i, y_hi, 2 * i, o_hi_done, V_ON + 2 * (i % 2))
                        split_high("pt", 0, p_hi, 0, p_hi_done)
                    if n >= 1 and j == 1:
                        split_h("h1", n - 1, V_FFN)
                        squares(1, n - 1)
            for m in range(2):
                for j in range(UPP):
                    high(U_F + m * UPP + j + RING)
                    if m == 0 and j == 1:
                        split_h("h1", PO - 1, V_FFN)
                        squares(1, PO - 1)
                    if m == 0 and j == UPP - 1:
                        act.wait_ge(rstd_done, 3)
                        stage_panel(P_F, act_tok, rstd[2], ACT.Silu)

            def split_act(f, i=0):
                for k in range(2):
                    n, bank, _ = job("a", 2 * f + k)
                    act.wait_ge(aux_done, 2 * i + (n + 1))
                    nc.scalar.copy(act_hi[:, 2 * k:2 * k + 2, :],
                                   aux[bank][:].rearrange("p (k t) -> p k t", t=TOK)).then_inc(act_hi_done, 1)

            split_act(0)
            with act.Fori(0, NF - 1) as f:
                for j in range(FU):
                    high(U_FL + j + RING, f, FU)
                    if j == UPP - 1:
                        stage_panel(P_FL, act_tok, rstd[2], ACT.Silu, f, FU)
                split_act(1, f)
            for n in range(PO):
                for k in range(ROWS_F):
                    high(U_FE + n * ROWS_F + k + RING)
                if n >= 1:
                    split_h("h2", n - 1, V_PLE)
                    squares(2, n - 1)
            for n in range(PO):
                high(U_PP + n + RING)
                if n == 1:
                    split_h("h2", PO - 1, V_PLE)
                    squares(2, PO - 1)
                stage_panel(P_PP + n, emb[:, :, n * N:(n + 1) * N])
            for n in range(PO):
                for j in range(UPP):
                    if U_PG + n * UPP + j + RING < U_END:
                        high(U_PG + n * UPP + j + RING)
                if n == 0:
                    act.wait_ge(rstd_done, 4)
                else:
                    act.wait_ge(h_added, TT * n)
                stage_panel(P_PG + n, gate_tok, rstd[3], ACT.Sigmoid)
                if n:
                    squares(3, n - 1)
            act.wait_ge(h_added, TT * PO)
            squares(3, PO - 1)

        @block.vector
        def _(dve):
            steps = [0]

            def link(ins):
                steps[0] += 1
                ins.then_inc(dve_step, 1)
                dve.wait_ge(dve_step, steps[0])

            def low(u, i=0, per=0):
                dve.wait_ge(hi_done, i * per + (u + 1))
                nc.vector.tensor_tensor(w_lo[u % RING][:], w_raw[u % RING][:], w_hi[u % RING][:],
                                        ALU.subtract).then_inc(lo_done, 1)

            def split_low(name, i, hi, lo, c, done, count, col=None):
                dve.wait_ge(done, count)
                b = bank_of(name, i)
                if col is None:
                    nc.vector.tensor_tensor(lo[:, c:c + 2, :], b[:].rearrange("p (k t) -> p k t", t=TOK),
                                            hi[:, c:c + 2, :], ALU.subtract).then_inc(read_of(name, i), 1)
                    return
                for k in range(2):
                    last = nc.vector.scalar_tensor_tensor(lo[:, c + k, :], b[:, k * TOK:(k + 1) * TOK],
                                                          vec[:, col + k:col + k + 1], hi[:, c + k, :],
                                                          ALU.mult, ALU.subtract)
                last.then_inc(read_of(name, i), 1)

            def inverse_root_of(count):
                dve.wait_ge(ssq_done, TT * PO * (count + 1))
                dve.wait_ge(rstd_done, count + 1)
                link(nc.vector.reduce_sum(ms[:], ssq[count % 3][:], AX_X))
                nc.vector.tensor_scalar(ms[:], ms[:], 1.0 / D, RMS_EPS, ALU.mult, ALU.add).then_inc(ms_done, 1)

            job_done(dve, "vec")
            nc.vector.tensor_copy(vec[:], bank_of("vec")[:, 0:NVEC]).then_inc(read_of("vec"), 1)
            for c in range(UPP):
                split_low("x", c, a_hi, a_lo, 2 * c, x_hi_done, c + 1)
                low(c)
                if c == 4:
                    dve.wait_ge(fg_hi_done, 1)
                    nc.vector.tensor_tensor(fg_lo[:], fg_raw[:], fg_hi[:], ALU.subtract).then_inc(fg_split, 1)
            nc.vector.memset(poolu[:, :, 0:PAD], 0.0).then_inc(zeros, 1)
            dve.wait_ge(consts, 9)
            for g in range(4):
                link(nc.vector.tensor_scalar(inv_count[:, g, :], iota_f[:], float(2 << g), None, ALU.min))
                link(nc.vector.reciprocal(inv_count[:, g, :], inv_count[:, g, :]))
            y_count = [0]
            gates = [0]

            def gate(i, dst):
                gates[0] += 1
                dve.wait_ge(tanh_done, gates[0])
                nc.vector.scalar_tensor_tensor(dst, tanh[i % 2][:], 1.0,
                                               bank_of("t", i)[:].rearrange("p (k t) -> p k t", t=TOK),
                                               ALU.add, ALU.mult).then_inc(read_of("t", i), 1)

            def y_low(src, c, n):
                y_count[0] += 1
                dve.wait_ge(y_hi_done, y_count[0])
                nc.vector.scalar_tensor_tensor(y_lo[:, c:c + n, :], src, 0.5, y_hi[:, c:c + n, :],
                                               ALU.mult, ALU.subtract).then_inc(y_done, 1)

            def attention(u):
                for h in range(NH):
                    if u == HEAD0 + HEAD_STEP * h:
                        if h == 0:
                            dve.wait_ge(consts, 7)
                            job_read(dve, "ci")
                        job_done(dve, "s", h)
                        b = bank_of("s", h)
                        first = nc.vector.scalar_tensor_tensor(logits[:, 0:P], b[:, 0:P], cum_i[:, 0, h:h + 1],
                                                               causal[:, 0:P], ALU.add, ALU.add)
                        nc.vector.scalar_tensor_tensor(logits[:, P:3 * P], b[:, P:3 * P], cum_i[:, 1, h:h + 1],
                                                       causal[:, P:3 * P], ALU.add, ALU.add).then_inc(read_of("s", h), 1)
                        job_read(dve, "s", h)
                        nc.vector.tensor_reduce(neg_max[:, 0:1], logits[:, 0:P], AX_X, ALU.max, negate=True)
                        nc.vector.tensor_reduce(neg_max[:, 1:2], logits[:, P:3 * P], AX_X, ALU.max,
                                                negate=True).then_inc(max_done, 1)
                    if u == HEAD0 + HEAD_STEP * h + 1:
                        dve.wait_ge(exp_done, 2 * (h + 1))
                        nc.vector.reciprocal(inv_sum[:], row_sum[:]).then_inc(inv_done, 1)
                        dve.wait_ge(inv_done, h + 1)
                        for t, c in ((0, slice(0, P)), (1, slice(P, 3 * P))):
                            nc.vector.tensor_scalar(probs[:, c], probs[:, c], inv_sum[:, t:t + 1], None,
                                                    ALU.mult).then_inc(probs_done, 1)
                    if u == HEAD0 + HEAD_STEP * h + 3:
                        job_done(dve, "ot", h)
                        nc.vector.tensor_tensor(y_head[:], bank_of("ot", h)[:, 0:TOK], gaT[:, h, :],
                                                ALU.mult).then_inc(read_of("ot", h), 1)
                        y_low(y_head[:], h, 1)

            for p in range(NP1):
                for j in range(UPP):
                    u = U_IN + p * UPP + j
                    if u >= 4:
                        low(u + RING)
                    if (p, j) == (1, 2):
                        dve.wait_ge(vec_in, 7 * 16)
                        job_done(dve, "fgt")
                        nc.vector.tensor_scalar(fgz[:], bank_of("fgt")[0:NH, 0:TOK], bf_col[:], None, ALU.add).then_inc(read_of("fgt"), 1)
                    if (p, j) == (1, 4):
                        dve.wait_ge(fg_ln, 1)
                        link(nc.vector.tensor_scalar(fgz[:], fgz[:], 0.0, None, ALU.min))
                        link(nc.vector.tensor_tensor(fge[:], fgz[:], fge[:], ALU.subtract))
                        link(nc.vector.memset(ncum[:], 1.0))
                        nc.vector.tensor_tensor_scan(fgz[:], ncum[:], fge[:], 0.0, ALU.mult, ALU.add).then_inc(fg_cum, 1)
                        dve.wait_ge(fg_cum, 1)
                        nc.vector.tensor_scalar(ncum[:], fgz[:], -1.0, None, ALU.mult).then_inc(fg_neg, 1)
                    if j == 1 and p >= 1:
                        q = p - 1
                        for i in (2 * q, 2 * q + 1):
                            if ("t", i) not in JOB:
                                continue
                            src = bank_of("t", i)[:].rearrange("p (k t) -> p k t", t=TOK)
                            k = 2 * (i % 2)
                            if q in (PK, PK + 1):
                                job_done(dve, "t", i)
                                nc.vector.tensor_copy(kT[:, 2 * (i - 4):2 * (i - 4) + 2, :], src).then_inc(read_of("t", i), 1)
                            if q in (PGA, PGA + 1):
                                gate(i, gaT[:, 2 * (i - 8):2 * (i - 8) + 2, :])
                            if q == PCH:
                                job_done(dve, "t", i)
                                job_read(dve, "t", 2 * PCC + 1)
                                nc.vector.tensor_tensor(convu[:, k:k + 2, 2:], src, convu[:, k:k + 2, 2:],
                                                        ALU.mult).then_inc(read_of("t", i), 1)
                            if q == PCG:
                                gate(i, convg[:, k:k + 2, :])
                            if q == PCB:
                                job_done(dve, "t", i)
                                nc.vector.tensor_tensor(convg[:, k:k + 2, :], src, convg[:, k:k + 2, :],
                                                        ALU.mult).then_inc(read_of("t", i), 1)
                    attention(u)
                    if (p, j) == (9, 2):
                        job_read(dve, "t", 2 * PPU)
                        job_read(dve, "t", 2 * PPU + 1)
                        E = PAD + TOK
                        link(nc.vector.tensor_tensor(sum_a[:, :, 1:E], poolu[:, :, 1:E], poolu[:, :, 0:E - 1], ALU.add))
                        link(nc.vector.tensor_tensor(sum_b[:, 1:4, 3:E], sum_a[:, 1:4, 3:E], sum_a[:, 1:4, 1:E - 2], ALU.add))
                    if (p, j) == (9, 3):
                        link(nc.vector.tensor_tensor(sum_a[:, 2:4, 7:E], sum_b[:, 2:4, 7:E], sum_b[:, 2:4, 3:E - 4], ALU.add))
                        link(nc.vector.tensor_tensor(sum_b[:, 3:4, 15:E], sum_a[:, 3:4, 15:E], sum_a[:, 3:4, 7:E - 8], ALU.add))
                        for g in range(4):
                            nc.vector.tensor_tensor(poolz[:, g, :], (sum_a, sum_b)[g % 2][:, g, PAD:E],
                                                    inv_count[:, g, :], ALU.mult).then_inc(dve_step, 1)
                            steps[0] += 1
                        dve.wait_ge(dve_step, steps[0])
                        nc.vector.tensor_tensor(poolz[:], poolz[:], poolu[:, :, PAD:E], ALU.subtract).then_inc(z_done, 1)
                        dve.wait_ge(z_done, 1)
                        nc.vector.memset(convu[:, :, 0:2], 0.0).then_inc(zeros, 1)
                    if (p, j) == (13, 2):
                        job_read(dve, "t", 2 * PCB + 1)
                        for b in range(4):
                            link(nc.vector.tensor_scalar(convy[:, b, :], convu[:, b, 0:TOK],
                                                         vec[:, V_CONV + b:V_CONV + b + 1], None, ALU.mult))
                            for tap in (1, 2):
                                c = V_CONV + 4 * tap + b
                                link(nc.vector.scalar_tensor_tensor(convy[:, b, :], convu[:, b, tap:tap + TOK],
                                                                    vec[:, c:c + 1], convy[:, b, :],
                                                                    ALU.mult, ALU.add))
                        nc.vector.tensor_tensor(convy[:], convy[:], convg[:], ALU.mult).then_inc(mixed, 1)
                    if (p, j) == (13, 4):
                        y_low(convy[:], 8, 4)

            for j in range(UPP):
                low(U_OUT + j + RING)
                if j == 1:
                    for i in range(2):
                        gate(2 * PPG + i, poolg[:, 2 * i:2 * i + 2, :])
                    job_read(dve, "t", 2 * PPG + 1)
                    for g in range(4):
                        last = nc.vector.scalar_tensor_tensor(
                            poolz[:, g, :], bank_of("pool", g // 2)[:, (g % 2) * TOK:(g % 2 + 1) * TOK],
                            vec[:, V_PS + g:V_PS + g + 1], poolg[:, g, :], ALU.mult, ALU.mult)
                        if g == 1:
                            last.then_inc(read_of("pool", 0), 1)
                    last.then_inc(read_of("pool", 1), 1)
                    y_low(poolz[:], 12, 4)
                if j == 5:
                    dve.wait_ge(lr_hi_done, 1)
                    nc.vector.tensor_tensor(lr_lo[:], lr_raw[:], lr_hi[:], ALU.subtract).then_inc(lr_split, 1)

            def residual(n, i=0, base_turn=0):
                p = P_OUT + n
                panel_done(dve, p)
                for t, b in enumerate(panel_banks(p)):
                    s = slice(n * N, (n + 1) * N)
                    nc.vector.scalar_tensor_tensor(h_tok[:, t, s], h_tok[:, t, s], ALPHA, b[:], ALU.mult,
                                                   ALU.add).then_inc(acc_read[p % 2], 1)
                for t in range(TT):
                    panel_read(dve, p, t + 1)
                    nc.vector.bn_stats(bn[:, t, n, :], h_tok[:, t, n * N:(n + 1) * N]).then_inc(bn_done, 1)

            dve.wait_ge(x_back, 16)
            residual(0)
            for n in range(1, PO):
                for j in range(UPP):
                    low(U_OUT + n * UPP + j + RING)
                residual(n)
            for t in range(TT):
                dve.wait_ge(bn_done, TT * PO)
                nc.vector.bn_aggr(mv[:, t, :], bn[:, t, :, :].rearrange("p n s -> p (n s)")).then_inc(var_done, 1)
            dve.wait_ge(var_done, 2)
            nc.vector.tensor_scalar(ms[:], mv[:, :, 1], LN_EPS, None, ALU.add).then_inc(ms_done, 1)
            dve.wait_ge(rstd_done, 1)
            for t in range(TT):
                nc.vector.tensor_scalar(h_tok[:, t, :], h_tok[:, t, :], mv[:, t, 0:1], rstd[0][:, t:t + 1],
                                        ALU.subtract, ALU.mult).then_inc(centred, 1)
            dve.wait_ge(gb_in, 32)
            k = 0
            for n in range(PO):
                for t in range(TT if n < 2 else 1):
                    s = slice(n * N, (n + 1) * N)
                    dve.wait_ge(centred, t + 1)
                    nc.vector.tensor_tensor(h_tok[:, t, s], h_tok[:, t, s], ln_gb[:, 0, s], ALU.mult).then_inc(ln_dve, 1)
                    k += 1
                    dve.wait_ge(ln_dve, k)
                    nc.vector.tensor_tensor(h_tok[:, t, s], h_tok[:, t, s], ln_gb[:, 1, s], ALU.add).then_inc(ln_dve, 1)
                    k += 1
            for c in range(UPP):
                split_low("hn", c, a_hi, a_lo, 2 * c, hn_hi_done, 2 * (c + 1), V_MIX + 2 * c)
                if c >= 4:
                    low(U_G + c)
            nc.vector.memset(lrt[:, :, 2 * RANK:], 1.0).then_inc(zeros, 1)
            link(nc.vector.memset(restart[:], 1.0))
            for c in (0, P, TOK):
                link(nc.vector.memset(restart[:, c:c + 1], 0.0))
            inverse_root_of(0)

            def flat(t):
                return t[:].rearrange("p d t -> p (d t)")

            def diff(s):
                way, h = s // NL, LEVELS[s % NL]
                if s >= 3:
                    job_done(dve, "step", s - 3)
                d, c = halves(flat(decayed[s % 3]), h), halves(flat(cum[way]), h)
                if way == 0:
                    mid = c[:, :, 0, h - 1:h].broadcast_to([P, DB * TOK // (2 * h), h])
                else:
                    mid = c[:, :, 1, 0:1].broadcast_to([P, DB * TOK // (2 * h), h])
                far, near = (1, 0) if way == 0 else (0, 1)
                if h == P:
                    nc.vector.tensor_copy(d[:, :, far, :], c[:, :, far, :]).then_inc(diff_done, 1)
                else:
                    nc.vector.tensor_tensor(d[:, :, far, :], c[:, :, far, :], mid, ALU.subtract).then_inc(diff_done, 1)
                nc.vector.tensor_tensor(d[:, :, near, :], mid, c[:, :, near, :], ALU.subtract).then_inc(diff_done, 1)

            def times(s):
                way, h = s // NL, LEVELS[s % NL]
                dve.wait_ge(decay_done, s + 1)
                if s == 0:
                    for i in range(8):
                        job_read(dve, "gt", i)
                d = halves(flat(decayed[s % 3]), h)
                src = halves(flat((gqT, gkT)[way]), h)
                nc.vector.tensor_tensor(d[:, :, 1, :], d[:, :, 1, :], src[:, :, 1, :], ALU.mult).then_inc(mul_dve, 1)

            def keep(s):
                way, h = s // NL, LEVELS[s % NL]
                job_done(dve, "step", s)
                b = bank_of("step", s)
                if h == P:
                    nc.vector.tensor_copy(at_off[:, :, way, :],
                                          b[:].rearrange("p (h i) -> p h i", i=P)).then_inc(read_of("step", s), 1)
                    return
                nb = P // (2 * h)
                dst = at_diag[:].rearrange("p h t (b s r) -> p (h t) b s r", s=2, r=h)[:, :, :, 1 - way, :]
                m = masks[:, s % NL, way, :].bitcast(I32).rearrange("p (a b r) -> p a b r", a=1, r=h).broadcast_to([P, GH * TT, nb, h])
                nc.vector.copy_predicated(dst, m, b[:].rearrange("p (c b r) -> p c b r", c=GH * TT, r=h)).then_inc(read_of("step", s), 1)

            def head_out(hd):
                dve.wait_ge(o_rstd_done, hd + 1)
                panel_read(dve, P_G + 8 + hd)
                for t in range(TT):
                    nc.vector.scalar_tensor_tensor(og[hd][:, t, :], bank_of("av", 2 * hd + t)[:],
                                                   o_rstd[:, hd, t:t + 1], og[hd][:, t, :], ALU.mult,
                                                   ALU.mult).then_inc(read_of("av", 2 * hd + t), 1)

            for g in range(NPG * UPP):
                if g >= 4:
                    low(U_G + g + RING)
                for name, i in gla_jobs(g):
                    if name == "gk":
                        job_done(dve, "gk", i)
                        if i == 4:
                            job_read(dve, "gt", 7)
                        way, k = i // 4, 2 * (i % 4)
                        nc.vector.tensor_scalar(cum[way][:, k:k + 2, :].rearrange("p k t -> p (k t)"), bank_of("gk", i)[:],
                                                0.0, None, ALU.min).then_inc(gk_min, 1)
                    if name == "dg":
                        job_done(dve, "dg", i)
                        idb = ident[:].rearrange("p (a t) -> p a t", a=1).broadcast_to([P, 4, P])
                        nc.vector.scalar_tensor_tensor(
                            at_diag[:, 2 * i:2 * i + 2, :, :].rearrange("p h t i -> p (h t) i"),
                            bank_of("dg", i)[:].rearrange("p (c i) -> p c i", i=P), 2.0, idb,
                            ALU.mult, ALU.mult).then_inc(read_of("dg", i), 1)
                    if name == "step":
                        keep(i)
                for way, when in ((0, 20), (1, 46)):
                    if g == when:
                        dve.wait_ge(gk_ln, way + 1)
                        link(nc.vector.tensor_tensor(flat(cum[way]), flat(cum[way]), flat(gate_tmp[way]), ALU.subtract))
                    if when <= g < when + 4:
                        for b in (2 * (g - when), 2 * (g - when) + 1):
                            c = cum[way][:, b, :]
                            r = restart[:, 0:TOK]
                            if way:
                                c, r = c[:, ::-1], restart[:, 1:TOK + 1][:, ::-1]
                            nc.vector.tensor_tensor_scan(c, r, c, 0.0, ALU.mult, ALU.add).then_inc(cum_done, 1)
                for s in range(STEPS):
                    if g == STEP0 + STEP_GAP * s - 4:
                        if s % NL == 0:
                            dve.wait_ge(cum_done, 8 * (s // NL + 1))
                        diff(s)
                    if g == STEP0 + STEP_GAP * s - 2:
                        times(s)
                for hd in range(GH):
                    if g == AV0 + 3 * hd:
                        dve.wait_ge(o_sq, TT * (hd + 1))
                        nc.vector.tensor_scalar(o_ms[:, hd, :], o_ssq[:, hd, :], 1.0 / GDV, RMS_EPS, ALU.mult,
                                                ALU.add).then_inc(o_ms_done, 1)
                if g in (AV0 + 1, AV0 + 4, AV0 + 7):
                    hd = (g - AV0 - 1) // 3
                    head_out(hd)
                if g in (AV0 + 2, AV0 + 5, AV0 + 8):
                    hd = (g - AV0 - 2) // 3
                    for i in (2 * hd, 2 * hd + 1):
                        split_low("o", i, y_hi, y_lo, 2 * i, o_hi_done, 2 * (i + 1), V_ON + 2 * (i % 2))

            head_out(GH - 1)

            def add_panel(n, p, i=0, uper=0):
                panel_done(dve, p, i, uper)
                for t, b in enumerate(panel_banks(p)):
                    s = slice(n * N, (n + 1) * N)
                    nc.vector.tensor_tensor(h_tok[:, t, s], h_tok[:, t, s], b[:], ALU.add).then_inc(acc_read[p % 2], 1)

            def split_h(name, n, col):
                for i in (2 * n, 2 * n + 1):
                    split_low(name, i, a_hi, a_lo, 2 * i, h1_hi_done if name == "h1" else h2_hi_done, 2 * (i + 1),
                              col + 2 * i)

            for n in range(PO):
                for j in range(UPP):
                    low(U_GO + n * UPP + j + RING)
                    if n == 0 and j == 1:
                        for i in (6, 7):
                            split_low("o", i, y_hi, y_lo, 2 * i, o_hi_done, 2 * (i + 1), V_ON + 2 * (i % 2))
                        split_low("pt", 0, p_hi, p_lo, 0, p_hi_done, 1)
                    if n >= 1 and j == 1:
                        split_h("h1", n - 1, V_FFN)
                add_panel(n, P_GO + n)

            def multiply(p, i=0, uper=0):
                panel_done(dve, p, i, uper)
                for t, b in enumerate(panel_banks(p)):
                    nc.vector.scalar_tensor_tensor(act_tok[:, t, :], b[:], rstd[2][:, t:t + 1], act_tok[:, t, :],
                                                   ALU.mult, ALU.mult).then_inc(acc_read[p % 2], 1)

            def split_act(f, i=0):
                for k in range(2):
                    n, bank, _ = job("a", 2 * f + k)
                    dve.wait_ge(act_hi_done, 2 * i + (2 * f + k + 1))
                    nc.vector.tensor_tensor(act_lo[:, 2 * k:2 * k + 2, :],
                                            aux[bank][:].rearrange("p (k t) -> p k t", t=TOK),
                                            act_hi[:, 2 * k:2 * k + 2, :], ALU.subtract).then_inc(aux_read[bank], 1)

            for m in range(2):
                for j in range(UPP):
                    low(U_F + m * UPP + j + RING)
                    if m == 0 and j == 1:
                        split_h("h1", PO - 1, V_FFN)
                        inverse_root_of(1)
            dve.wait_ge(rstd_done, 3)
            panel_read(dve, P_F)
            multiply(P_F + 1)
            split_act(0)
            with dve.Fori(0, NF - 1) as f:
                for j in range(FU):
                    low(U_FL + j + RING, f, FU)
                    if j == 2 * UPP - 1:
                        panel_read(dve, P_FL, 2, f, FP)
                        multiply(P_FL + 1, f, FU)
                    if j >= 2 * UPP and (j - 2 * UPP) % ROWS_F == ROWS_F - 1:
                        n = (j - 2 * UPP) // ROWS_F
                        add_panel(n, P_FL + 2 + n, f, FU)
                split_act(1, f)
            for n in range(PO):
                for k in range(ROWS_F):
                    low(U_FE + n * ROWS_F + k + RING)
                add_panel(n, P_FE + n)
                if n >= 1:
                    split_h("h2", n - 1, V_PLE)
            for n in range(PO):
                low(U_PP + n + RING)
                if n == 1:
                    split_h("h2", PO - 1, V_PLE)
                    inverse_root_of(2)

            k = 0
            for n in range(PO):
                for j in range(UPP):
                    if U_PG + n * UPP + j + RING < U_END:
                        low(U_PG + n * UPP + j + RING)
                panel_read(dve, P_PG + n)
                s = slice(n * N, (n + 1) * N)
                for t in range(TT):
                    k += 1
                    nc.vector.tensor_tensor(gate_tok[:, t, :], gate_tok[:, t, :], emb[:, t, s], ALU.mult).then_inc(gated, 1)
                    dve.wait_ge(gated, k)
                    nc.vector.tensor_tensor(h_tok[:, t, s], h_tok[:, t, s], gate_tok[:, t, :], ALU.add).then_inc(h_added, 1)
            inverse_root_of(3)
            dve.wait_ge(rstd_done, 5)
            dve.wait_ge(fin_in, 16)
            for t in range(TT):
                for c in range(2):
                    s = slice(c * 1024, (c + 1) * 1024)
                    nc.vector.scalar_tensor_tensor(h_tok[:, t, s], h_tok[:, t, s], rstd[0][:, t:t + 1], fin_w[:, s],
                                                   ALU.mult, ALU.mult).then_inc(scaled, 1)


_INS = ["x", "w_in", "b_f", "conv_w", "pool_w", "pool_scale", "w_out", "ln_g", "ln_b", "p_2", "mixer_norm_2",
        "gla_w_in_2", "gla_w_gate_up_2", "gla_b_gate_2", "gla_out_norm_2", "gla_w_out_2", "ffn_norm_2",
        "ffn_w_in_2", "ffn_w_out_2", "ple_norm_2", "ple_w_gate_2", "ple_w_proj_2", "final_norm_2"]


def kernel(**inputs):
    import numpy as np
    import concourse.bacc as bacc
    from concourse.bass_utils import run_bass_kernel_spmd

    nc = bacc.Bacc("TRN2", target_bir_lowering=False, num_devices=1)
    arrays, args = {}, []
    for name in _INS:
        a = np.ascontiguousarray(inputs[name])
        arrays[f"in_{name}"] = a
        args.append(nc.dram_tensor(f"in_{name}", a.shape, mybir.dt.from_np(a.dtype), kind="ExternalInput").ap())
    out = nc.dram_tensor("out", (1, TOK, D), F32, kind="ExternalOutput").ap()
    block_kernel(nc, *args, out)
    r = run_bass_kernel_spmd(nc, [arrays], core_ids=[0])
    return r.results[0]["out"]
```

```python
from contextlib import ExitStack

import concourse.bass as bass
from concourse import mybir

F32 = mybir.dt.float32
F32R = mybir.dt.float32r
I32 = mybir.dt.int32
ALU = mybir.AluOpType
ACT = mybir.ActivationFunctionType
AX_X = mybir.AxisListType.X

P = 128
N = 512
TOK = 256
TT = TOK // P
D = 2048
KD = D // P
UNIT = 2
UPP = KD // UNIT
RING = 4
ATT = 1024
NH = ATT // P
D_FF = 5632
NF = D_FF // N
ROWS_F = N // P // UNIT
PO = D // N
LN_EPS, RMS_EPS = 1e-5, 1e-6
ALPHA = 2.0 ** 0.25
GH, GDK, GDV = 4, 256, 512
RANK = 16
DB = GH * GDK // P

Q0, K0, V0, GA0, FG0 = 0, ATT, 2 * ATT, 3 * ATT, 4 * ATT
CB0 = FG0 + NH
CC0, CH0, CG0, PU0, PG0 = (CB0 + i * N for i in range(1, 6))
COLS1 = [Q0, Q0 + N, K0, K0 + N, GA0, GA0 + N, V0, V0 + N, PU0, CC0, CH0, CG0, CB0, PG0]
NP1 = len(COLS1)
(PQ, PK, PGA, PV, PPU, PCC, PCH, PCG, PCB, PPG) = (0, 2, 4, 6, 8, 9, 10, 11, 12, 13)
NPG = 12
LR0 = NPG * N

U_IN, P_IN = 0, 0
U_OUT, P_OUT = U_IN + NP1 * UPP, P_IN + NP1
U_PP, P_PP = U_OUT + PO * UPP, P_OUT + PO
U_G, P_G = U_PP + PO, P_PP + PO
U_GO, P_GO = U_G + NPG * UPP, P_G + NPG
U_F, P_F = U_GO + PO * UPP, P_GO + PO
U_FL, P_FL = U_F + 2 * UPP, P_F + 2
FU, FP = 2 * UPP + PO * ROWS_F, 2 + PO
U_FE, P_FE = U_FL + (NF - 1) * FU, P_FL + (NF - 1) * FP
U_PG, P_PG = U_FE + PO * ROWS_F, P_FE + PO
U_END = U_PG + PO * UPP

HEAD0, HEAD_STEP = U_IN + PV * UPP + 2 * UPP + 2, 4
TURN_LAG, VALUE_LAG = 3, 5
LEVELS = [1, 2, 4, 8, 16, 32, 64, 128]
NL = len(LEVELS)
STEPS = 2 * NL
STEP0, STEP_GAP = 37, 3
GK_BWD = (43, 44, 46, 47)
AV0 = 84
P_CHUNK = KD - UNIT

V_CONV, V_PS, V_MIX, V_ON, V_FFN, V_PLE, NVEC = 0, 12, 16, 32, 36, 52, 68


def small_products():
    order = [("x", i) for i in range(UPP)] + [("vec", 0)]
    for p in range(NP1):
        for j in range(UPP):
            u = p * UPP + j
            if (p, j) == (1, 0):
                order.append(("fg", 0))
            if j == 1 and p >= 1 and p - 1 not in (PV, PV + 1):
                order += [("t", 2 * (p - 1)), ("t", 2 * (p - 1) + 1)]
            if (p, j) == (1, 6):
                order.append(("ci", 0))
            if (p, j) == (13, 3):
                order += [("pool", 0), ("pool", 1)]
            order += head_jobs(u)
    order += [("t", 2 * PPG), ("t", 2 * PPG + 1), ("pt", 0)]
    order += [("hn", i) for i in range(UPP)]
    for g in range(NPG * UPP):
        order += [(name, i) for name, i in gla_jobs(g)]
    order += [("o", 6), ("o", 7)]
    order += [("h1", i) for i in range(2 * PO)]
    named = {}
    turns = [0, 0, 0, 0]
    for n, key in enumerate(order):
        named[key] = (n, n % 4, turns[n % 4])
        turns[n % 4] += 1
    n = len(order)
    for f in range(NF):
        for b in range(2):
            named[("a", 2 * f + b)] = (n, b, turns[b])
            turns[b] += 1
            n += 1
    for i in range(2 * PO):
        b = (2 + i) % 4
        named[("h2", i)] = (n, b, turns[b])
        turns[b] += 1
        n += 1
    return named


def panel_end(p):
    for u0, p0, units in ((U_PG, P_PG, UPP), (U_FE, P_FE, ROWS_F), (U_FL + 2 * UPP, P_FL + 2, ROWS_F),
                          (U_G, P_G, UPP), (U_PP, P_PP, 1)):
        if p >= p0:
            return u0 + (p - p0 + 1) * units
    return (p + 1) * UPP


def head_jobs(u):
    found = []
    for h in range(NH):
        for name, lag in (("s", 0), ("pt_", TURN_LAG), ("ot", VALUE_LAG)):
            if u == HEAD0 + HEAD_STEP * h + lag:
                found.append((name, h))
    return found


def gla_jobs(g):
    found = []
    if g == 8:
        found.append(("lr", 0))
    if g in (9, 17, 25, 33):
        p = (g - 9) // 8
        found += [("gt", 2 * p), ("gt", 2 * p + 1)]
    if g == 10:
        found.append(("lr_tok", 0))
    if g == 12:
        found.append(("lrt", 0))
    if 16 <= g < 20:
        found.append(("gk", g - 16))
    if g == 34:
        found += [("dg", 0), ("dg", 1)]
    if g >= STEP0 and (g - STEP0) % STEP_GAP == 0 and (g - STEP0) // STEP_GAP < STEPS:
        found.append(("step", (g - STEP0) // STEP_GAP))
    if g in GK_BWD:
        found.append(("gk", 4 + GK_BWD.index(g)))
    if g >= AV0 and (g - AV0) % 3 == 0 and (g - AV0) // 3 < GH:
        h = (g - AV0) // 3
        found += [("av", 2 * h), ("av", 2 * h + 1)]
    if g in (AV0 + 3, AV0 + 6, AV0 + 9):
        h = (g - AV0 - 3) // 3
        found += [("o", 2 * h), ("o", 2 * h + 1)]
    return found


def halves(ap, h):
    return ap.rearrange("p (q s r) -> p q s r", s=2, r=h)


def block_kernel(nc, x, w_in, b_f, conv_w, pool_w, pool_scale, w_out, ln_g, ln_b, p_2,
                 mixer_norm, gla_w_in, gla_w_gate_up, gla_b_gate, gla_out_norm, gla_w_out,
                 ffn_norm, ffn_w_in, ffn_w_out, ple_norm, ple_w_gate, ple_w_proj, final_norm, out):
    JOB = small_products()
    KB = 1024
    base = 16512

    def at(name, shape, dt, offset):
        return nc.alloc_sbuf_tensor_at(name, shape, dt, offset=base + offset)

    w_raw = [at(f"w_raw{s}", [P, UNIT, N], F32, s * 4 * KB) for s in range(RING)]
    w_hi = [at(f"w_hi{s}", [P, UNIT, N], F32R, (16 + s * 4) * KB) for s in range(RING)]
    w_lo = [at(f"w_lo{s}", [P, UNIT, N], F32R, (32 + s * 4) * KB) for s in range(RING)]
    a_hi = at("a_hi", [P, KD, TOK], F32R, 48 * KB)
    a_lo = at("a_lo", [P, KD, TOK], F32R, 64 * KB)
    y_hi = at("y_hi", [P, KD, TOK], F32R, 80 * KB)
    y_lo = at("y_lo", [P, KD, TOK], F32R, 96 * KB)
    x_tok = at("x_tok", [P, TT, D], F32, 80 * KB)
    decayed = [at(f"decayed{s}", [P, DB, TOK], F32, (80 + 8 * s) * KB) for s in range(3)]
    gate_up = at("gate_up", [2 * RANK + 1, 2, GH * GDK], F32, 104 * KB)
    h_tok = at("h_tok", [P, TT, D], F32, 112 * KB)
    qT = at("qT", [P, NH, TOK], F32, 112 * KB)
    kT = at("kT", [P, NH, TOK], F32, 120 * KB)
    W = 128 * KB
    stage = [at(f"stage{s}", [P, TT, N], F32, W + s * 4 * KB) for s in range(2)]
    v_tok = at("v_tok", [P, TT, ATT], F32, W + 8 * KB)
    gaT = at("gaT", [P, NH, TOK], F32, W + 16 * KB)
    PAD = 16
    poolu = at("poolu", [P, 4, PAD + TOK], F32, W + 24 * KB)
    convu = at("convu", [P, 4, 2 + TOK], F32, W + 24 * KB)
    sum_a = at("sum_a", [P, 4, PAD + TOK], F32, W + 28 * KB + 512)
    convg = at("convg", [P, 4, TOK], F32, W + 28 * KB + 512)
    sum_b = at("sum_b", [P, 4, PAD + TOK], F32, W + 33 * KB)
    convy = at("convy", [P, 4, TOK], F32, W + 33 * KB)
    poolz = at("poolz", [P, 4, TOK], F32, W + 37 * KB + 512)
    poolg = at("poolg", [P, 4, TOK], F32, W + 41 * KB + 512)
    tanh = [at(f"tanh{s}", [P, 2, TOK], F32, W + (45 + 2 * s) * KB + 512) for s in range(2)]
    logits = at("logits", [P, 3 * P], F32, W + 49 * KB + 512)
    probs = at("probs", [P, 3 * P], F32, W + 51 * KB)
    probsT = at("probsT", [P, 3 * P], F32, W + 52 * KB + 512)
    y_head = at("y_head", [P, TOK], F32, W + 54 * KB)
    sel = at("sel", [NH, NH, P], F32, W + 55 * KB)
    inv_count = at("inv_count", [P, 4, TOK], F32, W + 59 * KB)
    causal = at("causal", [P, 3 * P], F32, W + 63 * KB)
    pool_sb = at("pool_sb", [P, 4, P], F32, W + 64 * KB + 512)
    ln_gb = at("ln_gb", [P, 2, D], F32, W)
    og = [at(f"og{s}", [P, TT, N], F32, W + 4 * s * KB) for s in range(4)]
    gate_tmp = [decayed[0], at("gate_tmp", [P, DB, TOK], F32, W)]
    gv = at("gv", [P, TT, GH * GDV], F32, W + 16 * KB)
    gqT = at("gqT", [P, DB, TOK], F32, W + 32 * KB)
    gkT = at("gkT", [P, DB, TOK], F32, W + 40 * KB)
    cum = [at("cum_fwd", [P, DB, TOK], F32, W + 48 * KB), at("cum_bwd", [P, DB, TOK], F32, W + 8 * KB)]
    at_diag = at("at_diag", [P, GH, TT, P], F32, W + 56 * KB)
    at_off = at("at_off", [P, GH, 2, P], F32, W + 60 * KB)
    lr_raw = at("lr_raw", [P, KD, 2 * RANK], F32, W + 56 * KB)
    lr_hi = at("lr_hi", [P, KD, 2 * RANK], F32R, W + 58 * KB)
    lr_lo = at("lr_lo", [P, KD, 2 * RANK], F32R, W + 60 * KB)
    lrt = at("lrt", [P, TT, 2 * RANK + 1], F32, W + 64 * KB)
    lrT = at("lrT", [2 * RANK + 1, TOK], F32, W + 64 * KB + 288)
    restart = at("restart", [P, TOK + 1], F32, W + 65 * KB + 288)
    act_tok = at("act_tok", [P, TT, N], F32, W)
    act_hi = at("act_hi", [P, N // P, TOK], F32R, W + 4 * KB)
    act_lo = at("act_lo", [P, N // P, TOK], F32R, W + 8 * KB)
    emb = at("emb", [P, TT, D], F32, W + 16 * KB)
    fin_w = at("fin_w", [P, D], F32, W + 32 * KB)
    gate_tok = at("gate_tok", [P, TT, N], F32, W + 40 * KB)
    p_tok = at("p_tok", [P, TT, 2 * P], F32, W + 48 * KB)
    C = W + 66 * KB + 512
    off = [C]

    def small(name, shape, dt=F32):
        size = 4
        for s in shape[1:]:
            size *= s
        t = at(name, shape, dt, off[0])
        off[0] += (size + 31) // 32 * 32
        return t

    ident = small("ident", [P, P])
    masks = small("masks", [P, NL - 1, 2, 64])
    vec_raw = small("vec_raw", [NVEC, P])
    vec = small("vec", [P, NVEC])
    square = small("square", [P, N])
    fg_raw = small("fg_raw", [P, KD, NH])
    fg_hi = small("fg_hi", [P, KD, NH], F32R)
    fg_lo = small("fg_lo", [P, KD, NH], F32R)
    ncum = small("ncum", [NH, TOK])
    fgz = at("fgz", [NH, TOK], F32, W + 49 * KB + 512)
    fge = at("fge", [NH, TOK], F32, W + 51 * KB)
    cum_i = small("cum_i", [P, TT, NH])
    bf_col = small("bf_col", [NH, 1])
    neg_max = small("neg_max", [P, 2])
    row_sum = small("row_sum", [P, 2])
    inv_sum = small("inv_sum", [P, 2])
    bn = small("bn", [P, TT, PO, 6])
    mv = small("mv", [P, TT, 2])
    ms = small("ms", [P, TT])
    minus_half = small("minus_half", [P, TT])
    rstd = [small(f"rstd{i}", [P, TT]) for i in range(4)]
    ssq = [small(f"ssq{i}", [P, TT, PO]) for i in range(3)]
    o_ssq = small("o_ssq", [P, GH, TT])
    o_ms = small("o_ms", [P, GH, TT])
    o_rstd = small("o_rstd", [P, GH, TT])
    iota_i = at("iota_i", [P, TOK], I32, W + 45 * KB + 512)
    iota_f = at("iota_f", [P, TOK], F32, W + 46 * KB + 512)
    assert base + off[0] <= 229344, off[0]

    emb_dram = nc.dram_tensor("emb_dram", (P, TT, D), F32, kind="Internal").ap()

    with ExitStack() as ctx:
        def sem(name):
            return ctx.enter_context(nc.semaphore(name))

        acc = [ctx.enter_context(nc.psum_tensor(f"acc{i}", [P, N], F32)) for i in range(4)]
        aux = [ctx.enter_context(nc.psum_tensor(f"aux{i}", [P, N], F32)) for i in range(4)]

        landed = [sem(f"landed{s}") for s in range(RING)]
        hi_done, lo_done = sem("hi_done"), sem("lo_done")
        unit_used = sem("unit_used")
        acc_read = [sem(f"acc_read{b}") for b in range(2)]
        aux_done = sem("aux_done")
        aux_read = [sem(f"aux_read{b}") for b in range(4)]
        x_in, x_back = [sem(f"x_in{c}") for c in range(PO)], sem("x_back")
        vec_in, fg_in, pool_in = sem("vec_in"), sem("fg_in"), sem("pool_in")
        gb_in, lr_in, up_in, p_in, fin_in = (sem(n) for n in ("gb_in", "lr_in", "up_in", "p_in", "fin_in"))
        emb_out, emb_in = sem("emb_out"), sem("emb_in")
        up_clear = sem("up_clear")
        consts = sem("consts")
        zeros = sem("zeros")
        x_hi_done, hn_hi_done, o_hi_done, h1_hi_done = (sem(n) for n in ("x_hi_done", "hn_hi_done", "o_hi_done", "h1_hi_done"))
        act_hi_done, h2_hi_done, p_hi_done, fg_hi_done, lr_hi_done = (
            sem(n) for n in ("act_hi_done", "h2_hi_done", "p_hi_done", "fg_hi_done", "lr_hi_done"))
        fg_split, lr_split = sem("fg_split"), sem("lr_split")
        tanh_done = sem("tanh_done")
        fg_abs, fg_exp, fg_ln, fg_cum, fg_neg = (
            sem(n) for n in ("fg_abs", "fg_exp", "fg_ln", "fg_cum", "fg_neg"))
        max_done, exp_done, inv_done, probs_done, y_hi_done, y_done = (
            sem(n) for n in ("max_done", "exp_done", "inv_done", "probs_done", "y_hi_done", "y_done"))
        mixed = sem("mixed")
        z_done = sem("z_done")
        bn_done, var_done, ms_done, rstd_done = (sem(n) for n in ("bn_done", "var_done", "ms_done", "rstd_done"))
        centred, ln_dve, ln_pool = sem("centred"), sem("ln_dve"), sem("ln_pool")
        ssq_done = sem("ssq_done")
        gk_min, gk_exp, gk_abs, gk_ln, cum_done = (sem(n) for n in ("gk_min", "gk_exp", "gk_abs", "gk_ln", "cum_done"))
        diff_done, decay_done, mul_dve, mul_pool = (sem(n) for n in ("diff_done", "decay_done", "mul_dve", "mul_pool"))
        o_sq, o_ms_done, o_rstd_done = (sem(n) for n in ("o_sq", "o_ms_done", "o_rstd_done"))
        gated, h_added, scaled = sem("gated"), sem("h_added"), sem("scaled")
        scaled_act = sem("scaled_act")
        last_tile = sem("last_tile")
        weighted = sem("weighted")
        stored = sem("stored")
        dve_step = sem("dve_step")
        act_step = sem("act_step")

        block = ctx.enter_context(nc.Block())

        def job(name, i=0):
            return JOB[(name, i)]

        def job_done(eng, name, i=0):
            eng.wait_ge(aux_done, job(name, i)[0] + 1)

        def job_read(eng, name, i=0):
            _, bank, turn = job(name, i)
            eng.wait_ge(aux_read[bank], turn + 1)

        def bank_of(name, i=0):
            return aux[job(name, i)[1]]

        def read_of(name, i=0):
            return aux_read[job(name, i)[1]]

        def panel_banks(p):
            return acc[2 * (p % 2)], acc[2 * (p % 2) + 1]

        def panel_done(eng, p, i=0, uper=0):
            eng.wait_ge(unit_used, i * uper + panel_end(p))

        def panel_read(eng, p, tiles=2, i=0, per=0):
            eng.wait_ge(acc_read[p % 2], i * per + (2 * (p // 2) + tiles))

        @block.sync
        def _(sp):
            def load(u, src, i=0, per=0):
                if u >= RING:
                    sp.wait_ge(lo_done, i * per + (u - RING + 1))
                    if per:
                        sp.nop(nofuse=True)
                sp.dma_start(w_raw[u % RING][:], src).then_inc(landed[u % RING], 16)

            def rows(w, r, col):
                return w[r:r + UNIT * P, col].rearrange("(c p) n -> p c n", p=P)

            def panel(w, u, col, i=0, per=0):
                for j in range(UPP):
                    load(u + j, rows(w, j * UNIT * P, col), i, per)

            xs = x[0].rearrange("(t p) d -> p t d", p=P)
            for c in range(PO):
                sp.dma_start(x_tok[:, :, c * N:(c + 1) * N], xs[:, :, c * N:(c + 1) * N]).then_inc(x_in[c], 16)
                load(U_IN + c, rows(w_in[0], c * UNIT * P, slice(COLS1[0], COLS1[0] + N)))
            for j in range(PO, UPP):
                load(U_IN + j, rows(w_in[0], j * UNIT * P, slice(COLS1[0], COLS1[0] + N)))
            for p, c in enumerate(COLS1[1:], 1):
                panel(w_in[0], U_IN + p * UPP, slice(c, c + N))
            with sp.Fori(0, PO) as n:
                panel(w_out[0], U_OUT, bass.ds(n * N, N), n, UPP)
            for n in range(PO):
                load(U_PP + n, rows(ple_w_proj[0], 0, slice(n * N, (n + 1) * N)))
            with sp.Fori(0, NPG) as n:
                panel(gla_w_in[0], U_G, bass.ds(n * N, N), n, UPP)
            with sp.Fori(0, PO) as n:
                panel(gla_w_out[0], U_GO, bass.ds(n * N, N), n, UPP)
            panel(ffn_w_in[0], U_F, slice(0, N))
            panel(ffn_w_in[0], U_F + UPP, slice(D_FF, D_FF + N))

            def out_rows(f, n, k):
                r = f * N + k * UNIT * P
                return ffn_w_out[0][bass.ds(r, UNIT * P), n * N:(n + 1) * N].rearrange("(c p) n -> p c n", p=P)

            with sp.Fori(0, NF - 1) as f:
                panel(ffn_w_in[0], U_FL, bass.ds(f * N + N, N), f, FU)
                panel(ffn_w_in[0], U_FL + UPP, bass.ds(f * N + (D_FF + N), N), f, FU)
                for n in range(PO):
                    for k in range(ROWS_F):
                        load(U_FL + 2 * UPP + n * ROWS_F + k, out_rows(f, n, k), f, FU)
            for n in range(PO):
                for k in range(ROWS_F):
                    load(U_FE + n * ROWS_F + k, out_rows(NF - 1, n, k))
            with sp.Fori(0, PO) as n:
                panel(ple_w_gate[0], U_PG, bass.ds(n * N, N), n, UPP)
            outs = out[0].rearrange("(t p) d -> p t d", p=P)
            stores = ((scaled, 1, 0, 3 * N, 4 * N), (scaled, 2, 0, 0, 3 * N), (scaled, 3, 1, 3 * N, 4 * N),
                      (scaled, 4, 1, 0, N), (scaled_act, 1, 1, N, 3 * N))
            for done, count, t, lo, hi in stores:
                sp.wait_ge(done, count)
                sp.dma_start(outs[:, t, lo:hi], h_tok[:, t, lo:hi]).then_inc(stored, 16)
            sp.wait_ge(stored, 16 * len(stores))

        @block.gpsimd
        def _(pool):
            nc.gpsimd.memset(ident[:], 0.0).then_inc(consts, 1)
            pool.wait_ge(consts, 1)
            nc.gpsimd.affine_select(ident[:], ident[:], [[-1, P]], ALU.not_equal, 1.0, base=0,
                                    channel_multiplier=1).then_inc(consts, 1)
            with nc.allow_non_contiguous_dma(reason="columns of eight"):
                pool.dma_start(fg_raw[:], w_in[0][:, FG0:FG0 + NH].rearrange("(c p) n -> p c n", p=P)).then_inc(fg_in, 16)
            for r, n, src in ((V_CONV, 12, conv_w[0].rearrange("k (b p) -> (k b) p", p=P)),
                              (V_PS, 4, pool_scale[0].rearrange("(b p) -> b p", p=P)),
                              (V_MIX, 16, mixer_norm[0].rearrange("(b p) -> b p", p=P)),
                              (V_ON, 4, gla_out_norm[0].rearrange("(b p) -> b p", p=P)),
                              (V_FFN, 16, ffn_norm[0].rearrange("(b p) -> b p", p=P)),
                              (V_PLE, 16, ple_norm[0].rearrange("(b p) -> b p", p=P))):
                pool.dma_start(vec_raw[r:r + n, :], src).then_inc(vec_in, 16)
            pool.dma_start(bf_col[:], b_f[0].rearrange("(h a) -> h a", a=1)).then_inc(vec_in, 16)
            pool.dma_start(pool_sb[:], pool_w[0].rearrange("g c d -> c g d")).then_inc(pool_in, 16)
            nc.gpsimd.memset(sel[:], 0.0).then_inc(consts, 1)
            pool.wait_ge(consts, 3)
            nc.gpsimd.affine_select(sel[:], sel[:], [[-1, NH], [0, P]], ALU.not_equal, 1.0, base=0,
                                    channel_multiplier=1).then_inc(consts, 1)
            nc.gpsimd.memset(causal[:], 0.0).then_inc(consts, 1)
            pool.wait_ge(consts, 5)
            for c in (0, 2 * P):
                nc.gpsimd.affine_select(causal[:, c:c + P], causal[:, c:c + P], [[-1, P]], ALU.is_ge, -3.0e38,
                                        base=0, channel_multiplier=1).then_inc(consts, 1)
            nc.gpsimd.iota(iota_i[:], [[1, TOK]], base=1, channel_multiplier=0).then_inc(consts, 1)
            pool.wait_ge(consts, 8)
            nc.gpsimd.tensor_copy(iota_f[:], iota_i[:]).then_inc(consts, 1)
            nc.gpsimd.memset(minus_half[:], -0.5).then_inc(consts, 1)
            nc.gpsimd.memset(masks[:], 1.0).then_inc(consts, 1)
            pool.wait_ge(consts, 11)
            k = 11
            for li, h in enumerate(LEVELS[:-1]):
                nb = P // (2 * h)
                for way in range(2):
                    m = masks[:, li, way, :].rearrange("p (b r) -> p b r", r=h)
                    lo = h * way
                    nc.gpsimd.affine_select(m, m, [[-2 * h, nb], [0, h]], ALU.is_ge, 0.0, base=-lo,
                                            channel_multiplier=1).then_inc(consts, 1)
                    k += 1
                    pool.wait_ge(consts, k)
                    nc.gpsimd.affine_select(m, m, [[2 * h, nb], [0, h]], ALU.is_ge, 0.0, base=lo + h - 1,
                                            channel_multiplier=-1).then_inc(consts, 1)
                    k += 1
                    pool.wait_ge(consts, k)

            job_done(pool, "s", NH - 1)
            pool.dma_start(h_tok[:], x[0].rearrange("(t p) d -> p t d", p=P)).then_inc(x_back, 16)
            pool.wait_ge(y_done, NH + 2)
            pool.dma_start(p_tok[:], p_2[0, 0].rearrange("(t p) d -> p t d", p=P)).then_inc(p_in, 16)
            pool.dma_start(ln_gb[:, 0, :], ln_g[0].partition_broadcast(P)).then_inc(gb_in, 16)
            pool.dma_start(ln_gb[:, 1, :], ln_b[0].partition_broadcast(P)).then_inc(gb_in, 16)
            pool.dma_start(lr_raw[:], gla_w_in[0][:, LR0:LR0 + 2 * RANK].rearrange("(c p) n -> p c n", p=P)).then_inc(lr_in, 16)
            pool.wait_ge(ms_done, 1)
            nc.gpsimd.tensor_tensor(rstd[0][:], ms[:], minus_half[:], ALU.pow).then_inc(rstd_done, 1)
            pool.wait_ge(gb_in, 32)
            for n in (2, 3):
                pool.wait_ge(centred, 2 * (n + 1))
                s = slice(n * N, (n + 1) * N)
                nc.gpsimd.tensor_tensor(h_tok[:, 1, s], h_tok[:, 1, s], ln_gb[:, 0, s], ALU.mult).then_inc(ln_pool, 1)
                pool.wait_ge(ln_pool, 2 * (n - 2) + 1)
                nc.gpsimd.tensor_tensor(h_tok[:, 1, s], h_tok[:, 1, s], ln_gb[:, 1, s], ALU.add).then_inc(ln_pool, 1)
            pool.wait_ge(unit_used, U_PP)
            nc.gpsimd.memset(gate_up[:], 0.0).then_inc(up_clear, 1)
            pool.wait_ge(up_clear, 1)
            for z in range(2):
                pool.dma_start(gate_up[z * RANK:(z + 1) * RANK, z, :], gla_w_gate_up[0, z]).then_inc(up_in, 16)
                pool.dma_start(gate_up[2 * RANK:2 * RANK + 1, z, :], gla_b_gate[0, z:z + 1, :]).then_inc(up_in, 16)
            panel_read(pool, P_PP + 2)
            panel_read(pool, P_PP + 3)
            pool.dma_start(emb_dram, emb[:]).then_inc(emb_out, 16)
            pool.wait_ge(ms_done, 2)
            nc.gpsimd.tensor_tensor(rstd[1][:], ms[:], minus_half[:], ALU.pow).then_inc(rstd_done, 1)
            for s in range(STEPS):
                way, h = s // NL, LEVELS[s % NL]
                pool.wait_ge(decay_done, s + 1)
                if s == 0:
                    for i in range(8):
                        job_read(pool, "gt", i)
                d = halves(decayed[s % 3][:].rearrange("p d t -> p (d t)"), h)
                src = halves((gkT, gqT)[way][:].rearrange("p d t -> p (d t)"), h)
                nc.gpsimd.tensor_tensor(d[:, :, 0, :], d[:, :, 0, :], src[:, :, 0, :], ALU.mult).then_inc(mul_pool, 1)
            for hd in range(GH):
                pool.wait_ge(o_ms_done, hd + 1)
                nc.gpsimd.tensor_tensor(o_rstd[:, hd, :], o_ms[:, hd, :], minus_half[:], ALU.pow).then_inc(o_rstd_done, 1)
            job_done(pool, "av", 2 * GH - 1)
            pool.wait_ge(emb_out, 16)
            pool.dma_start(emb[:], emb_dram).then_inc(emb_in, 16)
            pool.wait_ge(unit_used, U_GO + UPP)
            pool.dma_start(fin_w[:], final_norm.partition_broadcast(P)).then_inc(fin_in, 16)
            pool.wait_ge(fin_in, 16)
            for i in (2, 3):
                pool.wait_ge(ms_done, i + 1)
                nc.gpsimd.tensor_tensor(rstd[i][:], ms[:], minus_half[:], ALU.pow).then_inc(rstd_done, 1)
            for n in range(PO - 1):
                for t in range(TT):
                    pool.wait_ge(ssq_done, 3 * TT * PO + TT * (n + 1))
                    s = slice(n * N, (n + 1) * N)
                    nc.gpsimd.tensor_tensor(h_tok[:, t, s], h_tok[:, t, s], fin_w[:, s], ALU.mult).then_inc(weighted, 1)
            for t in range(TT):
                pool.wait_ge(ms_done, 5 + t)
                nc.gpsimd.tensor_tensor(rstd[0][:, t:t + 1], ms[:, t:t + 1], minus_half[:, t:t + 1],
                                        ALU.pow).then_inc(rstd_done, 1)

        @block.tensor
        def _(pe):
            def unit(u, p, hi, lo, k, first, last, i=0, per=0, pper=0):
                pe.wait_ge(lo_done, i * per + (u + 1))
                if first and p >= 2:
                    panel_read(pe, p - 2, 2, i, pper)
                banks = panel_banks(p)
                for c in range(UNIT):
                    for t in range(TT):
                        tok = slice(t * P, (t + 1) * P)
                        st, en = first and c == 0, last and c == UNIT - 1
                        wh, wl = w_hi[u % RING][:, c, :], w_lo[u % RING][:, c, :]
                        pe.matmul(banks[t][:], hi[:, k + c, tok], wh, start=st, stop=False)
                        pe.matmul(banks[t][:], hi[:, k + c, tok], wl, start=False, stop=False)
                        mm = pe.matmul(banks[t][:], lo[:, k + c, tok], wh, start=False, stop=en)
                mm.then_inc(unit_used, 1)

            def begin(name, i=0):
                _, bank, turn = job(name, i)
                if turn:
                    pe.wait_ge(aux_read[bank], turn)
                return aux[bank]

            def turn_tiles(src, b, cols):
                for k in range(2):
                    for t in range(TT):
                        mm = pe.transpose(b[:, (k * TT + t) * P:(k * TT + t + 1) * P],
                                          src[:, t, cols + k * P:cols + (k + 1) * P], ident[:])
                return mm

            def turn_x(c):
                if c % 2 == 0:
                    pe.wait_ge(x_in[c // 2], 16)
                b = begin("x", c)
                turn_tiles(x_tok, b, 2 * c * P).then_inc(aux_done, 1)

            def turn_stage(p):
                panel_read(pe, P_IN + p)
                for i in range(2):
                    b = begin("t", 2 * p + i)
                    turn_tiles(stage[p % 2], b, 2 * i * P).then_inc(aux_done, 1)

            def thin(name, hi, lo, n):
                o = begin(name)[0:n, 0:TOK]
                for k in range(KD):
                    pe.matmul(o, hi[:, k, :], a_hi[:, k, :], start=k == 0, stop=False)
                    pe.matmul(o, lo[:, k, :], a_hi[:, k, :], start=False, stop=False)
                    mm = pe.matmul(o, hi[:, k, :], a_lo[:, k, :], start=False, stop=k == KD - 1)
                mm.then_inc(aux_done, 1)

            def scores(h):
                if h == 0:
                    job_read(pe, "ci")
                b = begin("s", h)
                for c, n, q in ((0, P, 0), (P, TOK, P)):
                    o = b[:, c:c + n]
                    pe.matmul(o, qT[:, h, q:q + P], kT[:, h, 0:n], start=True, stop=False)
                    mm = pe.matmul(o, sel[:, h, :], ncum[:, 0:n], start=False, stop=True)
                mm.then_inc(aux_done, 1)

            def turn_probs(h):
                b = begin("pt_", h)
                pe.wait_ge(probs_done, 2 * (h + 1))
                for c in range(3):
                    mm = pe.transpose(b[:, c * P:(c + 1) * P], probs[:, c * P:(c + 1) * P], ident[:])
                mm.then_inc(aux_done, 1)

            def weigh_values(h):
                job_read(pe, "pt_", h)
                b = begin("ot", h)
                f = slice(h * P, (h + 1) * P)
                pe.matmul(b[:, 0:TOK], v_tok[:, 0, f], probsT[:, 0:TOK], start=True, stop=False)
                pe.matmul(b[:, P:TOK], v_tok[:, 1, f], probsT[:, TOK:3 * P], start=False,
                          stop=True).then_inc(aux_done, 1)

            pe.wait_ge(consts, 2)
            for c in range(2):
                turn_x(c)
            for p in range(NP1):
                for j in range(UPP):
                    u = U_IN + p * UPP + j
                    if p == 0:
                        job_read(pe, "x", j)
                    unit(u, P_IN + p, a_hi, a_lo, 2 * j, j == 0, j == UPP - 1)
                    if p == 0 and j < UPP - 2:
                        turn_x(2 + j)
                    if (p, j) == (0, UPP - 1):
                        pe.wait_ge(vec_in, 7 * 16)
                        b = begin("vec")
                        pe.transpose(b[:, 0:NVEC], vec_raw[:], ident[0:NVEC, 0:NVEC]).then_inc(aux_done, 1)
                    if (p, j) == (1, 0):
                        pe.wait_ge(fg_split, 1)
                        thin("fg", fg_hi, fg_lo, NH)
                    if j == 1 and p >= 1 and p - 1 not in (PV, PV + 1):
                        turn_stage(p - 1)
                    if (p, j) == (1, 6):
                        pe.wait_ge(fg_cum, 1)
                        b = begin("ci")
                        for t in range(TT):
                            mm = pe.transpose(b[:, t * NH:(t + 1) * NH], fgz[:, t * P:(t + 1) * P], ident[0:NH, 0:NH])
                        mm.then_inc(aux_done, 1)
                    if (p, j) == (13, 3):
                        pe.wait_ge(z_done, 1)
                        pe.wait_ge(pool_in, 16)
                        for i in range(2):
                            b = begin("pool", i)
                            for k in range(2):
                                mm = pe.matmul(b[:, k * TOK:(k + 1) * TOK], pool_sb[:, 2 * i + k, :],
                                               poolz[:, 2 * i + k, :], start=True, stop=True)
                            mm.then_inc(aux_done, 1)
                    for name, h in head_jobs(u):
                        {"s": scores, "pt_": turn_probs, "ot": weigh_values}[name](h)

            def out_panel(n, j, i=0, per=0, pper=0):
                unit(U_OUT + n * UPP + j, P_OUT + n, y_hi, y_lo, 2 * j, j == 0, j == UPP - 1, i, per, pper)

            for j in range(UPP):
                pe.wait_ge(y_done, NH if j < 4 else NH + 1 if j < 6 else NH + 2)
                out_panel(0, j)
                if j == 1:
                    turn_stage(PPG)
                if j == UPP - 1:
                    pe.wait_ge(p_in, 16)
                    b = begin("pt")
                    turn_tiles(p_tok, b, 0).then_inc(aux_done, 1)
            for n in range(1, PO):
                for j in range(UPP):
                    out_panel(n, j)
            job_read(pe, "pt")
            for n in range(PO):
                unit(U_PP + n, P_PP + n, a_hi, a_lo, P_CHUNK, True, True)

            def turn_hn(c):
                n = c // 2
                pe.wait_ge(ln_dve, 2 * (2 * (n + 1)) if n < 2 else 8 + 2 * (n - 1))
                if n >= 2:
                    pe.wait_ge(ln_pool, 2 * (n - 1))
                b = begin("hn", c)
                turn_tiles(h_tok, b, 2 * c * P).then_inc(aux_done, 1)

            def diagonal(i):
                b = begin("dg", i)
                for c in range(4):
                    hd, t = 2 * i + c // 2, c % 2
                    tok = slice(t * P, (t + 1) * P)
                    for kb in range(2):
                        mm = pe.matmul(b[:, c * P:(c + 1) * P], gkT[:, 2 * hd + kb, tok], gqT[:, 2 * hd + kb, tok],
                                       start=kb == 0, stop=kb == 1)
                mm.then_inc(aux_done, 1)

            def step(s):
                way, h = s // NL, LEVELS[s % NL]
                pe.wait_ge(mul_dve, s + 1)
                pe.wait_ge(mul_pool, s + 1)
                b = begin("step", s)
                d = decayed[s % 3]
                if h == P:
                    for hd in range(GH):
                        for kb in range(2):
                            tiles = [d[:, 2 * hd + kb, t * P:(t + 1) * P] for t in range(TT)]
                            mm = pe.matmul(b[:, hd * P:(hd + 1) * P], tiles[way], tiles[1 - way],
                                           start=kb == 0, stop=kb == 1)
                else:
                    for c in range(GH * TT):
                        hd, t = c // 2, c % 2
                        for kb in range(2):
                            tile = d[:, 2 * hd + kb, t * P:(t + 1) * P]
                            mm = pe.matmul(b[:, c * 64:(c + 1) * 64], tile, halves(tile, h)[:, :, 1 - way, :],
                                           start=kb == 0, stop=kb == 1)
                mm.then_inc(aux_done, 1)

            def apply_values(hd):
                f = slice(hd * GDV, (hd + 1) * GDV)
                if hd == 0:
                    job_read(pe, "step", STEPS - 1)
                    panel_read(pe, P_G + 7)
                for t in range(TT):
                    b = begin("av", 2 * hd + t)
                    pe.matmul(b[:], at_diag[:, hd, t, :], gv[:, t, f], start=True, stop=False)
                    pe.matmul(b[:], at_off[:, hd, 1 - t, :], gv[:, 1 - t, f], start=False,
                              stop=True).then_inc(aux_done, 1)

            def turn_o(hd):
                for t in range(TT):
                    job_read(pe, "av", 2 * hd + t)
                for i in range(2):
                    b = begin("o", 2 * hd + i)
                    turn_tiles(og[hd], b, 2 * i * P).then_inc(aux_done, 1)

            for c in range(2):
                turn_hn(c)
            for g in range(NPG * UPP):
                p, j = g // UPP, g % UPP
                if p == 0:
                    job_read(pe, "hn", j)
                unit(U_G + g, P_G + p, a_hi, a_lo, 2 * j, j == 0, j == UPP - 1)
                if g < UPP - 2:
                    turn_hn(2 + g)
                for name, i in gla_jobs(g):
                    if name == "lr":
                        pe.wait_ge(lr_split, 1)
                        thin("lr", lr_hi, lr_lo, 2 * RANK)
                    if name == "gt":
                        if i % 2 == 0:
                            panel_read(pe, P_G + i // 2)
                        b = begin("gt", i)
                        turn_tiles(og[i // 2], b, 2 * (i % 2) * P).then_inc(aux_done, 1)
                    if name == "lr_tok":
                        job_read(pe, "lr")
                        b = begin("lr_tok")
                        for t in range(TT):
                            mm = pe.transpose(b[:, t * 2 * RANK:(t + 1) * 2 * RANK], lrT[0:2 * RANK, t * P:(t + 1) * P],
                                              ident[0:2 * RANK, 0:2 * RANK])
                        mm.then_inc(aux_done, 1)
                    if name == "lrt":
                        job_read(pe, "lr_tok")
                        b = begin("lrt")
                        for t in range(TT):
                            mm = pe.transpose(b[0:2 * RANK + 1, t * P:(t + 1) * P], lrt[:, t, :], ident[:])
                        mm.then_inc(aux_done, 1)
                    if name == "gk":
                        if i == 0:
                            job_read(pe, "lrt")
                            pe.wait_ge(up_in, 64)
                        b = begin("gk", i)
                        for k in range(2):
                            blk = 2 * (i % 4) + k
                            mm = pe.matmul(b[:, k * TOK:(k + 1) * TOK], gate_up[:, i // 4, blk * P:(blk + 1) * P],
                                           lrT[:], start=True, stop=True)
                        mm.then_inc(aux_done, 1)
                    if name == "dg":
                        if i == 0:
                            job_read(pe, "gt", 6)
                            job_read(pe, "gt", 7)
                        diagonal(i)
                    if name == "step":
                        step(i)
                    if name == "av" and i % 2 == 0:
                        apply_values(i // 2)
                    if name == "o" and i % 2 == 0:
                        turn_o(i // 2)

            def turn_h(name, i, panel):
                b = begin(name, i)
                turn_tiles(h_tok, b, i * 2 * P).then_inc(aux_done, 1)

            for n in range(PO):
                for j in range(UPP):
                    if n == 0 and j == 0:
                        for i in range(6):
                            job_read(pe, "o", i)
                    if n == 0 and j == 6:
                        job_read(pe, "o", 6)
                        job_read(pe, "o", 7)
                    unit(U_GO + n * UPP + j, P_GO + n, y_hi, y_lo, 2 * j, j == 0, j == UPP - 1)
                    if n == 0 and j == 1:
                        turn_o(3)
                    if n >= 1 and j == 1:
                        panel_read(pe, P_GO + n - 1)
                        turn_h("h1", 2 * n - 2, n - 1)
                        turn_h("h1", 2 * n - 1, n - 1)

            for j in range(UPP):
                job_read(pe, "h1", j)
                unit(U_F + j, P_F, a_hi, a_lo, 2 * j, j == 0, j == UPP - 1)
                if j == 1:
                    panel_read(pe, P_GO + 3)
                    turn_h("h1", 6, 3)
                    turn_h("h1", 7, 3)
            for j in range(UPP):
                unit(U_F + UPP + j, P_F + 1, a_hi, a_lo, 2 * j, j == 0, j == UPP - 1)

            def turn_act(f):
                for k in range(2):
                    n, bank, turn = job("a", k)
                    pe.wait_ge(aux_read[bank], f + turn)
                    turn_tiles(act_tok, aux[bank], 2 * k * P).then_inc(aux_done, 1)

            def hidden_rows(u, p, hi, lo, n, i=0, per=0, pper=0):
                for k in range(ROWS_F):
                    unit(u + n * ROWS_F + k, p + n, hi, lo, 2 * k, k == 0, k == ROWS_F - 1, i, per, pper)

            def ffn_step(f, last=False):
                for m in range(2):
                    for j in range(UPP):
                        unit(U_FL + m * UPP + j, P_FL + m, a_hi, a_lo, 2 * j, j == 0, j == UPP - 1, f, FU, FP)
                        if (m, j) == (0, 2):
                            panel_read(pe, P_F + 1, 2, f, FP)
                            turn_act(f)
                for k in range(2):
                    n, bank, turn = job("a", k)
                    pe.wait_ge(aux_read[bank], f + (turn + 1))
                for n in range(PO):
                    hidden_rows(U_FL + 2 * UPP, P_FL + 2, act_hi, act_lo, n, f, FU, FP)
                    if last and n == 1:
                        panel_read(pe, P_FL + 1, 2, f, FP)
                        turn_act(f + 1)

            with pe.Fori(0, NF - 2) as f:
                ffn_step(f)
            ffn_step(NF - 2, last=True)
            for k in range(2):
                job_read(pe, "a", 2 * (NF - 1) + k)
            for n in range(PO):
                hidden_rows(U_FE, P_FE, y_hi, y_lo, n)
                if n >= 1:
                    panel_read(pe, P_FE + n - 1)
                    turn_h("h2", 2 * n - 2, n - 1)
                    turn_h("h2", 2 * n - 1, n - 1)
            for n in range(PO):
                for j in range(UPP):
                    if n == 0:
                        job_read(pe, "h2", j)
                    if n == PO - 1 and j >= UPP - RING:
                        continue
                    unit(U_PG + n * UPP + j, P_PG + n, a_hi, a_lo, 2 * j, j == 0, j == UPP - 1)
                    if (n, j) == (0, 1):
                        panel_read(pe, P_FE + 3)
                        turn_h("h2", 6, 3)
                        turn_h("h2", 7, 3)

            banks = panel_banks(P_PG + PO - 1)
            for t in range(TT):
                tok = slice(t * P, (t + 1) * P)
                for j in range(UPP - RING, UPP):
                    u = U_PG + (PO - 1) * UPP + j
                    pe.wait_ge(lo_done, u + 1)
                    for c in range(UNIT):
                        k = 2 * j + c
                        wh, wl = w_hi[u % RING][:, c, :], w_lo[u % RING][:, c, :]
                        pe.matmul(banks[t][:], a_hi[:, k, tok], wh, start=False, stop=False)
                        pe.matmul(banks[t][:], a_hi[:, k, tok], wl, start=False, stop=False)
                        mm = pe.matmul(banks[t][:], a_lo[:, k, tok], wh, start=False, stop=k == KD - 1)
                mm.then_inc(last_tile, 1)

        @block.scalar
        def _(act):
            def high(u, i=0, per=0):
                turns = per // RING
                act.wait_ge(landed[u % RING], (16 * turns) * i + 16 * (u // RING + 1))
                if u >= RING:
                    act.wait_ge(unit_used, i * per + (u - RING + 1))
                nc.scalar.copy(w_hi[u % RING][:], w_raw[u % RING][:]).then_inc(hi_done, 1)

            def stage_panel(p, dst, scale=None, func=ACT.Copy, i=0, uper=0):
                panel_done(act, p, i, uper)
                for t, b in enumerate(panel_banks(p)):
                    s = 1.0 if scale is None else scale[:, t:t + 1]
                    nc.scalar.activation(dst[:, t, :], b[:], func, scale=s).then_inc(acc_read[p % 2], 1)

            def split_high(name, i, dst, c, done, col=None):
                job_done(act, name, i)
                b = bank_of(name, i)
                if col is None:
                    nc.scalar.copy(dst[:, c:c + 2, :], b[:].rearrange("p (k t) -> p k t", t=TOK)).then_inc(done, 1)
                    return
                for k in range(2):
                    nc.scalar.activation(dst[:, c + k, :], b[:, k * TOK:(k + 1) * TOK], ACT.Copy,
                                         scale=vec[:, col + k:col + k + 1]).then_inc(done, 1)

            counts = {id(ssq_done): 0, id(o_sq): 0}
            last_square = []

            def sum_of_squares(src, dst, done):
                if last_square:
                    act.wait_ge(*last_square[-1])
                nc.scalar.activation(square[:], src, ACT.Square, accum_out=dst).then_inc(done, 1)
                counts[id(done)] += 1
                last_square.append((done, counts[id(done)]))

            for c in range(UPP):
                split_high("x", c, a_hi, 2 * c, x_hi_done)
                if c < RING:
                    high(c)
                if c == 4:
                    act.wait_ge(fg_in, 16)
                    nc.scalar.copy(fg_hi[:], fg_raw[:]).then_inc(fg_hi_done, 1)
                if c >= 4:
                    high(c)
            tanhs = [0]

            def gate_tanh(i):
                job_done(act, "t", i)
                if tanhs[0] >= 2:
                    job_read(act, "t", last_gate[tanhs[0] - 2])
                nc.scalar.activation(tanh[i % 2][:].rearrange("p k t -> p (k t)"), bank_of("t", i)[:], ACT.Tanh,
                                     scale=0.5).then_inc(tanh_done, 1)
                tanhs[0] += 1

            last_gate = [2 * p + k for p in (PGA, PGA + 1, PCG, PPG) for k in range(2)]

            for p in range(NP1):
                for j in range(UPP):
                    u = U_IN + p * UPP + j
                    if u >= 4:
                        high(u + RING)
                    if j == 1 and p >= 1:
                        q = p - 1
                        for i in (2 * q, 2 * q + 1):
                            src = bank_of("t", i)[:].rearrange("p (k t) -> p k t", t=TOK) if ("t", i) in JOB else None
                            if q in (PQ, PQ + 1):
                                job_done(act, "t", i)
                                nc.scalar.activation(qT[:, 2 * i:2 * i + 2, :], src, ACT.Copy,
                                                     scale=float(P) ** -0.5).then_inc(read_of("t", i), 1)
                            if q == PCC:
                                job_done(act, "t", i)
                                k = 2 * (i % 2)
                                act.wait_ge(zeros, 2)
                                nc.scalar.copy(convu[:, k:k + 2, 2:], src).then_inc(read_of("t", i), 1)
                            if q == PPU:
                                job_done(act, "t", i)
                                k = 2 * (i % 2)
                                act.wait_ge(zeros, 1)
                                nc.scalar.copy(poolu[:, k:k + 2, PAD:], src).then_inc(read_of("t", i), 1)
                            if q in (PGA, PGA + 1, PCG):
                                gate_tanh(i)
                    if (p, j) == (1, 3):
                        job_read(act, "fg")
                        nc.scalar.activation(fge[:], fgz[:], ACT.Abs).then_inc(fg_abs, 1)
                        act.wait_ge(fg_abs, 1)
                        nc.scalar.activation(fge[:], fge[:], ACT.Exp, scale=-1.0).then_inc(fg_exp, 1)
                        act.wait_ge(fg_exp, 1)
                        nc.scalar.activation(fge[:], fge[:], ACT.Ln, bias=1.0).then_inc(fg_ln, 1)
                    if (p, j) == (1, 6):
                        job_done(act, "ci")
                        nc.scalar.copy(cum_i[:].rearrange("p t n -> p (t n)"), bank_of("ci")[:, 0:TT * NH]).then_inc(read_of("ci"), 1)
                    for h in range(NH):
                        if u == HEAD0 + HEAD_STEP * h:
                            act.wait_ge(max_done, h + 1)
                            if h:
                                job_done(act, "pt_", h - 1)
                            for t, c in ((0, slice(0, P)), (1, slice(P, 3 * P))):
                                nc.scalar.activation(probs[:, c], logits[:, c], ACT.Exp, bias=neg_max[:, t:t + 1],
                                                     accum_out=row_sum[:, t:t + 1]).then_inc(exp_done, 1)
                        if u == HEAD0 + HEAD_STEP * h + TURN_LAG:
                            job_done(act, "pt_", h)
                            if h:
                                job_done(act, "ot", h - 1)
                            nc.scalar.copy(probsT[:], bank_of("pt_", h)[:, 0:3 * P]).then_inc(read_of("pt_", h), 1)
                        if u == HEAD0 + HEAD_STEP * h + VALUE_LAG:
                            job_read(act, "ot", h)
                            nc.scalar.activation(y_hi[:, h, :], y_head[:], ACT.Copy, scale=0.5).then_inc(y_hi_done, 1)
                    if (p, j) == (13, 4):
                        act.wait_ge(mixed, 1)
                        nc.scalar.activation(y_hi[:, 8:12, :], convy[:], ACT.Copy, scale=0.5).then_inc(y_hi_done, 1)
                    if j == UPP - 1:
                        if p >= 2 and ("t", 2 * (p - 2)) in JOB and p not in (PV, PV + 1):
                            job_done(act, "t", 2 * (p - 2) + 1)
                        dst = v_tok[:, :, (p - PV) * N:(p - PV + 1) * N] if p in (PV, PV + 1) else stage[p % 2]
                        stage_panel(P_IN + p, dst)

            for j in range(UPP):
                high(U_OUT + j + RING)
                if j == 1:
                    gate_tanh(2 * PPG)
                    gate_tanh(2 * PPG + 1)
                    job_read(act, "pool", 1)
                    nc.scalar.activation(y_hi[:, 12:16, :], poolz[:], ACT.Copy, scale=0.5).then_inc(y_hi_done, 1)
                if j == UPP - 1:
                    split_high("pt", 0, a_hi, P_CHUNK, p_hi_done)
            with act.Fori(0, PO - 1) as n:
                for j in range(UPP):
                    high(U_OUT + UPP + j + RING, n, UPP)
            for n in range(PO):
                high(U_PP + n + RING)
                stage_panel(P_PP + n, emb[:, :, n * N:(n + 1) * N])
            def squares(i, n):
                for t in range(TT):
                    sum_of_squares(h_tok[:, t, n * N:(n + 1) * N], ssq[i % 3][:, t, n:n + 1], ssq_done)

            for c in range(UPP):
                split_high("hn", c, a_hi, 2 * c, hn_hi_done, V_MIX + 2 * c)
                if c >= 4:
                    high(U_G + c)
                if c in (3, 5, 7):
                    squares(0, (c - 3) // 2)

            def exp_step(s):
                act.wait_ge(diff_done, 2 * (s + 1))
                d = decayed[s % 3][:].rearrange("p d t -> p (d t)")
                nc.scalar.activation(d, d, ACT.Exp, scale=1.0 / 16.0).then_inc(decay_done, 1)

            for g in range(NPG * UPP):
                p, j = g // UPP, g % UPP
                if g >= 4:
                    high(U_G + g + RING)
                if g == 4:
                    squares(0, PO - 1)
                if g == 5:
                    act.wait_ge(lr_in, 16)
                    nc.scalar.copy(lr_hi[:], lr_raw[:]).then_inc(lr_hi_done, 1)
                if g == 8:
                    job_done(act, "lr")
                    nc.scalar.copy(lrT[0:2 * RANK, :], bank_of("lr")[0:2 * RANK, 0:TOK]).then_inc(read_of("lr"), 1)
                if g == 10:
                    job_done(act, "lr_tok")
                    for t in range(TT):
                        last = nc.scalar.activation(lrt[:, t, 0:2 * RANK],
                                                    bank_of("lr_tok")[:, t * 2 * RANK:(t + 1) * 2 * RANK],
                                                    ACT.Copy, scale=rstd[1][:, t:t + 1])
                    last.then_inc(read_of("lr_tok"), 1)
                if g == 12:
                    job_done(act, "lrt")
                    nc.scalar.copy(lrT[:], bank_of("lrt")[0:2 * RANK + 1, 0:TOK]).then_inc(read_of("lrt"), 1)
                if g in (9, 17, 25, 33):
                    q = (g - 9) // 8
                    for i in (2 * q, 2 * q + 1):
                        job_done(act, "gt", i)
                        src = bank_of("gt", i)[:].rearrange("p (k t) -> p k t", t=TOK)
                        dst, k = (gqT, 2 * i) if q < 2 else (gkT, 2 * (i - 4))
                        nc.scalar.activation(dst[:, k:k + 2, :], src, ACT.Copy,
                                             scale=1.0 / 16.0 if q < 2 else 1.0).then_inc(read_of("gt", i), 1)
                for name, i in gla_jobs(g):
                    if name == "gk":
                        act.wait_ge(gk_min, i + 1)
                        e = gate_tmp[i // 4][:, 2 * (i % 4):2 * (i % 4) + 2, :].rearrange("p k t -> p (k t)")
                        nc.scalar.activation(e, bank_of("gk", i)[:], ACT.Abs).then_inc(read_of("gk", i), 1)
                        act.wait_ge(read_of("gk", i), job("gk", i)[2] + 1)
                        nc.scalar.activation(e, e, ACT.Exp, scale=-1.0).then_inc(gk_exp, 1)
                for way, when in ((0, 19), (1, 49)):
                    if g == when:
                        act.wait_ge(gk_exp, 4 * (way + 1))
                        e = gate_tmp[way][:].rearrange("p k t -> p (k t)")
                        nc.scalar.activation(e, e, ACT.Ln, bias=1.0).then_inc(gk_ln, 1)
                for s in range(STEPS):
                    if g == STEP0 + STEP_GAP * s - 4:
                        exp_step(s)
                for hd in range(GH):
                    if g == AV0 + 3 * hd:
                        for t in range(TT):
                            job_done(act, "av", 2 * hd + t)
                            sum_of_squares(bank_of("av", 2 * hd + t)[:], o_ssq[:, hd, t:t + 1], o_sq)
                    if hd < 3 and g == AV0 + 3 * hd + 3:
                        for i in (2 * hd, 2 * hd + 1):
                            split_high("o", i, y_hi, 2 * i, o_hi_done, V_ON + 2 * (i % 2))
                if j == UPP - 1:
                    if p < 4:
                        act.wait_ge(rstd_done, 2)
                        stage_panel(P_G + p, og[p], rstd[1])
                    elif p < 8:
                        act.wait_ge(emb_out, 16)
                        stage_panel(P_G + p, gv[:, :, (p - 4) * N:(p - 3) * N], rstd[1])
                    else:
                        act.wait_ge(cum_done, 2 * DB)
                        if p >= 10:
                            act.wait_ge(diff_done, 2 * STEPS)
                        stage_panel(P_G + p, og[p - 8], rstd[1], ACT.Silu)

            def split_h(name, n, col):
                for i in (2 * n, 2 * n + 1):
                    split_high(name, i, a_hi, 2 * i, h1_hi_done if name == "h1" else h2_hi_done, col + 2 * i)

            for n in range(PO):
                for j in range(UPP):
                    high(U_GO + n * UPP + j + RING)
                    if n == 0 and j == 1:
                        for i in (6, 7):
                            split_high("o", i, y_hi, 2 * i, o_hi_done, V_ON + 2 * (i % 2))
                    if n >= 1 and j == 1:
                        split_h("h1", n - 1, V_FFN)
                        squares(1, n - 1)
            for m in range(2):
                for j in range(UPP):
                    high(U_F + m * UPP + j + RING)
                    if m == 0 and j == 1:
                        split_h("h1", PO - 1, V_FFN)
                        squares(1, PO - 1)
                    if m == 0 and j == UPP - 1:
                        act.wait_ge(rstd_done, 3)
                        stage_panel(P_F, act_tok, rstd[2], ACT.Silu)

            def split_act(f, dst):
                for k in range(2):
                    n, bank, _ = job("a", k)
                    act.wait_ge(aux_done, 2 * f + (n + 1))
                    nc.scalar.copy(dst[:, 2 * k:2 * k + 2, :],
                                   aux[bank][:].rearrange("p (k t) -> p k t", t=TOK)).then_inc(act_hi_done, 1)

            def ffn_step(f, last=False):
                for j in range(FU):
                    high(U_FL + j + RING, f, FU)
                    if j == 2:
                        split_act(f, act_hi)
                    if j == UPP - 1:
                        stage_panel(P_FL, act_tok, rstd[2], ACT.Silu, f, FU)
                    if last and j == 2 * UPP + 2 * ROWS_F - 1:
                        split_act(f + 1, y_hi)

            with act.Fori(0, NF - 2) as f:
                ffn_step(f)
            ffn_step(NF - 2, last=True)
            for n in range(PO):
                for k in range(ROWS_F):
                    high(U_FE + n * ROWS_F + k + RING)
                if n >= 1:
                    split_h("h2", n - 1, V_PLE)
                    squares(2, n - 1)
            for n in range(PO):
                for j in range(UPP):
                    if U_PG + n * UPP + j + RING < U_END:
                        high(U_PG + n * UPP + j + RING)
                    if (n, j) == (0, 1):
                        split_h("h2", PO - 1, V_PLE)
                        squares(2, PO - 1)
                    if n >= 1 and j == 2:
                        act.wait_ge(h_added, TT * n)
                        squares(3, n - 1)
                if n == 0:
                    act.wait_ge(rstd_done, 4)
                if n < PO - 1:
                    stage_panel(P_PG + n, gate_tok, rstd[3], ACT.Sigmoid)
            p, n = P_PG + PO - 1, PO - 1
            for t in range(TT):
                act.wait_ge(last_tile, t + 1)
                nc.scalar.activation(gate_tok[:, t, :], panel_banks(p)[t][:], ACT.Sigmoid,
                                     scale=rstd[3][:, t:t + 1]).then_inc(acc_read[p % 2], 1)
                act.wait_ge(h_added, TT * n + t + 1)
                sum_of_squares(h_tok[:, t, n * N:(n + 1) * N], ssq[0][:, t, n:n + 1], ssq_done)
            act.wait_ge(rstd_done, 6)
            s = slice(N, 3 * N)
            act.wait_ge(weighted, 2 * (PO - 1))
            nc.scalar.activation(h_tok[:, 1, s], h_tok[:, 1, s], ACT.Copy, scale=rstd[0][:, 1:2]).then_inc(scaled_act, 1)

        @block.vector
        def _(dve):
            steps = [0]

            def link(ins):
                steps[0] += 1
                ins.then_inc(dve_step, 1)
                dve.wait_ge(dve_step, steps[0])

            def low(u, i=0, per=0):
                dve.wait_ge(hi_done, i * per + (u + 1))
                nc.vector.tensor_tensor(w_lo[u % RING][:], w_raw[u % RING][:], w_hi[u % RING][:],
                                        ALU.subtract).then_inc(lo_done, 1)

            def split_low(name, i, hi, lo, c, done, count, col=None):
                dve.wait_ge(done, count)
                b = bank_of(name, i)
                if col is None:
                    nc.vector.tensor_tensor(lo[:, c:c + 2, :], b[:].rearrange("p (k t) -> p k t", t=TOK),
                                            hi[:, c:c + 2, :], ALU.subtract).then_inc(read_of(name, i), 1)
                    return
                for k in range(2):
                    last = nc.vector.scalar_tensor_tensor(lo[:, c + k, :], b[:, k * TOK:(k + 1) * TOK],
                                                          vec[:, col + k:col + k + 1], hi[:, c + k, :],
                                                          ALU.mult, ALU.subtract)
                last.then_inc(read_of(name, i), 1)

            def inverse_root_of(count):
                dve.wait_ge(ssq_done, TT * PO * (count + 1))
                dve.wait_ge(rstd_done, count + 1)
                link(nc.vector.reduce_sum(ms[:], ssq[count % 3][:], AX_X))
                nc.vector.tensor_scalar(ms[:], ms[:], 1.0 / D, RMS_EPS, ALU.mult, ALU.add).then_inc(ms_done, 1)

            for c in range(UPP):
                split_low("x", c, a_hi, a_lo, 2 * c, x_hi_done, c + 1)
                low(c)
                if c == 4:
                    dve.wait_ge(fg_hi_done, 1)
                    nc.vector.tensor_tensor(fg_lo[:], fg_raw[:], fg_hi[:], ALU.subtract).then_inc(fg_split, 1)
            nc.vector.memset(poolu[:, :, 0:PAD], 0.0).then_inc(zeros, 1)
            y_count = [0]
            gates = [0]

            def gate(i, dst):
                gates[0] += 1
                dve.wait_ge(tanh_done, gates[0])
                nc.vector.scalar_tensor_tensor(dst, tanh[i % 2][:], 1.0,
                                               bank_of("t", i)[:].rearrange("p (k t) -> p k t", t=TOK),
                                               ALU.add, ALU.mult).then_inc(read_of("t", i), 1)

            def y_low(src, c, n):
                y_count[0] += 1
                dve.wait_ge(y_hi_done, y_count[0])
                nc.vector.scalar_tensor_tensor(y_lo[:, c:c + n, :], src, 0.5, y_hi[:, c:c + n, :],
                                               ALU.mult, ALU.subtract).then_inc(y_done, 1)

            def attention(u):
                for h in range(NH):
                    if u == HEAD0 + HEAD_STEP * h:
                        if h == 0:
                            dve.wait_ge(consts, 7)
                            job_read(dve, "ci")
                        job_done(dve, "s", h)
                        b = bank_of("s", h)
                        first = nc.vector.scalar_tensor_tensor(logits[:, 0:P], b[:, 0:P], cum_i[:, 0, h:h + 1],
                                                               causal[:, 0:P], ALU.add, ALU.add)
                        nc.vector.scalar_tensor_tensor(logits[:, P:3 * P], b[:, P:3 * P], cum_i[:, 1, h:h + 1],
                                                       causal[:, P:3 * P], ALU.add, ALU.add).then_inc(read_of("s", h), 1)
                        job_read(dve, "s", h)
                        nc.vector.tensor_reduce(neg_max[:, 0:1], logits[:, 0:P], AX_X, ALU.max, negate=True)
                        nc.vector.tensor_reduce(neg_max[:, 1:2], logits[:, P:3 * P], AX_X, ALU.max,
                                                negate=True).then_inc(max_done, 1)
                    if u == HEAD0 + HEAD_STEP * h + 1:
                        dve.wait_ge(exp_done, 2 * (h + 1))
                        nc.vector.reciprocal(inv_sum[:], row_sum[:]).then_inc(inv_done, 1)
                        dve.wait_ge(inv_done, h + 1)
                        for t, c in ((0, slice(0, P)), (1, slice(P, 3 * P))):
                            nc.vector.tensor_scalar(probs[:, c], probs[:, c], inv_sum[:, t:t + 1], None,
                                                    ALU.mult).then_inc(probs_done, 1)
                    if u == HEAD0 + HEAD_STEP * h + VALUE_LAG:
                        job_done(dve, "ot", h)
                        nc.vector.tensor_tensor(y_head[:], bank_of("ot", h)[:, 0:TOK], gaT[:, h, :],
                                                ALU.mult).then_inc(read_of("ot", h), 1)
                        y_low(y_head[:], h, 1)

            for p in range(NP1):
                for j in range(UPP):
                    u = U_IN + p * UPP + j
                    if (p, j) == (0, UPP - 1):
                        job_done(dve, "vec")
                        nc.vector.tensor_copy(vec[:], bank_of("vec")[:, 0:NVEC]).then_inc(read_of("vec"), 1)
                    if (p, j) == (1, 2):
                        dve.wait_ge(vec_in, 7 * 16)
                        job_done(dve, "fg")
                        nc.vector.tensor_scalar(fgz[:], bank_of("fg")[0:NH, 0:TOK], bf_col[:], None, ALU.add).then_inc(read_of("fg"), 1)
                    if (p, j) == (1, 4):
                        dve.wait_ge(fg_ln, 1)
                        link(nc.vector.tensor_scalar(fgz[:], fgz[:], 0.0, None, ALU.min))
                        link(nc.vector.tensor_tensor(fge[:], fgz[:], fge[:], ALU.subtract))
                        link(nc.vector.memset(ncum[:], 1.0))
                        nc.vector.tensor_tensor_scan(fgz[:], ncum[:], fge[:], 0.0, ALU.mult, ALU.add).then_inc(fg_cum, 1)
                        dve.wait_ge(fg_cum, 1)
                        nc.vector.tensor_scalar(ncum[:], fgz[:], -1.0, None, ALU.mult).then_inc(fg_neg, 1)
                    if j == 1 and p >= 1:
                        q = p - 1
                        for i in (2 * q, 2 * q + 1):
                            if ("t", i) not in JOB:
                                continue
                            src = bank_of("t", i)[:].rearrange("p (k t) -> p k t", t=TOK)
                            k = 2 * (i % 2)
                            if q in (PK, PK + 1):
                                job_done(dve, "t", i)
                                nc.vector.tensor_copy(kT[:, 2 * (i - 4):2 * (i - 4) + 2, :], src).then_inc(read_of("t", i), 1)
                            if q in (PGA, PGA + 1):
                                gate(i, gaT[:, 2 * (i - 8):2 * (i - 8) + 2, :])
                            if q == PCH:
                                job_done(dve, "t", i)
                                job_read(dve, "t", 2 * PCC + 1)
                                nc.vector.tensor_tensor(convu[:, k:k + 2, 2:], src, convu[:, k:k + 2, 2:],
                                                        ALU.mult).then_inc(read_of("t", i), 1)
                            if q == PCG:
                                gate(i, convg[:, k:k + 2, :])
                            if q == PCB:
                                job_done(dve, "t", i)
                                nc.vector.tensor_tensor(convg[:, k:k + 2, :], src, convg[:, k:k + 2, :],
                                                        ALU.mult).then_inc(read_of("t", i), 1)
                    attention(u)
                    if u >= 4:
                        low(u + RING)
                    if (p, j) == (2, 2):
                        dve.wait_ge(consts, 9)
                        link(nc.vector.reciprocal(iota_f[:], iota_f[:]))
                    if (p, j) == (2, 4):
                        for g in range(4):
                            nc.vector.tensor_scalar(inv_count[:, g, :], iota_f[:], 1.0 / (2 << g), None,
                                                    ALU.max).then_inc(dve_step, 1)
                        steps[0] += 4
                    if (p, j) == (9, 2):
                        job_read(dve, "t", 2 * PPU)
                        job_read(dve, "t", 2 * PPU + 1)
                        E = PAD + TOK
                        link(nc.vector.tensor_tensor(sum_a[:, :, 1:E], poolu[:, :, 1:E], poolu[:, :, 0:E - 1], ALU.add))
                        link(nc.vector.tensor_tensor(sum_b[:, 1:4, 3:E], sum_a[:, 1:4, 3:E], sum_a[:, 1:4, 1:E - 2], ALU.add))
                    if (p, j) == (9, 3):
                        link(nc.vector.tensor_tensor(sum_a[:, 2:4, 7:E], sum_b[:, 2:4, 7:E], sum_b[:, 2:4, 3:E - 4], ALU.add))
                        link(nc.vector.tensor_tensor(sum_b[:, 3:4, 15:E], sum_a[:, 3:4, 15:E], sum_a[:, 3:4, 7:E - 8], ALU.add))
                        for g in range(4):
                            nc.vector.tensor_tensor(poolz[:, g, :], (sum_a, sum_b)[g % 2][:, g, PAD:E],
                                                    inv_count[:, g, :], ALU.mult).then_inc(dve_step, 1)
                            steps[0] += 1
                        dve.wait_ge(dve_step, steps[0])
                        nc.vector.tensor_tensor(poolz[:], poolz[:], poolu[:, :, PAD:E], ALU.subtract).then_inc(z_done, 1)
                        dve.wait_ge(z_done, 1)
                        nc.vector.memset(convu[:, :, 0:2], 0.0).then_inc(zeros, 1)
                    if (p, j) == (13, 2):
                        job_read(dve, "t", 2 * PCB + 1)
                        for b in range(4):
                            link(nc.vector.tensor_scalar(convy[:, b, :], convu[:, b, 0:TOK],
                                                         vec[:, V_CONV + b:V_CONV + b + 1], None, ALU.mult))
                            for tap in (1, 2):
                                c = V_CONV + 4 * tap + b
                                link(nc.vector.scalar_tensor_tensor(convy[:, b, :], convu[:, b, tap:tap + TOK],
                                                                    vec[:, c:c + 1], convy[:, b, :],
                                                                    ALU.mult, ALU.add))
                        nc.vector.tensor_tensor(convy[:], convy[:], convg[:], ALU.mult).then_inc(mixed, 1)
                    if (p, j) == (13, 4):
                        y_low(convy[:], 8, 4)

            for j in range(UPP):
                low(U_OUT + j + RING)
                if j == 1:
                    for i in range(2):
                        gate(2 * PPG + i, poolg[:, 2 * i:2 * i + 2, :])
                    job_read(dve, "t", 2 * PPG + 1)
                    for g in range(4):
                        last = nc.vector.scalar_tensor_tensor(
                            poolz[:, g, :], bank_of("pool", g // 2)[:, (g % 2) * TOK:(g % 2 + 1) * TOK],
                            vec[:, V_PS + g:V_PS + g + 1], poolg[:, g, :], ALU.mult, ALU.mult)
                        if g == 1:
                            last.then_inc(read_of("pool", 0), 1)
                    last.then_inc(read_of("pool", 1), 1)
                    y_low(poolz[:], 12, 4)
                if j == UPP - 1:
                    split_low("pt", 0, a_hi, a_lo, P_CHUNK, p_hi_done, 1)

            def residual(n, i=0, base_turn=0):
                p = P_OUT + n
                panel_done(dve, p)
                for t, b in enumerate(panel_banks(p)):
                    s = slice(n * N, (n + 1) * N)
                    nc.vector.scalar_tensor_tensor(h_tok[:, t, s], h_tok[:, t, s], ALPHA, b[:], ALU.mult,
                                                   ALU.add).then_inc(acc_read[p % 2], 1)
                for t in range(TT):
                    panel_read(dve, p, t + 1)
                    nc.vector.bn_stats(bn[:, t, n, :], h_tok[:, t, n * N:(n + 1) * N]).then_inc(bn_done, 1)

            dve.wait_ge(x_back, 16)
            residual(0)
            for n in range(1, PO):
                for j in range(UPP):
                    low(U_OUT + n * UPP + j + RING)
                residual(n)
            for t in range(TT):
                dve.wait_ge(bn_done, TT * PO)
                nc.vector.bn_aggr(mv[:, t, :], bn[:, t, :, :].rearrange("p n s -> p (n s)")).then_inc(var_done, 1)
            dve.wait_ge(var_done, 2)
            nc.vector.tensor_scalar(ms[:], mv[:, :, 1], LN_EPS, None, ALU.add).then_inc(ms_done, 1)
            dve.wait_ge(rstd_done, 1)
            dve.wait_ge(gb_in, 32)

            def split_hn(c):
                split_low("hn", c, a_hi, a_lo, 2 * c, hn_hi_done, 2 * (c + 1), V_MIX + 2 * c)

            k = 0
            for n in range(PO):
                for m in ((0,), (1, 2, 3), (), ())[n]:
                    for t in range(TT):
                        s = slice(m * N, (m + 1) * N)
                        nc.vector.tensor_scalar(h_tok[:, t, s], h_tok[:, t, s], mv[:, t, 0:1], rstd[0][:, t:t + 1],
                                                ALU.subtract, ALU.mult).then_inc(centred, 1)
                for t in range(TT if n < 2 else 1):
                    s = slice(n * N, (n + 1) * N)
                    dve.wait_ge(centred, TT * n + t + 1)
                    nc.vector.tensor_tensor(h_tok[:, t, s], h_tok[:, t, s], ln_gb[:, 0, s], ALU.mult).then_inc(ln_dve, 1)
                    k += 1
                    dve.wait_ge(ln_dve, k)
                    nc.vector.tensor_tensor(h_tok[:, t, s], h_tok[:, t, s], ln_gb[:, 1, s], ALU.add).then_inc(ln_dve, 1)
                    k += 1
                low(U_PP + n + RING)
                for c in ((), (0, 1), (2,), (3,))[n]:
                    split_hn(c)
            for c in range(RING, UPP):
                split_hn(c)
                low(U_G + c)

            def flat(t):
                return t[:].rearrange("p d t -> p (d t)")

            def diff(s):
                way, h = s // NL, LEVELS[s % NL]
                if s >= 3:
                    job_done(dve, "step", s - 3)
                d, c = halves(flat(decayed[s % 3]), h), halves(flat(cum[way]), h)
                if way == 0:
                    mid = c[:, :, 0, h - 1:h].broadcast_to([P, DB * TOK // (2 * h), h])
                else:
                    mid = c[:, :, 1, 0:1].broadcast_to([P, DB * TOK // (2 * h), h])
                far, near = (1, 0) if way == 0 else (0, 1)
                if h == P:
                    nc.vector.tensor_copy(d[:, :, far, :], c[:, :, far, :]).then_inc(diff_done, 1)
                else:
                    nc.vector.tensor_tensor(d[:, :, far, :], c[:, :, far, :], mid, ALU.subtract).then_inc(diff_done, 1)
                nc.vector.tensor_tensor(d[:, :, near, :], mid, c[:, :, near, :], ALU.subtract).then_inc(diff_done, 1)

            def times(s):
                way, h = s // NL, LEVELS[s % NL]
                dve.wait_ge(decay_done, s + 1)
                if s == 0:
                    for i in range(8):
                        job_read(dve, "gt", i)
                d = halves(flat(decayed[s % 3]), h)
                src = halves(flat((gqT, gkT)[way]), h)
                nc.vector.tensor_tensor(d[:, :, 1, :], d[:, :, 1, :], src[:, :, 1, :], ALU.mult).then_inc(mul_dve, 1)

            def keep(s):
                way, h = s // NL, LEVELS[s % NL]
                job_done(dve, "step", s)
                b = bank_of("step", s)
                if h == P:
                    nc.vector.tensor_copy(at_off[:, :, way, :],
                                          b[:].rearrange("p (h i) -> p h i", i=P)).then_inc(read_of("step", s), 1)
                    return
                nb = P // (2 * h)
                dst = at_diag[:].rearrange("p h t (b s r) -> p (h t) b s r", s=2, r=h)[:, :, :, 1 - way, :]
                m = masks[:, s % NL, way, :].bitcast(I32).rearrange("p (a b r) -> p a b r", a=1, r=h).broadcast_to([P, GH * TT, nb, h])
                nc.vector.copy_predicated(dst, m, b[:].rearrange("p (c b r) -> p c b r", c=GH * TT, r=h)).then_inc(read_of("step", s), 1)

            def head_out(hd):
                dve.wait_ge(o_rstd_done, hd + 1)
                panel_read(dve, P_G + 8 + hd)
                for t in range(TT):
                    nc.vector.scalar_tensor_tensor(og[hd][:, t, :], bank_of("av", 2 * hd + t)[:],
                                                   o_rstd[:, hd, t:t + 1], og[hd][:, t, :], ALU.mult,
                                                   ALU.mult).then_inc(read_of("av", 2 * hd + t), 1)

            for g in range(NPG * UPP):
                for name, i in gla_jobs(g):
                    if name == "gk":
                        job_done(dve, "gk", i)
                        if i == 4:
                            job_read(dve, "gt", 7)
                        way, k = i // 4, 2 * (i % 4)
                        nc.vector.tensor_scalar(cum[way][:, k:k + 2, :].rearrange("p k t -> p (k t)"), bank_of("gk", i)[:],
                                                0.0, None, ALU.min).then_inc(gk_min, 1)
                    if name == "dg":
                        job_done(dve, "dg", i)
                        idb = ident[:].rearrange("p (a t) -> p a t", a=1).broadcast_to([P, 4, P])
                        nc.vector.scalar_tensor_tensor(
                            at_diag[:, 2 * i:2 * i + 2, :, :].rearrange("p h t i -> p (h t) i"),
                            bank_of("dg", i)[:].rearrange("p (c i) -> p c i", i=P), 2.0, idb,
                            ALU.mult, ALU.mult).then_inc(read_of("dg", i), 1)
                    if name == "step":
                        keep(i)
                if g >= 4:
                    low(U_G + g + RING)
                if g == 4:
                    inverse_root_of(0)
                if g == 5:
                    dve.wait_ge(lr_hi_done, 1)
                    nc.vector.tensor_tensor(lr_lo[:], lr_raw[:], lr_hi[:], ALU.subtract).then_inc(lr_split, 1)
                    nc.vector.memset(lrt[:, :, 2 * RANK:], 1.0).then_inc(zeros, 1)
                    link(nc.vector.memset(restart[:], 1.0))
                    for c in (0, P, TOK):
                        link(nc.vector.memset(restart[:, c:c + 1], 0.0))
                for s in range(STEPS):
                    if g == STEP0 + STEP_GAP * s - 4:
                        if s % NL == 0:
                            dve.wait_ge(cum_done, 8 * (s // NL + 1))
                        diff(s)
                    if g == STEP0 + STEP_GAP * s - 2:
                        times(s)
                for way, when in ((0, 20), (1, 51)):
                    if g == when:
                        dve.wait_ge(gk_ln, way + 1)
                        link(nc.vector.tensor_tensor(flat(cum[way]), flat(cum[way]), flat(gate_tmp[way]), ALU.subtract))
                    if when <= g < when + 4:
                        for b in (2 * (g - when), 2 * (g - when) + 1):
                            c = cum[way][:, b, :]
                            r = restart[:, 0:TOK]
                            if way:
                                c, r = c[:, ::-1], restart[:, 1:TOK + 1][:, ::-1]
                            nc.vector.tensor_tensor_scan(c, r, c, 0.0, ALU.mult, ALU.add).then_inc(cum_done, 1)
                for hd in range(GH):
                    if g == AV0 + 3 * hd:
                        dve.wait_ge(o_sq, TT * (hd + 1))
                        nc.vector.tensor_scalar(o_ms[:, hd, :], o_ssq[:, hd, :], 1.0 / GDV, RMS_EPS, ALU.mult,
                                                ALU.add).then_inc(o_ms_done, 1)
                if g in (AV0 + 1, AV0 + 4, AV0 + 7):
                    hd = (g - AV0 - 1) // 3
                    head_out(hd)
                if g in (AV0 + 3, AV0 + 6, AV0 + 9):
                    hd = (g - AV0 - 3) // 3
                    for i in (2 * hd, 2 * hd + 1):
                        split_low("o", i, y_hi, y_lo, 2 * i, o_hi_done, 2 * (i + 1), V_ON + 2 * (i % 2))

            head_out(GH - 1)

            def add_panel(n, p, i=0, uper=0):
                panel_done(dve, p, i, uper)
                for t, b in enumerate(panel_banks(p)):
                    s = slice(n * N, (n + 1) * N)
                    nc.vector.tensor_tensor(h_tok[:, t, s], h_tok[:, t, s], b[:], ALU.add).then_inc(acc_read[p % 2], 1)

            def split_h(name, n, col):
                for i in (2 * n, 2 * n + 1):
                    split_low(name, i, a_hi, a_lo, 2 * i, h1_hi_done if name == "h1" else h2_hi_done, 2 * (i + 1),
                              col + 2 * i)

            for n in range(PO):
                for j in range(UPP):
                    low(U_GO + n * UPP + j + RING)
                    if n == 0 and j == 1:
                        for i in (6, 7):
                            split_low("o", i, y_hi, y_lo, 2 * i, o_hi_done, 2 * (i + 1), V_ON + 2 * (i % 2))
                    if n >= 1 and j == 1:
                        split_h("h1", n - 1, V_FFN)
                add_panel(n, P_GO + n)

            def multiply(p, i=0, uper=0):
                panel_done(dve, p, i, uper)
                for t, b in enumerate(panel_banks(p)):
                    nc.vector.scalar_tensor_tensor(act_tok[:, t, :], b[:], rstd[2][:, t:t + 1], act_tok[:, t, :],
                                                   ALU.mult, ALU.mult).then_inc(acc_read[p % 2], 1)

            def split_act(f, hi, lo):
                for k in range(2):
                    n, bank, _ = job("a", k)
                    dve.wait_ge(act_hi_done, 2 * f + (k + 1))
                    nc.vector.tensor_tensor(lo[:, 2 * k:2 * k + 2, :],
                                            aux[bank][:].rearrange("p (k t) -> p k t", t=TOK),
                                            hi[:, 2 * k:2 * k + 2, :], ALU.subtract).then_inc(aux_read[bank], 1)

            for m in range(2):
                for j in range(UPP):
                    low(U_F + m * UPP + j + RING)
                    if m == 0 and j == 1:
                        split_h("h1", PO - 1, V_FFN)
                        inverse_root_of(1)
            dve.wait_ge(rstd_done, 3)
            panel_read(dve, P_F)
            multiply(P_F + 1)

            def ffn_step(f, last=False):
                for j in range(FU):
                    low(U_FL + j + RING, f, FU)
                    if j == 2:
                        split_act(f, act_hi, act_lo)
                    if last and j == 2 * UPP + 2 * ROWS_F - 1:
                        split_act(f + 1, y_hi, y_lo)
                    if j == 2 * UPP - 1:
                        panel_read(dve, P_FL, 2, f, FP)
                        multiply(P_FL + 1, f, FU)
                    if j >= 2 * UPP and (j - 2 * UPP) % ROWS_F == ROWS_F - 1:
                        n = (j - 2 * UPP) // ROWS_F
                        add_panel(n, P_FL + 2 + n, f, FU)

            with dve.Fori(0, NF - 2) as f:
                ffn_step(f)
            ffn_step(NF - 2, last=True)
            for n in range(PO):
                for k in range(ROWS_F):
                    low(U_FE + n * ROWS_F + k + RING)
                add_panel(n, P_FE + n)
                if n >= 1:
                    split_h("h2", n - 1, V_PLE)
            for n in range(PO):
                for j in range(UPP):
                    if U_PG + n * UPP + j + RING < U_END:
                        low(U_PG + n * UPP + j + RING)
                    if (n, j) == (0, 1):
                        split_h("h2", PO - 1, V_PLE)
                        inverse_root_of(2)
                if n == 0:
                    dve.wait_ge(emb_in, 16)
                s = slice(n * N, (n + 1) * N)
                for t in range(TT):
                    panel_read(dve, P_PG + n, t + 1)
                    nc.vector.tensor_tensor(gate_tok[:, t, :], gate_tok[:, t, :], emb[:, t, s], ALU.mult).then_inc(gated, 1)
                    dve.wait_ge(gated, TT * n + t + 1)
                    nc.vector.tensor_tensor(h_tok[:, t, s], h_tok[:, t, s], gate_tok[:, t, :], ALU.add).then_inc(h_added, 1)
                    if n == PO - 1:
                        dve.wait_ge(ssq_done, TT * PO * 4 - TT + t + 1)
                        link(nc.vector.reduce_sum(ms[:, t:t + 1], ssq[0][:, t, :], AX_X))
                        nc.vector.tensor_scalar(ms[:, t:t + 1], ms[:, t:t + 1], 1.0 / D, RMS_EPS, ALU.mult,
                                                ALU.add).then_inc(ms_done, 1)
                        dve.wait_ge(rstd_done, 5 + t)
                        nc.vector.scalar_tensor_tensor(h_tok[:, t, s], h_tok[:, t, s], rstd[0][:, t:t + 1], fin_w[:, s],
                                                       ALU.mult, ALU.mult).then_inc(scaled, 1)
                        dve.wait_ge(weighted, 2 * (PO - 1))
                        r = slice(0, 3 * N if t == 0 else N)
                        nc.vector.tensor_scalar(h_tok[:, t, r], h_tok[:, t, r], rstd[0][:, t:t + 1], None,
                                                ALU.mult).then_inc(scaled, 1)


_INS = ["x", "w_in", "b_f", "conv_w", "pool_w", "pool_scale", "w_out", "ln_g", "ln_b", "p_2", "mixer_norm_2",
        "gla_w_in_2", "gla_w_gate_up_2", "gla_b_gate_2", "gla_out_norm_2", "gla_w_out_2", "ffn_norm_2",
        "ffn_w_in_2", "ffn_w_out_2", "ple_norm_2", "ple_w_gate_2", "ple_w_proj_2", "final_norm_2"]


def kernel(**inputs):
    import numpy as np
    import concourse.bacc as bacc
    from concourse.bass_utils import run_bass_kernel_spmd

    nc = bacc.Bacc("TRN2", target_bir_lowering=False, num_devices=1)
    arrays, args = {}, []
    for name in _INS:
        a = np.ascontiguousarray(inputs[name])
        arrays[f"in_{name}"] = a
        args.append(nc.dram_tensor(f"in_{name}", a.shape, mybir.dt.from_np(a.dtype), kind="ExternalInput").ap())
    out = nc.dram_tensor("out", (1, TOK, D), F32, kind="ExternalOutput").ap()
    block_kernel(nc, *args, out)
    r = run_bass_kernel_spmd(nc, [arrays], core_ids=[0])
    return r.results[0]["out"]
```

```python
from contextlib import ExitStack

import concourse.bass as bass
from concourse import mybir

F32 = mybir.dt.float32
F32R = mybir.dt.float32r
I32 = mybir.dt.int32
ALU = mybir.AluOpType
ACT = mybir.ActivationFunctionType
AX_X = mybir.AxisListType.X

P = 128
N = 512
TOK = 256
TT = TOK // P
D = 2048
KD = D // P
UNIT = 2
UPP = KD // UNIT
RING = 4
ATT = 1024
NH = ATT // P
D_FF = 5632
NF = D_FF // N
ROWS_F = N // P // UNIT
PO = D // N
LN_EPS, RMS_EPS = 1e-5, 1e-6
ALPHA = 2.0 ** 0.25
GH, GDK, GDV = 4, 256, 512
RANK = 16
DB = GH * GDK // P

Q0, K0, V0, GA0, FG0 = 0, ATT, 2 * ATT, 3 * ATT, 4 * ATT
CB0 = FG0 + NH
CC0, CH0, CG0, PU0, PG0 = (CB0 + i * N for i in range(1, 6))
COLS1 = [Q0, Q0 + N, K0, K0 + N, GA0, GA0 + N, V0, V0 + N, PU0, CC0, CH0, CG0, CB0, PG0]
NP1 = len(COLS1)
(PQ, PK, PGA, PV, PPU, PCC, PCH, PCG, PCB, PPG) = (0, 2, 4, 6, 8, 9, 10, 11, 12, 13)
NPG = 12
LR0 = NPG * N

U_IN, P_IN = 0, 0
U_OUT, P_OUT = U_IN + NP1 * UPP, P_IN + NP1
U_PP, P_PP = U_OUT + PO * UPP, P_OUT + PO
U_G, P_G = U_PP + PO, P_PP + PO
U_GO, P_GO = U_G + NPG * UPP, P_G + NPG
U_F, P_F = U_GO + PO * UPP, P_GO + PO
U_FL, P_FL = U_F + 2 * UPP, P_F + 2
FU, FP = 2 * UPP + PO * ROWS_F, 2 + PO
U_FE, P_FE = U_FL + (NF - 1) * FU, P_FL + (NF - 1) * FP
U_PG, P_PG = U_FE + PO * ROWS_F, P_FE + PO
U_END = U_PG + PO * UPP

HEAD0, HEAD_STEP = U_IN + PV * UPP + 2 * UPP + 2, 4
TURN_LAG, VALUE_LAG = 3, 5
LEVELS = [1, 2, 4, 8, 16, 32, 64, 128]
NL = len(LEVELS)
STEP0, STEP_GAP = 37, 6
GK0 = 14
LN_G, SUM_G = (19, 24), (20, 25)
AV0 = 84
P_CHUNK = KD - UNIT

V_CONV, V_PS, V_MIX, V_ON, V_FFN, V_PLE, NVEC = 0, 12, 16, 32, 36, 52, 68


def small_products():
    order = [("x", i) for i in range(UPP)] + [("vec", 0)]
    for p in range(NP1):
        for j in range(UPP):
            u = p * UPP + j
            if (p, j) == (1, 0):
                order.append(("fg", 0))
            if j == 1 and p >= 1 and p - 1 not in (PV, PV + 1):
                order += [("t", 2 * (p - 1)), ("t", 2 * (p - 1) + 1)]
            if (p, j) == (1, 6):
                order.append(("ci", 0))
            if (p, j) == (13, 3):
                order += [("pool", 0), ("pool", 1)]
            order += head_jobs(u)
    order += [("t", 2 * PPG), ("t", 2 * PPG + 1), ("pt", 0)]
    order += [("hn", i) for i in range(UPP)]
    for g in range(NPG * UPP):
        order += [(name, i) for name, i in gla_jobs(g)]
    order += [("o", 6), ("o", 7)]
    order += [("h1", i) for i in range(2 * PO)]
    named = {}
    turns = [0, 0, 0, 0]
    for n, key in enumerate(order):
        named[key] = (n, n % 4, turns[n % 4])
        turns[n % 4] += 1
    n = len(order)
    for f in range(NF):
        for b in range(2):
            named[("a", 2 * f + b)] = (n, b, turns[b])
            turns[b] += 1
            n += 1
    for i in range(2 * PO):
        b = (2 + i) % 4
        named[("h2", i)] = (n, b, turns[b])
        turns[b] += 1
        n += 1
    return named


def panel_end(p):
    for u0, p0, units in ((U_PG, P_PG, UPP), (U_FE, P_FE, ROWS_F), (U_FL + 2 * UPP, P_FL + 2, ROWS_F),
                          (U_G, P_G, UPP), (U_PP, P_PP, 1)):
        if p >= p0:
            return u0 + (p - p0 + 1) * units
    return (p + 1) * UPP


def head_jobs(u):
    found = []
    for h in range(NH):
        for name, lag in (("s", 0), ("pt_", TURN_LAG), ("ot", VALUE_LAG)):
            if u == HEAD0 + HEAD_STEP * h + lag:
                found.append((name, h))
    return found


def gla_jobs(g):
    found = []
    if g == 8:
        found.append(("lr", 0))
    if g in (9, 17, 25, 33):
        p = (g - 9) // 8
        found += [("gt", 2 * p), ("gt", 2 * p + 1)]
    if g == 10:
        found.append(("lr_tok", 0))
    if g == 12:
        found.append(("lrt", 0))
    if GK0 <= g < GK0 + 8:
        found.append(("gk", g - GK0))
    if g == 34:
        found += [("dg", 0), ("dg", 1)]
    if g >= STEP0 and (g - STEP0) % STEP_GAP == 0 and (g - STEP0) // STEP_GAP < NL:
        found += [("step", 2 * ((g - STEP0) // STEP_GAP) + i) for i in range(2)]
    if g >= AV0 and (g - AV0) % 3 == 0 and (g - AV0) // 3 < GH:
        h = (g - AV0) // 3
        found += [("av", 2 * h), ("av", 2 * h + 1)]
    if g in (AV0 + 3, AV0 + 6, AV0 + 9):
        h = (g - AV0 - 3) // 3
        found += [("o", 2 * h), ("o", 2 * h + 1)]
    return found


def halves(ap, h):
    return ap.rearrange("p (q s r) -> p q s r", s=2, r=h)


def block_kernel(nc, x, w_in, b_f, conv_w, pool_w, pool_scale, w_out, ln_g, ln_b, p_2,
                 mixer_norm, gla_w_in, gla_w_gate_up, gla_b_gate, gla_out_norm, gla_w_out,
                 ffn_norm, ffn_w_in, ffn_w_out, ple_norm, ple_w_gate, ple_w_proj, final_norm, out):
    JOB = small_products()
    KB = 1024
    base = 16512

    def at(name, shape, dt, offset):
        return nc.alloc_sbuf_tensor_at(name, shape, dt, offset=base + offset)

    w_raw = [at(f"w_raw{s}", [P, UNIT, N], F32, s * 4 * KB) for s in range(RING)]
    w_hi = [at(f"w_hi{s}", [P, UNIT, N], F32R, (16 + s * 4) * KB) for s in range(RING)]
    w_lo = [at(f"w_lo{s}", [P, UNIT, N], F32R, (32 + s * 4) * KB) for s in range(RING)]
    a_hi = at("a_hi", [P, KD, TOK], F32R, 48 * KB)
    a_lo = at("a_lo", [P, KD, TOK], F32R, 64 * KB)
    y_hi = at("y_hi", [P, KD, TOK], F32R, 80 * KB)
    y_lo = at("y_lo", [P, KD, TOK], F32R, 96 * KB)
    x_tok = at("x_tok", [P, TT, D], F32, 80 * KB)
    decayed = [at(f"decayed{s}", [P, DB, TOK], F32, (80 + 8 * s) * KB) for s in range(4)]
    gate_up = at("gate_up", [2 * RANK + 1, 2, GH * GDK], F32, 104 * KB)
    h_tok = at("h_tok", [P, TT, D], F32, 112 * KB)
    qT = at("qT", [P, NH, TOK], F32, 112 * KB)
    kT = at("kT", [P, NH, TOK], F32, 120 * KB)
    W = 128 * KB
    stage = [at(f"stage{s}", [P, TT, N], F32, W + s * 4 * KB) for s in range(2)]
    v_tok = at("v_tok", [P, TT, ATT], F32, W + 8 * KB)
    gaT = at("gaT", [P, NH, TOK], F32, W + 16 * KB)
    PAD = 16
    poolu = at("poolu", [P, 4, PAD + TOK], F32, W + 24 * KB)
    convu = at("convu", [P, 4, 2 + TOK], F32, W + 24 * KB)
    sum_a = at("sum_a", [P, 4, PAD + TOK], F32, W + 28 * KB + 512)
    convg = at("convg", [P, 4, TOK], F32, W + 28 * KB + 512)
    sum_b = at("sum_b", [P, 4, PAD + TOK], F32, W + 33 * KB)
    convy = at("convy", [P, 4, TOK], F32, W + 33 * KB)
    poolz = at("poolz", [P, 4, TOK], F32, W + 37 * KB + 512)
    poolg = at("poolg", [P, 4, TOK], F32, W + 41 * KB + 512)
    tanh = [at(f"tanh{s}", [P, 2, TOK], F32, W + (45 + 2 * s) * KB + 512) for s in range(2)]
    logits = at("logits", [P, 3 * P], F32, W + 49 * KB + 512)
    probs = at("probs", [P, 3 * P], F32, W + 51 * KB)
    probsT = at("probsT", [P, 3 * P], F32, W + 52 * KB + 512)
    y_head = at("y_head", [P, TOK], F32, W + 54 * KB)
    sel = at("sel", [NH, NH, P], F32, W + 55 * KB)
    inv_count = at("inv_count", [P, 4, TOK], F32, W + 59 * KB)
    causal = at("causal", [P, 3 * P], F32, W + 63 * KB)
    pool_sb = at("pool_sb", [P, 4, P], F32, W + 64 * KB + 512)
    ln_gb = at("ln_gb", [P, 2, D], F32, W)
    og = [at(f"og{s}", [P, TT, N], F32, W + 4 * s * KB) for s in range(4)]
    gate_tmp = decayed[0:2]
    gv = at("gv", [P, TT, GH * GDV], F32, W + 16 * KB)
    gqT = at("gqT", [P, DB, TOK], F32, W + 32 * KB)
    gkT = at("gkT", [P, DB, TOK], F32, W + 40 * KB)
    cum = [at("cum_fwd", [P, DB, TOK], F32, W + 48 * KB), at("cum_bwd", [P, DB, TOK], F32, W + 8 * KB)]
    at_diag = at("at_diag", [P, GH, TT, P], F32, W + 56 * KB)
    at_off = at("at_off", [P, GH, 2, P], F32, W + 60 * KB)
    lr_raw = at("lr_raw", [P, KD, 2 * RANK], F32, W + 56 * KB)
    lr_hi = at("lr_hi", [P, KD, 2 * RANK], F32R, W + 58 * KB)
    lr_lo = at("lr_lo", [P, KD, 2 * RANK], F32R, W + 60 * KB)
    lrt = at("lrt", [P, TT, 2 * RANK + 1], F32, W + 64 * KB)
    lrT = at("lrT", [2 * RANK + 1, TOK], F32, W + 64 * KB + 288)
    restart = at("restart", [P, TOK + 1], F32, W + 65 * KB + 288)
    act_tok = at("act_tok", [P, TT, N], F32, W)
    act_hi = at("act_hi", [P, N // P, TOK], F32R, W + 4 * KB)
    act_lo = at("act_lo", [P, N // P, TOK], F32R, W + 8 * KB)
    emb = at("emb", [P, TT, D], F32, W + 16 * KB)
    fin_w = at("fin_w", [P, D], F32, W + 32 * KB)
    gate_tok = at("gate_tok", [P, TT, N], F32, W + 40 * KB)
    p_tok = at("p_tok", [P, TT, 2 * P], F32, W + 48 * KB)
    C = W + 66 * KB + 512
    off = [C]

    def small(name, shape, dt=F32):
        size = 4
        for s in shape[1:]:
            size *= s
        t = at(name, shape, dt, off[0])
        off[0] += (size + 31) // 32 * 32
        return t

    ident = small("ident", [P, P])
    masks = small("masks", [P, NL - 1, P])
    vec_raw = small("vec_raw", [NVEC, P])
    vec = small("vec", [P, NVEC])
    square = small("square", [P, N])
    fg_raw = small("fg_raw", [P, KD, NH])
    fg_hi = small("fg_hi", [P, KD, NH], F32R)
    fg_lo = small("fg_lo", [P, KD, NH], F32R)
    ncum = small("ncum", [NH, TOK])
    fgz = at("fgz", [NH, TOK], F32, W + 49 * KB + 512)
    fge = at("fge", [NH, TOK], F32, W + 51 * KB)
    cum_i = small("cum_i", [P, TT, NH])
    bf_col = small("bf_col", [NH, 1])
    neg_max = small("neg_max", [P, 2])
    row_sum = small("row_sum", [P, 2])
    inv_sum = small("inv_sum", [P, 2])
    bn = small("bn", [P, TT, PO, 6])
    mv = small("mv", [P, TT, 2])
    ms = small("ms", [P, TT])
    minus_half = small("minus_half", [P, TT])
    rstd = [small(f"rstd{i}", [P, TT]) for i in range(4)]
    ssq = [small(f"ssq{i}", [P, TT, PO]) for i in range(3)]
    o_ssq = small("o_ssq", [P, GH, TT])
    o_ms = small("o_ms", [P, GH, TT])
    o_rstd = small("o_rstd", [P, GH, TT])
    iota_i = at("iota_i", [P, TOK], I32, W + 45 * KB + 512)
    iota_f = at("iota_f", [P, TOK], F32, W + 46 * KB + 512)
    assert base + off[0] <= 229344, off[0]

    emb_dram = nc.dram_tensor("emb_dram", (P, TT, D), F32, kind="Internal").ap()

    with ExitStack() as ctx:
        def sem(name):
            return ctx.enter_context(nc.semaphore(name))

        acc = [ctx.enter_context(nc.psum_tensor(f"acc{i}", [P, N], F32)) for i in range(4)]
        aux = [ctx.enter_context(nc.psum_tensor(f"aux{i}", [P, N], F32)) for i in range(4)]

        landed = [sem(f"landed{s}") for s in range(RING)]
        hi_done, lo_done = sem("hi_done"), sem("lo_done")
        unit_used = sem("unit_used")
        acc_read = [sem(f"acc_read{b}") for b in range(2)]
        aux_done = sem("aux_done")
        aux_read = [sem(f"aux_read{b}") for b in range(4)]
        x_in, x_back = [sem(f"x_in{c}") for c in range(UPP)], sem("x_back")
        vec_in, fg_in, pool_in = sem("vec_in"), sem("fg_in"), sem("pool_in")
        gb_in, lr_in, up_in, p_in, fin_in = (sem(n) for n in ("gb_in", "lr_in", "up_in", "p_in", "fin_in"))
        emb_out, emb_in = sem("emb_out"), sem("emb_in")
        up_clear = sem("up_clear")
        consts = sem("consts")
        zeros = sem("zeros")
        x_hi_done, hn_hi_done, o_hi_done, h1_hi_done = (sem(n) for n in ("x_hi_done", "hn_hi_done", "o_hi_done", "h1_hi_done"))
        act_hi_done, h2_hi_done, p_hi_done, fg_hi_done, lr_hi_done = (
            sem(n) for n in ("act_hi_done", "h2_hi_done", "p_hi_done", "fg_hi_done", "lr_hi_done"))
        fg_split, lr_split = sem("fg_split"), sem("lr_split")
        tanh_done = sem("tanh_done")
        fg_abs, fg_exp, fg_ln, fg_cum, fg_neg = (
            sem(n) for n in ("fg_abs", "fg_exp", "fg_ln", "fg_cum", "fg_neg"))
        max_done, exp_done, inv_done, probs_done, y_hi_done, y_done = (
            sem(n) for n in ("max_done", "exp_done", "inv_done", "probs_done", "y_hi_done", "y_done"))
        mixed = sem("mixed")
        z_done = sem("z_done")
        bn_done, var_done, ms_done, rstd_done = (sem(n) for n in ("bn_done", "var_done", "ms_done", "rstd_done"))
        centred, ln_dve, ln_pool = sem("centred"), sem("ln_dve"), sem("ln_pool")
        squared = sem("squared")
        gk_min, gk_exp, gk_ln, cum_done = (sem(n) for n in ("gk_min", "gk_exp", "gk_ln", "cum_done"))
        diff_done, decay_done, mul_dve, mul_pool = (sem(n) for n in ("diff_done", "decay_done", "mul_dve", "mul_pool"))
        o_ms_done, o_rstd_done = sem("o_ms_done"), sem("o_rstd_done")
        gated, h_added, scaled = sem("gated"), sem("h_added"), sem("scaled")
        scaled_act = sem("scaled_act")
        last_tile = sem("last_tile")
        weighted = sem("weighted")
        stored = sem("stored")
        dve_step = sem("dve_step")

        block = ctx.enter_context(nc.Block())

        def job(name, i=0):
            return JOB[(name, i)]

        def job_done(eng, name, i=0):
            eng.wait_ge(aux_done, job(name, i)[0] + 1)

        def job_read(eng, name, i=0):
            _, bank, turn = job(name, i)
            eng.wait_ge(aux_read[bank], turn + 1)

        def bank_of(name, i=0):
            return aux[job(name, i)[1]]

        def read_of(name, i=0):
            return aux_read[job(name, i)[1]]

        def norm_squares(i, n):
            return TT * (PO * i + n + (GH if i else 0))

        def head_squares(hd):
            return TT * (PO + hd)

        def panel_banks(p):
            return acc[2 * (p % 2)], acc[2 * (p % 2) + 1]

        def panel_done(eng, p, i=0, uper=0):
            eng.wait_ge(unit_used, i * uper + panel_end(p))

        def panel_read(eng, p, tiles=2, i=0, per=0):
            eng.wait_ge(acc_read[p % 2], i * per + (2 * (p // 2) + tiles))

        @block.sync
        def _(sp):
            def load(u, src, i=0, per=0):
                if u >= RING:
                    sp.wait_ge(lo_done, i * per + (u - RING + 1))
                    if per:
                        sp.nop(nofuse=True)
                sp.dma_start(w_raw[u % RING][:], src).then_inc(landed[u % RING], 16)

            def rows(w, r, col):
                return w[r:r + UNIT * P, col].rearrange("(c p) n -> p c n", p=P)

            def panel(w, u, col, i=0, per=0):
                for j in range(UPP):
                    load(u + j, rows(w, j * UNIT * P, col), i, per)

            xs = x[0].rearrange("(t p) d -> p t d", p=P)
            xw = UNIT * P
            for c in range(RING):
                sp.dma_start(x_tok[:, :, c * xw:(c + 1) * xw], xs[:, :, c * xw:(c + 1) * xw]).then_inc(x_in[c], 16)
                load(U_IN + c, rows(w_in[0], c * xw, slice(COLS1[0], COLS1[0] + N)))
            for c in range(RING, UPP):
                sp.dma_start(x_tok[:, :, c * xw:(c + 1) * xw], xs[:, :, c * xw:(c + 1) * xw]).then_inc(x_in[c], 16)
            for c in range(RING, UPP):
                load(U_IN + c, rows(w_in[0], c * xw, slice(COLS1[0], COLS1[0] + N)))
            for p, c in enumerate(COLS1[1:], 1):
                panel(w_in[0], U_IN + p * UPP, slice(c, c + N))
            with sp.Fori(0, PO) as n:
                panel(w_out[0], U_OUT, bass.ds(n * N, N), n, UPP)
            for n in range(PO):
                load(U_PP + n, rows(ple_w_proj[0], 0, slice(n * N, (n + 1) * N)))
            with sp.Fori(0, NPG) as n:
                panel(gla_w_in[0], U_G, bass.ds(n * N, N), n, UPP)
            with sp.Fori(0, PO) as n:
                panel(gla_w_out[0], U_GO, bass.ds(n * N, N), n, UPP)
            panel(ffn_w_in[0], U_F, slice(0, N))
            panel(ffn_w_in[0], U_F + UPP, slice(D_FF, D_FF + N))

            def out_rows(f, n, k):
                r = f * N + k * UNIT * P
                return ffn_w_out[0][bass.ds(r, UNIT * P), n * N:(n + 1) * N].rearrange("(c p) n -> p c n", p=P)

            with sp.Fori(0, NF - 1) as f:
                panel(ffn_w_in[0], U_FL, bass.ds(f * N + N, N), f, FU)
                panel(ffn_w_in[0], U_FL + UPP, bass.ds(f * N + (D_FF + N), N), f, FU)
                for n in range(PO):
                    for k in range(ROWS_F):
                        load(U_FL + 2 * UPP + n * ROWS_F + k, out_rows(f, n, k), f, FU)
            for n in range(PO):
                for k in range(ROWS_F):
                    load(U_FE + n * ROWS_F + k, out_rows(NF - 1, n, k))
            with sp.Fori(0, PO) as n:
                panel(ple_w_gate[0], U_PG, bass.ds(n * N, N), n, UPP)
            outs = out[0].rearrange("(t p) d -> p t d", p=P)
            stores = ((scaled, 1, 0, 3 * N, 4 * N), (scaled, 2, 0, 0, 3 * N), (scaled, 3, 1, 3 * N, 4 * N),
                      (scaled, 4, 1, 0, N), (scaled_act, 1, 1, N, 3 * N))
            for done, count, t, lo, hi in stores:
                sp.wait_ge(done, count)
                sp.dma_start(outs[:, t, lo:hi], h_tok[:, t, lo:hi]).then_inc(stored, 16)
            sp.wait_ge(stored, 16 * len(stores))

        @block.gpsimd
        def _(pool):
            nc.gpsimd.memset(ident[:], 0.0).then_inc(consts, 1)
            pool.wait_ge(consts, 1)
            nc.gpsimd.affine_select(ident[:], ident[:], [[-1, P]], ALU.not_equal, 1.0, base=0,
                                    channel_multiplier=1).then_inc(consts, 1)
            with nc.allow_non_contiguous_dma(reason="columns of eight"):
                pool.dma_start(fg_raw[:], w_in[0][:, FG0:FG0 + NH].rearrange("(c p) n -> p c n", p=P)).then_inc(fg_in, 16)
            for r, n, src in ((V_CONV, 12, conv_w[0].rearrange("k (b p) -> (k b) p", p=P)),
                              (V_PS, 4, pool_scale[0].rearrange("(b p) -> b p", p=P)),
                              (V_MIX, 16, mixer_norm[0].rearrange("(b p) -> b p", p=P)),
                              (V_ON, 4, gla_out_norm[0].rearrange("(b p) -> b p", p=P)),
                              (V_FFN, 16, ffn_norm[0].rearrange("(b p) -> b p", p=P)),
                              (V_PLE, 16, ple_norm[0].rearrange("(b p) -> b p", p=P))):
                pool.dma_start(vec_raw[r:r + n, :], src).then_inc(vec_in, 16)
            pool.dma_start(bf_col[:], b_f[0].rearrange("(h a) -> h a", a=1)).then_inc(vec_in, 16)
            pool.dma_start(pool_sb[:], pool_w[0].rearrange("g c d -> c g d")).then_inc(pool_in, 16)
            nc.gpsimd.memset(sel[:], 0.0).then_inc(consts, 1)
            pool.wait_ge(consts, 3)
            nc.gpsimd.affine_select(sel[:], sel[:], [[-1, NH], [0, P]], ALU.not_equal, 1.0, base=0,
                                    channel_multiplier=1).then_inc(consts, 1)
            nc.gpsimd.memset(causal[:], 0.0).then_inc(consts, 1)
            pool.wait_ge(consts, 5)
            for c in (0, 2 * P):
                nc.gpsimd.affine_select(causal[:, c:c + P], causal[:, c:c + P], [[-1, P]], ALU.is_ge, -3.0e38,
                                        base=0, channel_multiplier=1).then_inc(consts, 1)
            nc.gpsimd.iota(iota_i[:], [[1, TOK]], base=1, channel_multiplier=0).then_inc(consts, 1)
            pool.wait_ge(consts, 8)
            nc.gpsimd.tensor_copy(iota_f[:], iota_i[:]).then_inc(consts, 1)
            nc.gpsimd.memset(minus_half[:], -0.5).then_inc(consts, 1)
            nc.gpsimd.memset(masks[:], 1.0).then_inc(consts, 1)
            pool.wait_ge(consts, 11)
            k = 11
            for li, h in enumerate(LEVELS[:-1]):
                nb = P // (2 * h)
                for way in range(2):
                    m = halves(masks[:, li, :], h)[:, :, 1 - way, :]
                    lo = h * way
                    nc.gpsimd.affine_select(m, m, [[-2 * h, nb], [0, h]], ALU.is_ge, 0.0, base=-lo,
                                            channel_multiplier=1).then_inc(consts, 1)
                    k += 1
                    pool.wait_ge(consts, k)
                    nc.gpsimd.affine_select(m, m, [[2 * h, nb], [0, h]], ALU.is_ge, 0.0, base=lo + h - 1,
                                            channel_multiplier=-1).then_inc(consts, 1)
                    k += 1
                    pool.wait_ge(consts, k)

            job_done(pool, "s", NH - 1)
            pool.dma_start(h_tok[:], x[0].rearrange("(t p) d -> p t d", p=P)).then_inc(x_back, 16)
            pool.wait_ge(y_done, NH + 2)
            pool.dma_start(p_tok[:], p_2[0, 0].rearrange("(t p) d -> p t d", p=P)).then_inc(p_in, 16)
            pool.dma_start(ln_gb[:, 0, :], ln_g[0].partition_broadcast(P)).then_inc(gb_in, 16)
            pool.dma_start(ln_gb[:, 1, :], ln_b[0].partition_broadcast(P)).then_inc(gb_in, 16)
            pool.dma_start(lr_raw[:], gla_w_in[0][:, LR0:LR0 + 2 * RANK].rearrange("(c p) n -> p c n", p=P)).then_inc(lr_in, 16)
            pool.wait_ge(ms_done, 1)
            nc.gpsimd.tensor_tensor(rstd[0][:], ms[:], minus_half[:], ALU.pow).then_inc(rstd_done, 1)
            pool.wait_ge(gb_in, 32)
            for n in range(1, PO):
                pool.wait_ge(centred, 2 * (n + 1))
                s = slice(n * N, (n + 1) * N)
                nc.gpsimd.tensor_tensor(h_tok[:, 1, s], h_tok[:, 1, s], ln_gb[:, 0, s], ALU.mult).then_inc(ln_pool, 1)
                pool.wait_ge(ln_pool, 2 * n - 1)
                nc.gpsimd.tensor_tensor(h_tok[:, 1, s], h_tok[:, 1, s], ln_gb[:, 1, s], ALU.add).then_inc(ln_pool, 1)
            pool.wait_ge(unit_used, U_PP)
            nc.gpsimd.memset(gate_up[:], 0.0).then_inc(up_clear, 1)
            pool.wait_ge(up_clear, 1)
            for z in range(2):
                pool.dma_start(gate_up[z * RANK:(z + 1) * RANK, z, :], gla_w_gate_up[0, z]).then_inc(up_in, 16)
                pool.dma_start(gate_up[2 * RANK:2 * RANK + 1, z, :], gla_b_gate[0, z:z + 1, :]).then_inc(up_in, 16)
            panel_read(pool, P_PP + 2)
            panel_read(pool, P_PP + 3)
            pool.dma_start(emb_dram, emb[:]).then_inc(emb_out, 16)
            pool.wait_ge(ms_done, 2)
            nc.gpsimd.tensor_tensor(rstd[1][:], ms[:], minus_half[:], ALU.pow).then_inc(rstd_done, 1)
            for s in range(NL):
                pool.wait_ge(decay_done, 2 * s + 1)
                if s == 0:
                    for i in range(4, 8):
                        job_read(pool, "gt", i)
                d = decayed[2 * (s % 2)]
                nc.gpsimd.tensor_tensor(d[:], d[:], gkT[:], ALU.mult).then_inc(mul_pool, 1)
            for hd in range(GH):
                pool.wait_ge(o_ms_done, hd + 1)
                nc.gpsimd.tensor_tensor(o_rstd[:, hd, :], o_ms[:, hd, :], minus_half[:], ALU.pow).then_inc(o_rstd_done, 1)
            job_done(pool, "av", 2 * GH - 1)
            pool.wait_ge(emb_out, 16)
            pool.dma_start(emb[:], emb_dram).then_inc(emb_in, 16)
            pool.wait_ge(unit_used, U_GO + UPP)
            pool.dma_start(fin_w[:], final_norm.partition_broadcast(P)).then_inc(fin_in, 16)
            pool.wait_ge(fin_in, 16)
            for i in (2, 3):
                pool.wait_ge(ms_done, i + 1)
                nc.gpsimd.tensor_tensor(rstd[i][:], ms[:], minus_half[:], ALU.pow).then_inc(rstd_done, 1)
            for n in range(PO - 1):
                for t in range(TT):
                    pool.wait_ge(squared, norm_squares(3, n + 1))
                    s = slice(n * N, (n + 1) * N)
                    nc.gpsimd.tensor_tensor(h_tok[:, t, s], h_tok[:, t, s], fin_w[:, s], ALU.mult).then_inc(weighted, 1)
            for t in range(TT):
                pool.wait_ge(ms_done, 5 + t)
                nc.gpsimd.tensor_tensor(rstd[0][:, t:t + 1], ms[:, t:t + 1], minus_half[:, t:t + 1],
                                        ALU.pow).then_inc(rstd_done, 1)

        @block.tensor
        def _(pe):
            def unit(u, p, hi, lo, k, first, last, i=0, per=0, pper=0):
                pe.wait_ge(lo_done, i * per + (u + 1))
                if first and p >= 2:
                    panel_read(pe, p - 2, 2, i, pper)
                banks = panel_banks(p)
                for c in range(UNIT):
                    for t in range(TT):
                        tok = slice(t * P, (t + 1) * P)
                        st, en = first and c == 0, last and c == UNIT - 1
                        wh, wl = w_hi[u % RING][:, c, :], w_lo[u % RING][:, c, :]
                        pe.matmul(banks[t][:], hi[:, k + c, tok], wh, start=st, stop=False)
                        pe.matmul(banks[t][:], hi[:, k + c, tok], wl, start=False, stop=False)
                        mm = pe.matmul(banks[t][:], lo[:, k + c, tok], wh, start=False, stop=en)
                mm.then_inc(unit_used, 1)

            def begin(name, i=0):
                _, bank, turn = job(name, i)
                if turn:
                    pe.wait_ge(aux_read[bank], turn)
                return aux[bank]

            def turn_tiles(src, b, cols):
                for k in range(2):
                    for t in range(TT):
                        mm = pe.transpose(b[:, (k * TT + t) * P:(k * TT + t + 1) * P],
                                          src[:, t, cols + k * P:cols + (k + 1) * P], ident[:])
                return mm

            def turn_x(c):
                pe.wait_ge(x_in[c], 16)
                b = begin("x", c)
                turn_tiles(x_tok, b, 2 * c * P).then_inc(aux_done, 1)

            def turn_stage(p):
                panel_read(pe, P_IN + p)
                for i in range(2):
                    b = begin("t", 2 * p + i)
                    turn_tiles(stage[p % 2], b, 2 * i * P).then_inc(aux_done, 1)

            def thin(name, hi, lo, n):
                o = begin(name)[0:n, 0:TOK]
                for k in range(KD):
                    pe.matmul(o, hi[:, k, :], a_hi[:, k, :], start=k == 0, stop=False)
                    pe.matmul(o, lo[:, k, :], a_hi[:, k, :], start=False, stop=False)
                    mm = pe.matmul(o, hi[:, k, :], a_lo[:, k, :], start=False, stop=k == KD - 1)
                mm.then_inc(aux_done, 1)

            def scores(h):
                if h == 0:
                    pe.wait_ge(fg_neg, 1)
                b = begin("s", h)
                for c, n, q in ((0, P, 0), (P, TOK, P)):
                    o = b[:, c:c + n]
                    pe.matmul(o, qT[:, h, q:q + P], kT[:, h, 0:n], start=True, stop=False)
                    mm = pe.matmul(o, sel[:, h, :], ncum[:, 0:n], start=False, stop=True)
                mm.then_inc(aux_done, 1)

            def turn_probs(h):
                b = begin("pt_", h)
                pe.wait_ge(probs_done, 2 * (h + 1))
                for c in range(3):
                    mm = pe.transpose(b[:, c * P:(c + 1) * P], probs[:, c * P:(c + 1) * P], ident[:])
                mm.then_inc(aux_done, 1)

            def weigh_values(h):
                job_read(pe, "pt_", h)
                b = begin("ot", h)
                f = slice(h * P, (h + 1) * P)
                pe.matmul(b[:, 0:TOK], v_tok[:, 0, f], probsT[:, 0:TOK], start=True, stop=False)
                pe.matmul(b[:, P:TOK], v_tok[:, 1, f], probsT[:, TOK:3 * P], start=False,
                          stop=True).then_inc(aux_done, 1)

            pe.wait_ge(consts, 2)
            for c in range(2):
                turn_x(c)
            for p in range(NP1):
                for j in range(UPP):
                    u = U_IN + p * UPP + j
                    if p == 0:
                        job_read(pe, "x", j)
                    unit(u, P_IN + p, a_hi, a_lo, 2 * j, j == 0, j == UPP - 1)
                    if p == 0 and j < UPP - 2:
                        turn_x(2 + j)
                    if (p, j) == (0, UPP - 1):
                        pe.wait_ge(vec_in, 7 * 16)
                        b = begin("vec")
                        pe.transpose(b[:, 0:NVEC], vec_raw[:], ident[0:NVEC, 0:NVEC]).then_inc(aux_done, 1)
                    if (p, j) == (1, 0):
                        pe.wait_ge(fg_split, 1)
                        thin("fg", fg_hi, fg_lo, NH)
                    if j == 1 and p >= 1 and p - 1 not in (PV, PV + 1):
                        turn_stage(p - 1)
                    if (p, j) == (1, 6):
                        pe.wait_ge(fg_cum, 1)
                        b = begin("ci")
                        for t in range(TT):
                            mm = pe.transpose(b[:, t * NH:(t + 1) * NH], fgz[:, t * P:(t + 1) * P], ident[0:NH, 0:NH])
                        mm.then_inc(aux_done, 1)
                    if (p, j) == (13, 3):
                        pe.wait_ge(z_done, 1)
                        pe.wait_ge(pool_in, 16)
                        for i in range(2):
                            b = begin("pool", i)
                            for k in range(2):
                                mm = pe.matmul(b[:, k * TOK:(k + 1) * TOK], pool_sb[:, 2 * i + k, :],
                                               poolz[:, 2 * i + k, :], start=True, stop=True)
                            mm.then_inc(aux_done, 1)
                    for name, h in head_jobs(u):
                        {"s": scores, "pt_": turn_probs, "ot": weigh_values}[name](h)

            def out_panel(n, j, i=0, per=0, pper=0):
                unit(U_OUT + n * UPP + j, P_OUT + n, y_hi, y_lo, 2 * j, j == 0, j == UPP - 1, i, per, pper)

            for j in range(UPP):
                pe.wait_ge(y_done, NH if j < 4 else NH + 1 if j < 6 else NH + 2)
                out_panel(0, j)
                if j == 1:
                    turn_stage(PPG)
                if j == UPP - 1:
                    pe.wait_ge(p_in, 16)
                    b = begin("pt")
                    turn_tiles(p_tok, b, 0).then_inc(aux_done, 1)
            for n in range(1, PO):
                for j in range(UPP):
                    out_panel(n, j)

            def turn_hn(c):
                n = c // 2
                pe.wait_ge(ln_dve, 4 + 2 * n)
                if n:
                    pe.wait_ge(ln_pool, 2 * n)
                b = begin("hn", c)
                turn_tiles(h_tok, b, 2 * c * P).then_inc(aux_done, 1)

            def diagonal(i):
                b = begin("dg", i)
                for c in range(4):
                    hd, t = 2 * i + c // 2, c % 2
                    tok = slice(t * P, (t + 1) * P)
                    for kb in range(2):
                        mm = pe.matmul(b[:, c * P:(c + 1) * P], gkT[:, 2 * hd + kb, tok], gqT[:, 2 * hd + kb, tok],
                                       start=kb == 0, stop=kb == 1)
                mm.then_inc(aux_done, 1)

            def step(n):
                s, pair, h = n // 2, n % 2, LEVELS[n // 2]
                pe.wait_ge(mul_dve, s + 1)
                pe.wait_ge(mul_pool, s + 1)
                b = begin("step", n)
                keys, queries = decayed[2 * (s % 2)], decayed[2 * (s % 2) + 1]
                for c in range(2 * TT):
                    hd, t = 2 * pair + c // TT, c % TT
                    q = 1 - t if h == P else t
                    for kb in range(2):
                        mm = pe.matmul(b[:, c * P:(c + 1) * P], keys[:, 2 * hd + kb, t * P:(t + 1) * P],
                                       queries[:, 2 * hd + kb, q * P:(q + 1) * P], start=kb == 0, stop=kb == 1)
                mm.then_inc(aux_done, 1)

            def apply_values(hd):
                f = slice(hd * GDV, (hd + 1) * GDV)
                if hd == 0:
                    job_read(pe, "step", 2 * NL - 2)
                    job_read(pe, "step", 2 * NL - 1)
                    panel_read(pe, P_G + 7)
                for t in range(TT):
                    b = begin("av", 2 * hd + t)
                    pe.matmul(b[:], at_diag[:, hd, t, :], gv[:, t, f], start=True, stop=False)
                    pe.matmul(b[:], at_off[:, hd, 1 - t, :], gv[:, 1 - t, f], start=False,
                              stop=True).then_inc(aux_done, 1)

            def turn_o(hd):
                for t in range(TT):
                    job_read(pe, "av", 2 * hd + t)
                for i in range(2):
                    b = begin("o", 2 * hd + i)
                    turn_tiles(og[hd], b, 2 * i * P).then_inc(aux_done, 1)

            job_read(pe, "pt")
            for n in range(PO):
                if n == PO - 1:
                    turn_hn(0)
                    turn_hn(1)
                unit(U_PP + n, P_PP + n, a_hi, a_lo, P_CHUNK, True, True)
            for g in range(NPG * UPP):
                p, j = g // UPP, g % UPP
                if p == 0:
                    job_read(pe, "hn", j)
                unit(U_G + g, P_G + p, a_hi, a_lo, 2 * j, j == 0, j == UPP - 1)
                if g < UPP - 2:
                    turn_hn(2 + g)
                for name, i in gla_jobs(g):
                    if name == "lr":
                        pe.wait_ge(lr_split, 1)
                        thin("lr", lr_hi, lr_lo, 2 * RANK)
                    if name == "gt":
                        if i % 2 == 0:
                            panel_read(pe, P_G + i // 2)
                        b = begin("gt", i)
                        turn_tiles(og[(i // 2) % 2], b, 2 * (i % 2) * P).then_inc(aux_done, 1)
                    if name == "lr_tok":
                        job_read(pe, "lr")
                        b = begin("lr_tok")
                        for t in range(TT):
                            mm = pe.transpose(b[:, t * 2 * RANK:(t + 1) * 2 * RANK], lrT[0:2 * RANK, t * P:(t + 1) * P],
                                              ident[0:2 * RANK, 0:2 * RANK])
                        mm.then_inc(aux_done, 1)
                    if name == "lrt":
                        job_read(pe, "lr_tok")
                        b = begin("lrt")
                        for t in range(TT):
                            mm = pe.transpose(b[0:2 * RANK + 1, t * P:(t + 1) * P], lrt[:, t, :], ident[:])
                        mm.then_inc(aux_done, 1)
                    if name == "gk":
                        if i == 0:
                            job_read(pe, "lrt")
                            pe.wait_ge(up_in, 64)
                        b = begin("gk", i)
                        for k in range(2):
                            blk = 2 * (i % 4) + k
                            mm = pe.matmul(b[:, k * TOK:(k + 1) * TOK], gate_up[:, i // 4, blk * P:(blk + 1) * P],
                                           lrT[:], start=True, stop=True)
                        mm.then_inc(aux_done, 1)
                    if name == "dg":
                        if i == 0:
                            job_read(pe, "gt", 6)
                            job_read(pe, "gt", 7)
                        diagonal(i)
                    if name == "step":
                        step(i)
                    if name == "av" and i % 2 == 0:
                        apply_values(i // 2)
                    if name == "o" and i % 2 == 0:
                        turn_o(i // 2)

            def turn_h(name, i):
                b = begin(name, i)
                turn_tiles(h_tok, b, i * 2 * P).then_inc(aux_done, 1)

            for n in range(PO):
                for j in range(UPP):
                    if n == 0 and j == 0:
                        for i in range(6):
                            job_read(pe, "o", i)
                    if n == 0 and j == 6:
                        job_read(pe, "o", 6)
                        job_read(pe, "o", 7)
                    unit(U_GO + n * UPP + j, P_GO + n, y_hi, y_lo, 2 * j, j == 0, j == UPP - 1)
                    if n == 0 and j == 1:
                        turn_o(3)
                    if n >= 1 and j == 1:
                        panel_read(pe, P_GO + n - 1)
                        turn_h("h1", 2 * n - 2)
                        turn_h("h1", 2 * n - 1)

            for j in range(UPP):
                job_read(pe, "h1", j)
                unit(U_F + j, P_F, a_hi, a_lo, 2 * j, j == 0, j == UPP - 1)
                if j == 1:
                    panel_read(pe, P_GO + 3)
                    turn_h("h1", 6)
                    turn_h("h1", 7)
            for j in range(UPP):
                unit(U_F + UPP + j, P_F + 1, a_hi, a_lo, 2 * j, j == 0, j == UPP - 1)

            def turn_act(f):
                for k in range(2):
                    n, bank, turn = job("a", k)
                    pe.wait_ge(aux_read[bank], f + turn)
                    turn_tiles(act_tok, aux[bank], 2 * k * P).then_inc(aux_done, 1)

            def hidden_rows(u, p, hi, lo, n, i=0, per=0, pper=0):
                for k in range(ROWS_F):
                    unit(u + n * ROWS_F + k, p + n, hi, lo, 2 * k, k == 0, k == ROWS_F - 1, i, per, pper)

            def ffn_step(f, last=False):
                for m in range(2):
                    for j in range(UPP):
                        unit(U_FL + m * UPP + j, P_FL + m, a_hi, a_lo, 2 * j, j == 0, j == UPP - 1, f, FU, FP)
                        if (m, j) == (0, 2):
                            panel_read(pe, P_F + 1, 2, f, FP)
                            turn_act(f)
                for k in range(2):
                    n, bank, turn = job("a", k)
                    pe.wait_ge(aux_read[bank], f + (turn + 1))
                for n in range(PO):
                    hidden_rows(U_FL + 2 * UPP, P_FL + 2, act_hi, act_lo, n, f, FU, FP)
                    if last and n == 1:
                        panel_read(pe, P_FL + 1, 2, f, FP)
                        turn_act(f + 1)

            with pe.Fori(0, NF - 2) as f:
                ffn_step(f)
            ffn_step(NF - 2, last=True)
            for k in range(2):
                job_read(pe, "a", 2 * (NF - 1) + k)
            for n in range(PO):
                hidden_rows(U_FE, P_FE, y_hi, y_lo, n)
                if n >= 1:
                    panel_read(pe, P_FE + n - 1)
                    turn_h("h2", 2 * n - 2)
                    turn_h("h2", 2 * n - 1)
            for n in range(PO):
                for j in range(UPP):
                    if n == 0:
                        job_read(pe, "h2", j)
                    if n == PO - 1 and j >= UPP - RING:
                        continue
                    unit(U_PG + n * UPP + j, P_PG + n, a_hi, a_lo, 2 * j, j == 0, j == UPP - 1)
                    if (n, j) == (0, 1):
                        panel_read(pe, P_FE + 3)
                        turn_h("h2", 6)
                        turn_h("h2", 7)

            banks = panel_banks(P_PG + PO - 1)
            for t in range(TT):
                tok = slice(t * P, (t + 1) * P)
                for j in range(UPP - RING, UPP):
                    u = U_PG + (PO - 1) * UPP + j
                    pe.wait_ge(lo_done, u + 1)
                    for c in range(UNIT):
                        k = 2 * j + c
                        wh, wl = w_hi[u % RING][:, c, :], w_lo[u % RING][:, c, :]
                        pe.matmul(banks[t][:], a_hi[:, k, tok], wh, start=False, stop=False)
                        pe.matmul(banks[t][:], a_hi[:, k, tok], wl, start=False, stop=False)
                        mm = pe.matmul(banks[t][:], a_lo[:, k, tok], wh, start=False, stop=k == KD - 1)
                mm.then_inc(last_tile, 1)

        @block.scalar
        def _(act):
            def high(u, i=0, per=0):
                turns = per // RING
                act.wait_ge(landed[u % RING], (16 * turns) * i + 16 * (u // RING + 1))
                if u >= RING:
                    act.wait_ge(unit_used, i * per + (u - RING + 1))
                nc.scalar.copy(w_hi[u % RING][:], w_raw[u % RING][:]).then_inc(hi_done, 1)

            def stage_panel(p, dst, scale=None, func=ACT.Copy, i=0, uper=0):
                panel_done(act, p, i, uper)
                for t, b in enumerate(panel_banks(p)):
                    s = 1.0 if scale is None else scale[:, t:t + 1]
                    nc.scalar.activation(dst[:, t, :], b[:], func, scale=s).then_inc(acc_read[p % 2], 1)

            def split_high(name, i, dst, c, done, col=None):
                job_done(act, name, i)
                b = bank_of(name, i)
                if col is None:
                    nc.scalar.copy(dst[:, c:c + 2, :], b[:].rearrange("p (k t) -> p k t", t=TOK)).then_inc(done, 1)
                    return
                for k in range(2):
                    nc.scalar.activation(dst[:, c + k, :], b[:, k * TOK:(k + 1) * TOK], ACT.Copy,
                                         scale=vec[:, col + k:col + k + 1]).then_inc(done, 1)

            def sum_of_squares(src, dst, count):
                if count > 1:
                    act.wait_ge(squared, count - 1)
                nc.scalar.activation(square[:], src, ACT.Square, accum_out=dst).then_inc(squared, 1)

            for c in range(UPP):
                split_high("x", c, a_hi, 2 * c, x_hi_done)
                if c < RING:
                    high(c)
                if c == 4:
                    act.wait_ge(fg_in, 16)
                    nc.scalar.copy(fg_hi[:], fg_raw[:]).then_inc(fg_hi_done, 1)
                if c >= 4:
                    high(c)
            tanhs = [0]

            def gate_tanh(i):
                job_done(act, "t", i)
                if tanhs[0] >= 2:
                    job_read(act, "t", last_gate[tanhs[0] - 2])
                nc.scalar.activation(tanh[i % 2][:].rearrange("p k t -> p (k t)"), bank_of("t", i)[:], ACT.Tanh,
                                     scale=0.5).then_inc(tanh_done, 1)
                tanhs[0] += 1

            last_gate = [2 * p + k for p in (PGA, PGA + 1, PCG, PPG) for k in range(2)]

            for p in range(NP1):
                for j in range(UPP):
                    u = U_IN + p * UPP + j
                    if u >= 4:
                        high(u + RING)
                    if j == 1 and p >= 1:
                        q = p - 1
                        for i in (2 * q, 2 * q + 1):
                            src = bank_of("t", i)[:].rearrange("p (k t) -> p k t", t=TOK) if ("t", i) in JOB else None
                            if q in (PQ, PQ + 1):
                                job_done(act, "t", i)
                                nc.scalar.activation(qT[:, 2 * i:2 * i + 2, :], src, ACT.Copy,
                                                     scale=float(P) ** -0.5).then_inc(read_of("t", i), 1)
                            if q == PCC:
                                job_done(act, "t", i)
                                k = 2 * (i % 2)
                                act.wait_ge(zeros, 2)
                                nc.scalar.copy(convu[:, k:k + 2, 2:], src).then_inc(read_of("t", i), 1)
                            if q == PPU:
                                job_done(act, "t", i)
                                k = 2 * (i % 2)
                                act.wait_ge(zeros, 1)
                                nc.scalar.copy(poolu[:, k:k + 2, PAD:], src).then_inc(read_of("t", i), 1)
                            if q in (PGA, PGA + 1, PCG):
                                gate_tanh(i)
                    if (p, j) == (1, 3):
                        job_read(act, "fg")
                        nc.scalar.activation(fge[:], fgz[:], ACT.Abs).then_inc(fg_abs, 1)
                        act.wait_ge(fg_abs, 1)
                        nc.scalar.activation(fge[:], fge[:], ACT.Exp, scale=-1.0).then_inc(fg_exp, 1)
                        act.wait_ge(fg_exp, 1)
                        nc.scalar.activation(fge[:], fge[:], ACT.Ln, bias=1.0).then_inc(fg_ln, 1)
                    if (p, j) == (1, 6):
                        job_done(act, "ci")
                        nc.scalar.copy(cum_i[:].rearrange("p t n -> p (t n)"), bank_of("ci")[:, 0:TT * NH]).then_inc(read_of("ci"), 1)
                    for h in range(NH):
                        if u == HEAD0 + HEAD_STEP * h:
                            act.wait_ge(max_done, h + 1)
                            if h:
                                job_done(act, "pt_", h - 1)
                            for t, c in ((0, slice(0, P)), (1, slice(P, 3 * P))):
                                nc.scalar.activation(probs[:, c], logits[:, c], ACT.Exp, bias=neg_max[:, t:t + 1],
                                                     accum_out=row_sum[:, t:t + 1]).then_inc(exp_done, 1)
                        if u == HEAD0 + HEAD_STEP * h + TURN_LAG:
                            job_done(act, "pt_", h)
                            if h:
                                job_done(act, "ot", h - 1)
                            nc.scalar.copy(probsT[:], bank_of("pt_", h)[:, 0:3 * P]).then_inc(read_of("pt_", h), 1)
                        if u == HEAD0 + HEAD_STEP * h + VALUE_LAG:
                            job_read(act, "ot", h)
                            nc.scalar.activation(y_hi[:, h, :], y_head[:], ACT.Copy, scale=0.5).then_inc(y_hi_done, 1)
                    if (p, j) == (13, 4):
                        act.wait_ge(mixed, 1)
                        nc.scalar.activation(y_hi[:, 8:12, :], convy[:], ACT.Copy, scale=0.5).then_inc(y_hi_done, 1)
                    if j == UPP - 1:
                        if p >= 2 and ("t", 2 * (p - 2)) in JOB and p not in (PV, PV + 1):
                            job_done(act, "t", 2 * (p - 2) + 1)
                        dst = v_tok[:, :, (p - PV) * N:(p - PV + 1) * N] if p in (PV, PV + 1) else stage[p % 2]
                        stage_panel(P_IN + p, dst)

            for j in range(UPP):
                high(U_OUT + j + RING)
                if j == 1:
                    gate_tanh(2 * PPG)
                    gate_tanh(2 * PPG + 1)
                    job_read(act, "pool", 1)
                    nc.scalar.activation(y_hi[:, 12:16, :], poolz[:], ACT.Copy, scale=0.5).then_inc(y_hi_done, 1)
                if j == UPP - 1:
                    split_high("pt", 0, a_hi, P_CHUNK, p_hi_done)
            with act.Fori(0, PO - 1) as n:
                for j in range(UPP):
                    high(U_OUT + UPP + j + RING, n, UPP)
            for n in range(PO):
                high(U_PP + n + RING)
                stage_panel(P_PP + n, emb[:, :, n * N:(n + 1) * N])
                if n == PO - 2:
                    for c in range(2):
                        split_high("hn", c, a_hi, 2 * c, hn_hi_done, V_MIX + 2 * c)
            def squares(i, n):
                for t in range(TT):
                    sum_of_squares(h_tok[:, t, n * N:(n + 1) * N], ssq[i % 3][:, t, n:n + 1],
                                   norm_squares(i, n) + t + 1)

            for c in range(2, UPP):
                split_high("hn", c, a_hi, 2 * c, hn_hi_done, V_MIX + 2 * c)
                if c >= 4:
                    high(U_G + c)
                if c in (3, 5, 7):
                    squares(0, (c - 3) // 2)

            def exp_step(n):
                act.wait_ge(diff_done, 2 * (n + 1))
                d = decayed[n % 4][:].rearrange("p d t -> p (d t)")
                nc.scalar.activation(d, d, ACT.Exp, scale=1.0 / 16.0).then_inc(decay_done, 1)

            for g in range(NPG * UPP):
                p, j = g // UPP, g % UPP
                if g >= 4:
                    high(U_G + g + RING)
                if g == 4:
                    squares(0, PO - 1)
                if g == 5:
                    act.wait_ge(lr_in, 16)
                    nc.scalar.copy(lr_hi[:], lr_raw[:]).then_inc(lr_hi_done, 1)
                if g == 8:
                    job_done(act, "lr")
                    nc.scalar.copy(lrT[0:2 * RANK, :], bank_of("lr")[0:2 * RANK, 0:TOK]).then_inc(read_of("lr"), 1)
                if g == 10:
                    job_done(act, "lr_tok")
                    for t in range(TT):
                        last = nc.scalar.activation(lrt[:, t, 0:2 * RANK],
                                                    bank_of("lr_tok")[:, t * 2 * RANK:(t + 1) * 2 * RANK],
                                                    ACT.Copy, scale=rstd[1][:, t:t + 1])
                    last.then_inc(read_of("lr_tok"), 1)
                if g == 12:
                    job_done(act, "lrt")
                    nc.scalar.copy(lrT[:], bank_of("lrt")[0:2 * RANK + 1, 0:TOK]).then_inc(read_of("lrt"), 1)
                if g in (9, 17, 25, 33):
                    q = (g - 9) // 8
                    for i in (2 * q, 2 * q + 1):
                        job_done(act, "gt", i)
                        src = bank_of("gt", i)[:].rearrange("p (k t) -> p k t", t=TOK)
                        dst, k = (gqT, 2 * i) if q < 2 else (gkT, 2 * (i - 4))
                        nc.scalar.activation(dst[:, k:k + 2, :], src, ACT.Copy,
                                             scale=1.0 / 16.0 if q < 2 else 1.0).then_inc(read_of("gt", i), 1)
                for name, i in gla_jobs(g):
                    if name == "gk":
                        act.wait_ge(gk_min, i + 1)
                        e = gate_tmp[i // 4][:, 2 * (i % 4):2 * (i % 4) + 2, :].rearrange("p k t -> p (k t)")
                        nc.scalar.activation(e, bank_of("gk", i)[:], ACT.Abs).then_inc(read_of("gk", i), 1)
                        act.wait_ge(read_of("gk", i), job("gk", i)[2] + 1)
                        nc.scalar.activation(e, e, ACT.Exp, scale=-1.0).then_inc(gk_exp, 1)
                for way in range(2):
                    if g == LN_G[way]:
                        act.wait_ge(gk_exp, 4 * (way + 1))
                        e = gate_tmp[way][:].rearrange("p k t -> p (k t)")
                        nc.scalar.activation(e, e, ACT.Ln, bias=1.0).then_inc(gk_ln, 1)
                for s in range(NL):
                    for part in range(2):
                        if g == STEP0 + STEP_GAP * s - 5 + 2 * part:
                            exp_step(2 * s + part)
                for hd in range(GH):
                    if g == AV0 + 3 * hd:
                        for t in range(TT):
                            job_done(act, "av", 2 * hd + t)
                            sum_of_squares(bank_of("av", 2 * hd + t)[:], o_ssq[:, hd, t:t + 1],
                                           head_squares(hd) + t + 1)
                    if hd < 3 and g == AV0 + 3 * hd + 3:
                        for i in (2 * hd, 2 * hd + 1):
                            split_high("o", i, y_hi, 2 * i, o_hi_done, V_ON + 2 * (i % 2))
                if j == UPP - 1:
                    if p < 4:
                        act.wait_ge(rstd_done, 2)
                        stage_panel(P_G + p, og[p % 2], rstd[1])
                    elif p < 8:
                        act.wait_ge(emb_out, 16)
                        stage_panel(P_G + p, gv[:, :, (p - 4) * N:(p - 3) * N], rstd[1])
                    else:
                        if p >= 10:
                            act.wait_ge(diff_done, 4 * NL)
                        stage_panel(P_G + p, og[p - 8], rstd[1], ACT.Silu)

            def split_h(name, n, col):
                for i in (2 * n, 2 * n + 1):
                    split_high(name, i, a_hi, 2 * i, h1_hi_done if name == "h1" else h2_hi_done, col + 2 * i)

            for n in range(PO):
                for j in range(UPP):
                    high(U_GO + n * UPP + j + RING)
                    if n == 0 and j == 1:
                        for i in (6, 7):
                            split_high("o", i, y_hi, 2 * i, o_hi_done, V_ON + 2 * (i % 2))
                    if n >= 1 and j == 1:
                        split_h("h1", n - 1, V_FFN)
                        squares(1, n - 1)
            for m in range(2):
                for j in range(UPP):
                    high(U_F + m * UPP + j + RING)
                    if m == 0 and j == 1:
                        split_h("h1", PO - 1, V_FFN)
                        squares(1, PO - 1)
                    if m == 0 and j == UPP - 1:
                        act.wait_ge(rstd_done, 3)
                        stage_panel(P_F, act_tok, rstd[2], ACT.Silu)

            def split_act(f, dst):
                for k in range(2):
                    n, bank, _ = job("a", k)
                    act.wait_ge(aux_done, 2 * f + (n + 1))
                    nc.scalar.copy(dst[:, 2 * k:2 * k + 2, :],
                                   aux[bank][:].rearrange("p (k t) -> p k t", t=TOK)).then_inc(act_hi_done, 1)

            def ffn_step(f, last=False):
                for j in range(FU):
                    high(U_FL + j + RING, f, FU)
                    if j == 2:
                        split_act(f, act_hi)
                    if j == UPP - 1:
                        stage_panel(P_FL, act_tok, rstd[2], ACT.Silu, f, FU)
                    if last and j == 2 * UPP + 2 * ROWS_F - 1:
                        split_act(f + 1, y_hi)

            with act.Fori(0, NF - 2) as f:
                ffn_step(f)
            ffn_step(NF - 2, last=True)
            for n in range(PO):
                for k in range(ROWS_F):
                    high(U_FE + n * ROWS_F + k + RING)
                if n >= 1:
                    split_h("h2", n - 1, V_PLE)
                    squares(2, n - 1)
            for n in range(PO):
                for j in range(UPP):
                    if U_PG + n * UPP + j + RING < U_END:
                        high(U_PG + n * UPP + j + RING)
                    if (n, j) == (0, 1):
                        split_h("h2", PO - 1, V_PLE)
                        squares(2, PO - 1)
                    if n >= 1 and j == 2:
                        act.wait_ge(h_added, TT * n)
                        squares(3, n - 1)
                if n == 0:
                    act.wait_ge(rstd_done, 4)
                if n < PO - 1:
                    stage_panel(P_PG + n, gate_tok, rstd[3], ACT.Sigmoid)
            p, n = P_PG + PO - 1, PO - 1
            for t in range(TT):
                act.wait_ge(last_tile, t + 1)
                nc.scalar.activation(gate_tok[:, t, :], panel_banks(p)[t][:], ACT.Sigmoid,
                                     scale=rstd[3][:, t:t + 1]).then_inc(acc_read[p % 2], 1)
                act.wait_ge(h_added, TT * n + t + 1)
                sum_of_squares(h_tok[:, t, n * N:(n + 1) * N], ssq[0][:, t, n:n + 1], norm_squares(3, n) + t + 1)
            act.wait_ge(rstd_done, 6)
            s = slice(N, 3 * N)
            act.wait_ge(weighted, 2 * (PO - 1))
            nc.scalar.activation(h_tok[:, 1, s], h_tok[:, 1, s], ACT.Copy, scale=rstd[0][:, 1:2]).then_inc(scaled_act, 1)

        @block.vector
        def _(dve):
            steps = [0]

            def link(ins):
                steps[0] += 1
                ins.then_inc(dve_step, 1)
                dve.wait_ge(dve_step, steps[0])

            def low(u, i=0, per=0):
                dve.wait_ge(hi_done, i * per + (u + 1))
                nc.vector.tensor_tensor(w_lo[u % RING][:], w_raw[u % RING][:], w_hi[u % RING][:],
                                        ALU.subtract).then_inc(lo_done, 1)

            def split_low(name, i, hi, lo, c, done, count, col=None):
                dve.wait_ge(done, count)
                b = bank_of(name, i)
                if col is None:
                    nc.vector.tensor_tensor(lo[:, c:c + 2, :], b[:].rearrange("p (k t) -> p k t", t=TOK),
                                            hi[:, c:c + 2, :], ALU.subtract).then_inc(read_of(name, i), 1)
                    return
                for k in range(2):
                    last = nc.vector.scalar_tensor_tensor(lo[:, c + k, :], b[:, k * TOK:(k + 1) * TOK],
                                                          vec[:, col + k:col + k + 1], hi[:, c + k, :],
                                                          ALU.mult, ALU.subtract)
                last.then_inc(read_of(name, i), 1)

            def inverse_root_of(i):
                dve.wait_ge(squared, norm_squares(i, PO))
                dve.wait_ge(rstd_done, i + 1)
                link(nc.vector.reduce_sum(ms[:], ssq[i % 3][:], AX_X))
                nc.vector.tensor_scalar(ms[:], ms[:], 1.0 / D, RMS_EPS, ALU.mult, ALU.add).then_inc(ms_done, 1)

            for c in range(UPP):
                split_low("x", c, a_hi, a_lo, 2 * c, x_hi_done, c + 1)
                low(c)
                if c == 4:
                    dve.wait_ge(fg_hi_done, 1)
                    nc.vector.tensor_tensor(fg_lo[:], fg_raw[:], fg_hi[:], ALU.subtract).then_inc(fg_split, 1)
            nc.vector.memset(poolu[:, :, 0:PAD], 0.0).then_inc(zeros, 1)
            y_count = [0]
            gates = [0]

            def gate(i, dst):
                gates[0] += 1
                dve.wait_ge(tanh_done, gates[0])
                nc.vector.scalar_tensor_tensor(dst, tanh[i % 2][:], 1.0,
                                               bank_of("t", i)[:].rearrange("p (k t) -> p k t", t=TOK),
                                               ALU.add, ALU.mult).then_inc(read_of("t", i), 1)

            def y_low(src, c, n):
                y_count[0] += 1
                dve.wait_ge(y_hi_done, y_count[0])
                nc.vector.scalar_tensor_tensor(y_lo[:, c:c + n, :], src, 0.5, y_hi[:, c:c + n, :],
                                               ALU.mult, ALU.subtract).then_inc(y_done, 1)

            def attention(u):
                for h in range(NH):
                    if u == HEAD0 + HEAD_STEP * h:
                        if h == 0:
                            dve.wait_ge(consts, 7)
                            job_read(dve, "ci")
                        job_done(dve, "s", h)
                        b = bank_of("s", h)
                        nc.vector.scalar_tensor_tensor(logits[:, 0:P], b[:, 0:P], cum_i[:, 0, h:h + 1],
                                                       causal[:, 0:P], ALU.add, ALU.add)
                        nc.vector.scalar_tensor_tensor(logits[:, P:3 * P], b[:, P:3 * P], cum_i[:, 1, h:h + 1],
                                                       causal[:, P:3 * P], ALU.add, ALU.add).then_inc(read_of("s", h), 1)
                        job_read(dve, "s", h)
                        nc.vector.tensor_reduce(neg_max[:, 0:1], logits[:, 0:P], AX_X, ALU.max, negate=True)
                        nc.vector.tensor_reduce(neg_max[:, 1:2], logits[:, P:3 * P], AX_X, ALU.max,
                                                negate=True).then_inc(max_done, 1)
                    if u == HEAD0 + HEAD_STEP * h + 1:
                        dve.wait_ge(exp_done, 2 * (h + 1))
                        nc.vector.reciprocal(inv_sum[:], row_sum[:]).then_inc(inv_done, 1)
                        dve.wait_ge(inv_done, h + 1)
                        for t, c in ((0, slice(0, P)), (1, slice(P, 3 * P))):
                            nc.vector.tensor_scalar(probs[:, c], probs[:, c], inv_sum[:, t:t + 1], None,
                                                    ALU.mult).then_inc(probs_done, 1)
                    if u == HEAD0 + HEAD_STEP * h + VALUE_LAG:
                        job_done(dve, "ot", h)
                        nc.vector.tensor_tensor(y_head[:], bank_of("ot", h)[:, 0:TOK], gaT[:, h, :],
                                                ALU.mult).then_inc(read_of("ot", h), 1)
                        y_low(y_head[:], h, 1)

            for p in range(NP1):
                for j in range(UPP):
                    u = U_IN + p * UPP + j
                    if (p, j) == (0, UPP - 1):
                        job_done(dve, "vec")
                        nc.vector.tensor_copy(vec[:], bank_of("vec")[:, 0:NVEC]).then_inc(read_of("vec"), 1)
                    if (p, j) == (1, 2):
                        dve.wait_ge(vec_in, 7 * 16)
                        job_done(dve, "fg")
                        nc.vector.tensor_scalar(fgz[:], bank_of("fg")[0:NH, 0:TOK], bf_col[:], None, ALU.add).then_inc(read_of("fg"), 1)
                    if (p, j) == (1, 4):
                        dve.wait_ge(fg_ln, 1)
                        link(nc.vector.tensor_scalar(fgz[:], fgz[:], 0.0, None, ALU.min))
                        link(nc.vector.tensor_tensor(fge[:], fgz[:], fge[:], ALU.subtract))
                        link(nc.vector.memset(ncum[:], 1.0))
                        nc.vector.tensor_tensor_scan(fgz[:], ncum[:], fge[:], 0.0, ALU.mult, ALU.add).then_inc(fg_cum, 1)
                        dve.wait_ge(fg_cum, 1)
                        nc.vector.tensor_scalar(ncum[:], fgz[:], -1.0, None, ALU.mult).then_inc(fg_neg, 1)
                    if j == 1 and p >= 1:
                        q = p - 1
                        for i in (2 * q, 2 * q + 1):
                            if ("t", i) not in JOB:
                                continue
                            src = bank_of("t", i)[:].rearrange("p (k t) -> p k t", t=TOK)
                            k = 2 * (i % 2)
                            if q in (PK, PK + 1):
                                job_done(dve, "t", i)
                                nc.vector.tensor_copy(kT[:, 2 * (i - 4):2 * (i - 4) + 2, :], src).then_inc(read_of("t", i), 1)
                            if q in (PGA, PGA + 1):
                                gate(i, gaT[:, 2 * (i - 8):2 * (i - 8) + 2, :])
                            if q == PCH:
                                job_done(dve, "t", i)
                                job_read(dve, "t", 2 * PCC + 1)
                                nc.vector.tensor_tensor(convu[:, k:k + 2, 2:], src, convu[:, k:k + 2, 2:],
                                                        ALU.mult).then_inc(read_of("t", i), 1)
                            if q == PCG:
                                gate(i, convg[:, k:k + 2, :])
                            if q == PCB:
                                job_done(dve, "t", i)
                                nc.vector.tensor_tensor(convg[:, k:k + 2, :], src, convg[:, k:k + 2, :],
                                                        ALU.mult).then_inc(read_of("t", i), 1)
                    attention(u)
                    if u >= 4:
                        low(u + RING)
                    if (p, j) == (2, 2):
                        dve.wait_ge(consts, 9)
                        link(nc.vector.reciprocal(iota_f[:], iota_f[:]))
                    if (p, j) == (2, 4):
                        for g in range(4):
                            nc.vector.tensor_scalar(inv_count[:, g, :], iota_f[:], 1.0 / (2 << g), None,
                                                    ALU.max).then_inc(dve_step, 1)
                        steps[0] += 4
                    if (p, j) == (9, 2):
                        job_read(dve, "t", 2 * PPU)
                        job_read(dve, "t", 2 * PPU + 1)
                        E = PAD + TOK
                        link(nc.vector.tensor_tensor(sum_a[:, :, 1:E], poolu[:, :, 1:E], poolu[:, :, 0:E - 1], ALU.add))
                        link(nc.vector.tensor_tensor(sum_b[:, 1:4, 3:E], sum_a[:, 1:4, 3:E], sum_a[:, 1:4, 1:E - 2], ALU.add))
                    if (p, j) == (9, 3):
                        link(nc.vector.tensor_tensor(sum_a[:, 2:4, 7:E], sum_b[:, 2:4, 7:E], sum_b[:, 2:4, 3:E - 4], ALU.add))
                        link(nc.vector.tensor_tensor(sum_b[:, 3:4, 15:E], sum_a[:, 3:4, 15:E], sum_a[:, 3:4, 7:E - 8], ALU.add))
                        for g in range(4):
                            nc.vector.tensor_tensor(poolz[:, g, :], (sum_a, sum_b)[g % 2][:, g, PAD:E],
                                                    inv_count[:, g, :], ALU.mult).then_inc(dve_step, 1)
                            steps[0] += 1
                        dve.wait_ge(dve_step, steps[0])
                        nc.vector.tensor_tensor(poolz[:], poolz[:], poolu[:, :, PAD:E], ALU.subtract).then_inc(z_done, 1)
                        dve.wait_ge(z_done, 1)
                        nc.vector.memset(convu[:, :, 0:2], 0.0).then_inc(zeros, 1)
                    if (p, j) == (13, 2):
                        job_read(dve, "t", 2 * PCB + 1)
                        for b in range(4):
                            link(nc.vector.tensor_scalar(convy[:, b, :], convu[:, b, 0:TOK],
                                                         vec[:, V_CONV + b:V_CONV + b + 1], None, ALU.mult))
                            for tap in (1, 2):
                                c = V_CONV + 4 * tap + b
                                link(nc.vector.scalar_tensor_tensor(convy[:, b, :], convu[:, b, tap:tap + TOK],
                                                                    vec[:, c:c + 1], convy[:, b, :],
                                                                    ALU.mult, ALU.add))
                        nc.vector.tensor_tensor(convy[:], convy[:], convg[:], ALU.mult).then_inc(mixed, 1)
                    if (p, j) == (13, 4):
                        y_low(convy[:], 8, 4)

            for j in range(UPP):
                low(U_OUT + j + RING)
                if j == 1:
                    for i in range(2):
                        gate(2 * PPG + i, poolg[:, 2 * i:2 * i + 2, :])
                    job_read(dve, "t", 2 * PPG + 1)
                    for g in range(4):
                        last = nc.vector.scalar_tensor_tensor(
                            poolz[:, g, :], bank_of("pool", g // 2)[:, (g % 2) * TOK:(g % 2 + 1) * TOK],
                            vec[:, V_PS + g:V_PS + g + 1], poolg[:, g, :], ALU.mult, ALU.mult)
                        if g == 1:
                            last.then_inc(read_of("pool", 0), 1)
                    last.then_inc(read_of("pool", 1), 1)
                    y_low(poolz[:], 12, 4)
                if j == UPP - 1:
                    split_low("pt", 0, a_hi, a_lo, P_CHUNK, p_hi_done, 1)

            def residual(n):
                p = P_OUT + n
                panel_done(dve, p)
                for t, b in enumerate(panel_banks(p)):
                    s = slice(n * N, (n + 1) * N)
                    nc.vector.scalar_tensor_tensor(h_tok[:, t, s], h_tok[:, t, s], ALPHA, b[:], ALU.mult,
                                                   ALU.add).then_inc(acc_read[p % 2], 1)
                for t in range(TT):
                    panel_read(dve, p, t + 1)
                    nc.vector.bn_stats(bn[:, t, n, :], h_tok[:, t, n * N:(n + 1) * N]).then_inc(bn_done, 1)

            dve.wait_ge(x_back, 16)
            residual(0)
            for n in range(1, PO):
                for j in range(UPP if n < PO - 1 else UPP - 1):
                    low(U_OUT + n * UPP + j + RING)
                residual(n)
            for t in range(TT):
                dve.wait_ge(bn_done, TT * PO)
                nc.vector.bn_aggr(mv[:, t, :], bn[:, t, :, :].rearrange("p n s -> p (n s)")).then_inc(var_done, 1)
            dve.wait_ge(var_done, 2)
            nc.vector.tensor_scalar(ms[:], mv[:, :, 1], LN_EPS, None, ALU.add).then_inc(ms_done, 1)
            low(U_PP + PO - 1)
            dve.wait_ge(rstd_done, 1)
            dve.wait_ge(gb_in, 32)

            def split_hn(c):
                split_low("hn", c, a_hi, a_lo, 2 * c, hn_hi_done, 2 * (c + 1), V_MIX + 2 * c)

            def centre(n):
                s = slice(n * N, (n + 1) * N)
                for t in range(TT):
                    nc.vector.tensor_scalar(h_tok[:, t, s], h_tok[:, t, s], mv[:, t, 0:1], rstd[0][:, t:t + 1],
                                            ALU.subtract, ALU.mult).then_inc(centred, 1)

            def affine(n):
                s = slice(n * N, (n + 1) * N)
                for t in range(TT if n == 0 else 1):
                    dve.wait_ge(centred, TT * n + t + 1)
                    k = 2 * t if n == 0 else 2 * (n + 1)
                    nc.vector.tensor_tensor(h_tok[:, t, s], h_tok[:, t, s], ln_gb[:, 0, s], ALU.mult).then_inc(ln_dve, 1)
                    dve.wait_ge(ln_dve, k + 1)
                    nc.vector.tensor_tensor(h_tok[:, t, s], h_tok[:, t, s], ln_gb[:, 1, s], ALU.add).then_inc(ln_dve, 1)

            centre(0)
            centre(1)
            affine(0)
            low(U_G)
            affine(1)
            split_hn(0)
            split_hn(1)
            low(U_G + 1)
            centre(2)
            low(U_G + 2)
            split_hn(2)
            affine(2)
            split_hn(3)
            low(U_G + 3)
            centre(3)
            affine(3)
            for c in range(RING, UPP):
                split_hn(c)
                low(U_G + c)

            def flat(t):
                return t[:].rearrange("p d t -> p (d t)")

            def diff(n):
                s, part, h = n // 2, n % 2, LEVELS[n // 2]
                if s >= 2 and part == 0:
                    job_done(dve, "step", 2 * (s - 2) + 1)
                d = halves(flat(decayed[n % 4]), h)
                for way in range(2):
                    half = way if part == 0 else 1 - way
                    c = halves(flat(cum[way]), h)
                    mid = (c[:, :, 0, h - 1:h] if way == 0 else c[:, :, 1, 0:1]).broadcast_to([P, DB * TOK // (2 * h), h])
                    if part == 0:
                        last = nc.vector.tensor_tensor(d[:, :, half, :], mid, c[:, :, half, :], ALU.subtract)
                    elif h == P:
                        last = nc.vector.tensor_copy(d[:, :, half, :], c[:, :, half, :])
                    else:
                        last = nc.vector.tensor_tensor(d[:, :, half, :], c[:, :, half, :], mid, ALU.subtract)
                    last.then_inc(diff_done, 1)

            def times(s):
                dve.wait_ge(decay_done, 2 * s + 2)
                if s == 0:
                    for i in range(4):
                        job_read(dve, "gt", i)
                d = decayed[2 * (s % 2) + 1]
                nc.vector.tensor_tensor(d[:], d[:], gqT[:], ALU.mult).then_inc(mul_dve, 1)

            def keep(n):
                s, pair = n // 2, n % 2
                job_done(dve, "step", n)
                b = bank_of("step", n)
                dst = (at_off if LEVELS[s] == P else at_diag)[:, 2 * pair:2 * pair + 2, :, :].rearrange("p h t i -> p (h t) i")
                src = b[:].rearrange("p (c i) -> p c i", i=P)
                if LEVELS[s] == P:
                    last = nc.vector.tensor_copy(dst, src)
                else:
                    m = masks[:, s, :].bitcast(I32).rearrange("p (a i) -> p a i", a=1).broadcast_to([P, 2 * TT, P])
                    last = nc.vector.copy_predicated(dst, m, src)
                last.then_inc(read_of("step", n), 1)

            def head_out(hd):
                dve.wait_ge(o_rstd_done, hd + 1)
                panel_read(dve, P_G + 8 + hd)
                for t in range(TT):
                    nc.vector.scalar_tensor_tensor(og[hd][:, t, :], bank_of("av", 2 * hd + t)[:],
                                                   o_rstd[:, hd, t:t + 1], og[hd][:, t, :], ALU.mult,
                                                   ALU.mult).then_inc(read_of("av", 2 * hd + t), 1)

            for g in range(NPG * UPP):
                for name, i in gla_jobs(g):
                    if name == "gk":
                        job_done(dve, "gk", i)
                        way, k = i // 4, 2 * (i % 4)
                        nc.vector.tensor_scalar(cum[way][:, k:k + 2, :].rearrange("p k t -> p (k t)"), bank_of("gk", i)[:],
                                                0.0, None, ALU.min).then_inc(gk_min, 1)
                    if name == "dg":
                        job_done(dve, "dg", i)
                        idb = ident[:].rearrange("p (a t) -> p a t", a=1).broadcast_to([P, 4, P])
                        nc.vector.scalar_tensor_tensor(
                            at_diag[:, 2 * i:2 * i + 2, :, :].rearrange("p h t i -> p (h t) i"),
                            bank_of("dg", i)[:].rearrange("p (c i) -> p c i", i=P), 2.0, idb,
                            ALU.mult, ALU.mult).then_inc(read_of("dg", i), 1)
                    if name == "step":
                        keep(i)
                if g >= 4:
                    low(U_G + g + RING)
                if g == 4:
                    inverse_root_of(0)
                if g == 5:
                    dve.wait_ge(lr_hi_done, 1)
                    nc.vector.tensor_tensor(lr_lo[:], lr_raw[:], lr_hi[:], ALU.subtract).then_inc(lr_split, 1)
                    nc.vector.memset(lrt[:, :, 2 * RANK:], 1.0).then_inc(zeros, 1)
                    link(nc.vector.memset(restart[:], 1.0))
                    for c in (0, P, TOK):
                        link(nc.vector.memset(restart[:, c:c + 1], 0.0))
                for s in range(NL):
                    for part in range(2):
                        if g == STEP0 + STEP_GAP * s - 7 + 2 * part:
                            if s == 0 and part == 0:
                                dve.wait_ge(cum_done, 2 * DB)
                            diff(2 * s + part)
                    if g == STEP0 + STEP_GAP * s - 3:
                        times(s)
                for way, when in enumerate(SUM_G):
                    if g == when:
                        dve.wait_ge(gk_ln, way + 1)
                        link(nc.vector.tensor_tensor(flat(cum[way]), flat(cum[way]), flat(gate_tmp[way]), ALU.subtract))
                    if when <= g < when + 4:
                        for b in (2 * (g - when), 2 * (g - when) + 1):
                            c = cum[way][:, b, :]
                            r = restart[:, 0:TOK]
                            if way:
                                c, r = c[:, ::-1], restart[:, 1:TOK + 1][:, ::-1]
                            nc.vector.tensor_tensor_scan(c, r, c, 0.0, ALU.mult, ALU.add).then_inc(cum_done, 1)
                for hd in range(GH):
                    if g == AV0 + 3 * hd:
                        dve.wait_ge(squared, head_squares(hd + 1))
                        nc.vector.tensor_scalar(o_ms[:, hd, :], o_ssq[:, hd, :], 1.0 / GDV, RMS_EPS, ALU.mult,
                                                ALU.add).then_inc(o_ms_done, 1)
                if g in (AV0 + 1, AV0 + 4, AV0 + 7):
                    hd = (g - AV0 - 1) // 3
                    head_out(hd)
                if g in (AV0 + 3, AV0 + 6, AV0 + 9):
                    hd = (g - AV0 - 3) // 3
                    for i in (2 * hd, 2 * hd + 1):
                        split_low("o", i, y_hi, y_lo, 2 * i, o_hi_done, 2 * (i + 1), V_ON + 2 * (i % 2))

            head_out(GH - 1)

            def add_panel(n, p, i=0, uper=0):
                panel_done(dve, p, i, uper)
                for t, b in enumerate(panel_banks(p)):
                    s = slice(n * N, (n + 1) * N)
                    nc.vector.tensor_tensor(h_tok[:, t, s], h_tok[:, t, s], b[:], ALU.add).then_inc(acc_read[p % 2], 1)

            def split_h(name, n, col):
                for i in (2 * n, 2 * n + 1):
                    split_low(name, i, a_hi, a_lo, 2 * i, h1_hi_done if name == "h1" else h2_hi_done, 2 * (i + 1),
                              col + 2 * i)

            for n in range(PO):
                for j in range(UPP):
                    low(U_GO + n * UPP + j + RING)
                    if n == 0 and j == 1:
                        for i in (6, 7):
                            split_low("o", i, y_hi, y_lo, 2 * i, o_hi_done, 2 * (i + 1), V_ON + 2 * (i % 2))
                    if n >= 1 and j == 1:
                        split_h("h1", n - 1, V_FFN)
                add_panel(n, P_GO + n)

            def multiply(p, i=0, uper=0):
                panel_done(dve, p, i, uper)
                for t, b in enumerate(panel_banks(p)):
                    nc.vector.scalar_tensor_tensor(act_tok[:, t, :], b[:], rstd[2][:, t:t + 1], act_tok[:, t, :],
                                                   ALU.mult, ALU.mult).then_inc(acc_read[p % 2], 1)

            def split_act(f, hi, lo):
                for k in range(2):
                    n, bank, _ = job("a", k)
                    dve.wait_ge(act_hi_done, 2 * f + (k + 1))
                    nc.vector.tensor_tensor(lo[:, 2 * k:2 * k + 2, :],
                                            aux[bank][:].rearrange("p (k t) -> p k t", t=TOK),
                                            hi[:, 2 * k:2 * k + 2, :], ALU.subtract).then_inc(aux_read[bank], 1)

            for m in range(2):
                for j in range(UPP):
                    low(U_F + m * UPP + j + RING)
                    if m == 0 and j == 1:
                        split_h("h1", PO - 1, V_FFN)
                        inverse_root_of(1)
            dve.wait_ge(rstd_done, 3)
            panel_read(dve, P_F)
            multiply(P_F + 1)

            def ffn_step(f, last=False):
                for j in range(FU):
                    low(U_FL + j + RING, f, FU)
                    if j == 2:
                        split_act(f, act_hi, act_lo)
                    if last and j == 2 * UPP + 2 * ROWS_F - 1:
                        split_act(f + 1, y_hi, y_lo)
                    if j == 2 * UPP - 1:
                        panel_read(dve, P_FL, 2, f, FP)
                        multiply(P_FL + 1, f, FU)
                    if j >= 2 * UPP and (j - 2 * UPP) % ROWS_F == ROWS_F - 1:
                        n = (j - 2 * UPP) // ROWS_F
                        add_panel(n, P_FL + 2 + n, f, FU)

            with dve.Fori(0, NF - 2) as f:
                ffn_step(f)
            ffn_step(NF - 2, last=True)
            for n in range(PO):
                for k in range(ROWS_F):
                    low(U_FE + n * ROWS_F + k + RING)
                add_panel(n, P_FE + n)
                if n >= 1:
                    split_h("h2", n - 1, V_PLE)
            for n in range(PO):
                for j in range(UPP):
                    if U_PG + n * UPP + j + RING < U_END:
                        low(U_PG + n * UPP + j + RING)
                    if (n, j) == (0, 1):
                        split_h("h2", PO - 1, V_PLE)
                        inverse_root_of(2)
                if n == 0:
                    dve.wait_ge(emb_in, 16)
                s = slice(n * N, (n + 1) * N)
                for t in range(TT):
                    panel_read(dve, P_PG + n, t + 1)
                    nc.vector.tensor_tensor(gate_tok[:, t, :], gate_tok[:, t, :], emb[:, t, s], ALU.mult).then_inc(gated, 1)
                    dve.wait_ge(gated, TT * n + t + 1)
                    nc.vector.tensor_tensor(h_tok[:, t, s], h_tok[:, t, s], gate_tok[:, t, :], ALU.add).then_inc(h_added, 1)
                    if n == PO - 1:
                        dve.wait_ge(squared, norm_squares(3, n) + t + 1)
                        link(nc.vector.reduce_sum(ms[:, t:t + 1], ssq[0][:, t, :], AX_X))
                        nc.vector.tensor_scalar(ms[:, t:t + 1], ms[:, t:t + 1], 1.0 / D, RMS_EPS, ALU.mult,
                                                ALU.add).then_inc(ms_done, 1)
                        dve.wait_ge(rstd_done, 5 + t)
                        nc.vector.scalar_tensor_tensor(h_tok[:, t, s], h_tok[:, t, s], rstd[0][:, t:t + 1], fin_w[:, s],
                                                       ALU.mult, ALU.mult).then_inc(scaled, 1)
                        dve.wait_ge(weighted, 2 * (PO - 1))
                        r = slice(0, 3 * N if t == 0 else N)
                        nc.vector.tensor_scalar(h_tok[:, t, r], h_tok[:, t, r], rstd[0][:, t:t + 1], None,
                                                ALU.mult).then_inc(scaled, 1)


_INS = ["x", "w_in", "b_f", "conv_w", "pool_w", "pool_scale", "w_out", "ln_g", "ln_b", "p_2", "mixer_norm_2",
        "gla_w_in_2", "gla_w_gate_up_2", "gla_b_gate_2", "gla_out_norm_2", "gla_w_out_2", "ffn_norm_2",
        "ffn_w_in_2", "ffn_w_out_2", "ple_norm_2", "ple_w_gate_2", "ple_w_proj_2", "final_norm_2"]


def kernel(**inputs):
    import numpy as np
    import concourse.bacc as bacc
    from concourse.bass_utils import run_bass_kernel_spmd

    nc = bacc.Bacc("TRN2", target_bir_lowering=False, num_devices=1)
    arrays, args = {}, []
    for name in _INS:
        a = np.ascontiguousarray(inputs[name])
        arrays[f"in_{name}"] = a
        args.append(nc.dram_tensor(f"in_{name}", a.shape, mybir.dt.from_np(a.dtype), kind="ExternalInput").ap())
    out = nc.dram_tensor("out", (1, TOK, D), F32, kind="ExternalOutput").ap()
    block_kernel(nc, *args, out)
    r = run_bass_kernel_spmd(nc, [arrays], core_ids=[0])
    return r.results[0]["out"]
```
